# Optimizing a Trainium2 kernel written in Bass

```python
import jax, jax.numpy as jnp
from jax import lax
import numpy as np

D_MODEL = 1024
BATCH = 1
SEQ = 1024
DEPTH = 2

D_MIX = D_MODEL
NORM_EPS = 1e-6
ATT_HEADS = 4
QK_NOPE_DIM = 128
QK_ROPE_DIM = 64
V_HEAD_DIM = 128
ATT_WIDTH = ATT_HEADS * V_HEAD_DIM
Q_LORA_RANK = D_MODEL // 4
KV_LORA_RANK = D_MODEL // 8
ROPE_THETA = 10000.0
Q_BLOCK = 128
CONV_WIDTH = D_MIX // 4
CONV_KERNEL = 31
SGU_WIDTH = D_MIX // 4
SGU_GROUPS = 4
SGU_GROUP_DIM = SGU_WIDTH // SGU_GROUPS
SGU_CHUNK = 128
IN_SPLITS = (Q_LORA_RANK, KV_LORA_RANK, QK_ROPE_DIM, ATT_WIDTH,
             CONV_WIDTH, CONV_WIDTH, CONV_WIDTH,
             SGU_WIDTH, SGU_WIDTH, SGU_WIDTH)
D_IN = Q_LORA_RANK + KV_LORA_RANK + QK_ROPE_DIM + ATT_WIDTH + 3 * CONV_WIDTH + 3 * SGU_WIDTH

kernel_name = "hymba_style_mla_conformer_sgu_hybrid"

def rms_norm(x, g):
    xf = x.astype(jnp.float32)
    y = xf * lax.rsqrt(jnp.mean(xf * xf, axis=-1, keepdims=True) + NORM_EPS)
    return (y * g.astype(jnp.float32)).astype(x.dtype)

def layer_norm(x, g, b):
    xf = x.astype(jnp.float32)
    mu = jnp.mean(xf, axis=-1, keepdims=True)
    var = jnp.mean(jnp.square(xf - mu), axis=-1, keepdims=True)
    y = (xf - mu) * lax.rsqrt(var + NORM_EPS)
    return (y * g.astype(jnp.float32) + b.astype(jnp.float32)).astype(x.dtype)

def apply_rope(x, cos, sin):
    half = x.shape[-1] // 2
    x1, x2 = x[..., :half], x[..., half:]
    return jnp.concatenate([x1 * cos - x2 * sin, x2 * cos + x1 * sin], axis=-1)

def mla_mixer(q_lat, kv_lat, k_rope, positions, q_norm_g, w_uq, kv_norm_g, w_ukv):
    B, S, _ = q_lat.shape
    q = (rms_norm(q_lat, q_norm_g) @ w_uq).reshape(B, S, ATT_HEADS, QK_NOPE_DIM + QK_ROPE_DIM)
    q_nope, q_rope = q[..., :QK_NOPE_DIM], q[..., QK_NOPE_DIM:]
    kv = (rms_norm(kv_lat, kv_norm_g) @ w_ukv).reshape(B, S, ATT_HEADS, QK_NOPE_DIM + V_HEAD_DIM)
    k_nope, v = kv[..., :QK_NOPE_DIM], kv[..., QK_NOPE_DIM:]
    inv_freq = ROPE_THETA ** (-jnp.arange(0, QK_ROPE_DIM, 2, dtype=jnp.float32) / QK_ROPE_DIM)
    ang = positions.astype(jnp.float32)[..., None] * inv_freq
    cos, sin = jnp.cos(ang).astype(q.dtype), jnp.sin(ang).astype(q.dtype)
    q_rope = apply_rope(q_rope, cos[:, :, None, :], sin[:, :, None, :])
    k_rope = apply_rope(k_rope, cos, sin)
    scale = (QK_NOPE_DIM + QK_ROPE_DIM) ** -0.5
    nb = S // Q_BLOCK
    qn_blocks = q_nope.reshape(B, nb, Q_BLOCK, ATT_HEADS, QK_NOPE_DIM).transpose(1, 0, 2, 3, 4)
    qr_blocks = q_rope.reshape(B, nb, Q_BLOCK, ATT_HEADS, QK_ROPE_DIM).transpose(1, 0, 2, 3, 4)
    k_pos = jnp.arange(S)

    def one_block(args):
        qn, qr, blk = args
        s = (jnp.einsum('bqhd,bkhd->bhqk', qn, k_nope)
             + jnp.einsum('bqhr,bkr->bhqk', qr, k_rope)).astype(jnp.float32) * scale
        q_pos = blk * Q_BLOCK + jnp.arange(Q_BLOCK)
        s = jnp.where(k_pos[None, :] <= q_pos[:, None], s, -jnp.inf)
        p = jax.nn.softmax(s, axis=-1).astype(v.dtype)
        return jnp.einsum('bhqk,bkhd->bqhd', p, v)

    out = lax.map(one_block, (qn_blocks, qr_blocks, jnp.arange(nb)))
    return out.transpose(1, 0, 2, 3, 4).reshape(B, S, ATT_WIDTH)

def conv_mixer(a, b, conv_w, conv_b, ln_g, ln_b, w_pw2):
    h = a * jax.nn.sigmoid(b)
    h = lax.conv_general_dilated(
        h, conv_w[:, None, :].astype(h.dtype), window_strides=(1,),
        padding=[(CONV_KERNEL - 1, 0)],
        dimension_numbers=('NWC', 'WIO', 'NWC'),
        feature_group_count=CONV_WIDTH) + conv_b
    h = jax.nn.silu(layer_norm(h, ln_g, ln_b))
    return h @ w_pw2

def sgu_mixer(u, v, ln_g, ln_b, w_s, b_s):
    u = jax.nn.gelu(u, approximate=False)
    v = layer_norm(jax.nn.gelu(v, approximate=False), ln_g, ln_b)
    B, S, _ = v.shape
    nc = S // SGU_CHUNK
    v = v.reshape(B, nc, SGU_CHUNK, SGU_GROUPS, SGU_GROUP_DIM)
    causal = jnp.tril(jnp.ones((SGU_CHUNK, SGU_CHUNK), dtype=bool))
    w = jnp.where(causal[None], w_s, jnp.zeros_like(w_s))
    sv = jnp.einsum('gts,bnsgc->bntgc', w, v) + b_s.T[None, None, :, :, None]
    return u * sv.reshape(B, S, SGU_WIDTH)

def hybrid_layer(x, c, positions, w_ada, b_ada, g_pre, g_post, w_in, q_norm_g, w_uq,
                 kv_norm_g, w_ukv, conv_w, conv_b, conv_ln_g, conv_ln_b, w_pw2,
                 sgu_ln_g, sgu_ln_b, w_s, b_s, w_out):
    mod = jax.nn.silu(c) @ w_ada + b_ada
    shift, scale, gate = jnp.split(mod, 3, axis=-1)
    h = rms_norm(x, g_pre) * (1 + scale[:, None, :]) + shift[:, None, :]
    z = h @ w_in
    (q_lat, kv_lat, k_rope, g_att, conv_a, conv_b_in, g_conv,
     sgu_u, sgu_v, g_sgu) = jnp.split(z, np.cumsum(IN_SPLITS)[:-1].tolist(), axis=-1)
    y_att = mla_mixer(q_lat, kv_lat, k_rope, positions, q_norm_g, w_uq, kv_norm_g, w_ukv)
    y_conv = conv_mixer(conv_a, conv_b_in, conv_w, conv_b, conv_ln_g, conv_ln_b, w_pw2)
    y_sgu = sgu_mixer(sgu_u, sgu_v, sgu_ln_g, sgu_ln_b, w_s, b_s)
    y = jnp.concatenate([y_att * jax.nn.silu(g_att),
                         y_conv * jax.nn.silu(g_conv),
                         y_sgu * jax.nn.silu(g_sgu)], axis=-1) @ w_out
    return x + gate[:, None, :] * rms_norm(y, g_post)

def setup_inputs(seed: int = 0) -> dict:
    key = jax.random.key(seed)
    ks = jax.random.split(key, 32)
    f32 = jnp.float32
    L = DEPTH

    def nrm(k, shape, s):
        return jax.random.normal(k, shape, f32) * s

    def gain(k, shape):
        return 1.0 + 0.02 * jax.random.normal(k, shape, f32)

    b_ada = jnp.concatenate([nrm(ks[3], (L, D_MODEL), 0.02),
                             nrm(ks[4], (L, D_MODEL), 0.02),
                             gain(ks[5], (L, D_MODEL))], axis=-1)
    return {
        "x": jax.random.normal(ks[0], (BATCH, SEQ, D_MODEL), f32),
        "c": jax.random.normal(ks[1], (BATCH, D_MODEL), f32),
        "positions": jnp.tile(jnp.arange(SEQ, dtype=jnp.int32)[None, :], (BATCH, 1)),
        "w_ada": nrm(ks[2], (L, D_MODEL, 3 * D_MODEL), 0.1 * D_MODEL ** -0.5),
        "b_ada": b_ada,
        "g_pre": gain(ks[6], (L, D_MODEL)),
        "g_post": gain(ks[7], (L, D_MODEL)),
        "w_in": nrm(ks[8], (L, D_MODEL, D_IN), D_MODEL ** -0.5),
        "q_norm_g": gain(ks[9], (L, Q_LORA_RANK)),
        "w_uq": nrm(ks[10], (L, Q_LORA_RANK, ATT_HEADS * (QK_NOPE_DIM + QK_ROPE_DIM)), Q_LORA_RANK ** -0.5),
        "kv_norm_g": gain(ks[11], (L, KV_LORA_RANK)),
        "w_ukv": nrm(ks[12], (L, KV_LORA_RANK, ATT_HEADS * (QK_NOPE_DIM + V_HEAD_DIM)), KV_LORA_RANK ** -0.5),
        "conv_w": nrm(ks[13], (L, CONV_KERNEL, CONV_WIDTH), CONV_KERNEL ** -0.5),
        "conv_b": nrm(ks[14], (L, CONV_WIDTH), 0.02),
        "conv_ln_g": gain(ks[15], (L, CONV_WIDTH)),
        "conv_ln_b": nrm(ks[16], (L, CONV_WIDTH), 0.02),
        "w_pw2": nrm(ks[17], (L, CONV_WIDTH, CONV_WIDTH), CONV_WIDTH ** -0.5),
        "sgu_ln_g": gain(ks[18], (L, SGU_WIDTH)),
        "sgu_ln_b": nrm(ks[19], (L, SGU_WIDTH), 0.02),
        "w_s": nrm(ks[20], (L, SGU_GROUPS, SGU_CHUNK, SGU_CHUNK), SGU_CHUNK ** -0.5),
        "b_s": gain(ks[21], (L, SGU_GROUPS, SGU_CHUNK)),
        "w_out": nrm(ks[22], (L, D_MIX, D_MODEL), D_MIX ** -0.5),
    }

def reference(x, c, positions, w_ada, b_ada, g_pre, g_post, w_in, q_norm_g, w_uq,
              kv_norm_g, w_ukv, conv_w, conv_b, conv_ln_g, conv_ln_b, w_pw2,
              sgu_ln_g, sgu_ln_b, w_s, b_s, w_out):
    for l in range(DEPTH):
        x = hybrid_layer(x, c, positions, w_ada[l], b_ada[l], g_pre[l], g_post[l], w_in[l],
                         q_norm_g[l], w_uq[l], kv_norm_g[l], w_ukv[l], conv_w[l], conv_b[l],
                         conv_ln_g[l], conv_ln_b[l], w_pw2[l], sgu_ln_g[l], sgu_ln_b[l],
                         w_s[l], b_s[l], w_out[l])
    return x


_drawn_inputs = setup_inputs


def setup_inputs(seed=0):
    import zlib

    import numpy as np

    out = dict(_drawn_inputs(seed))
    spreads = {}
    factors = {'g_post': 2.694,
     'q_norm_g': 8.0,
     'kv_norm_g': 8.0,
     'conv_ln_g': 3.582,
     'conv_ln_b': 4.092,
     'sgu_ln_g': 6.957,
     'sgu_ln_b': 6.59,
     'b_s': 4.581}
    for name, (base, spread) in spreads.items():
        noise = np.random.default_rng([zlib.crc32(name.encode()), seed]).standard_normal(out[name].shape)
        drawn = base * np.exp(spread * noise) if base else spread * noise
        out[name] = __import__('jax').numpy.asarray(drawn.astype(out[name].dtype))
    for name, factor in factors.items():
        out[name] = (out[name] * factor).astype(out[name].dtype)
    return out
```

```python
from contextlib import ExitStack

import concourse.bass as bass
from concourse import mybir

ALU = mybir.AluOpType
ACT = mybir.ActivationFunctionType
F32 = mybir.dt.float32
F32R = mybir.dt.float32r
I32 = mybir.dt.int32
AX_X = mybir.AxisListType.X

P = 128
D = 1024
SEQ = 1024
DEPTH = 2
NT = SEQ // P
KD = D // P
HEADS = 4
NOPE = 128
ROPE = 64
Q_RANK = 256
KV_RANK = 128
CONV_K = 31
HALO = CONV_K - 1
EPS = 1e-6
SCALE = (NOPE + ROPE) ** -0.5
MASKED = -1e30
BANK = 512
CW = 256

Q, CONV_A, CONV_B, KV, SGU_V, SGU_U, G_ATT0, G_ATT1, G_SGU, G_CONV = range(10)
CHUNKS = [(0, 256), (960, 256), (1216, 256), (256, 192), (1984, 256), (1728, 256),
          (448, 256), (704, 256), (2240, 256), (1472, 256)]
NCH = len(CHUNKS)
UNITS = 6 * 0 + 8 * 8 + 2 * 4


def unit(c, i):
    if c == Q:
        return i
    if c in (CONV_A, CONV_B):
        return 8 + 4 * (c - CONV_A) + i
    return 16 + 8 * (c - KV) + i


Y_ATT, Y_CONV, Y_SGU = 0, 512, 768
W_PIECES = 2 * NCH + KD
STEPS = HEADS * NT


class BankRing:

    def __init__(self):
        self.uses = {}

    def take(self, name):
        n = len(self.uses)
        self.uses[name] = (n % 4, n // 4)
        return self.uses[name]


def trunk(nc, a, out, x_mid):
    with ExitStack() as ctx:
        base = 1152
        at = [base]

        def place(name, shape, dt, offset=None):
            size = 4
            for s in shape[1:]:
                size *= s
            if offset is None:
                offset = at[0]
                at[0] += (size + 31) // 32 * 32
            return nc.alloc_sbuf_tensor_at(name, shape, dt, offset=offset)

        def sem(name):
            return ctx.enter_context(nc.semaphore(name))

        act_hi = place("act_hi", [P, KD, SEQ], F32R)
        act_lo = place("act_lo", [P, KD, SEQ], F32R)
        Y = place("Y", [P, NT, D], F32)
        w_at = at[0]
        w_hi = place("w_hi", [P, 2, KD, CW], F32R)
        w_lo = place("w_lo", [P, 2, KD, CW], F32R)
        kb = 1024
        q_hi = place("q_hi", [P, SEQ], F32R, w_at)
        q_lo = place("q_lo", [P, SEQ], F32R, w_at + 4 * kb)
        qr_st = place("qr_st", [P, SEQ], F32R, w_at + 8 * kb)
        qr_lo = place("qr_lo", [ROPE, SEQ], F32R, w_at + 12 * kb)
        v_hi = place("v_hi", [P, NT, P], F32R, w_at + 16 * kb)
        v_lo = place("v_lo", [P, NT, P], F32R, w_at + 20 * kb)
        pt_hi = place("pt_hi", [P, NT, P], F32R, w_at + 24 * kb)
        pt_lo = place("pt_lo", [P, NT, P], F32R, w_at + 28 * kb)
        wraw = place("wraw", [P, 2, 1024], F32)
        araw = place("araw", [P, 2, BANK], F32)
        qk_at = at[0]
        qnT = place("qnT", [P, 2, SEQ], F32)
        kv_hi = place("kv_hi", [P, SEQ], F32R)
        kv_lo = place("kv_lo", [P, SEQ], F32R)
        kr_st = place("kr_st", [P, SEQ], F32R)
        yT_hi = place("yT_hi", [P, 2, KD, P], F32R, qk_at)
        yT_lo = place("yT_lo", [P, 2, KD, P], F32R, qk_at + 8 * kb)
        convh = place("convh", [P, 2, HALO + SEQ], F32)
        convo_at = at[0]
        convo = place("convo", [P, 2, BANK], F32)
        uk_raw = place("uk_raw", [P, HEADS, NOPE], F32, convo_at)
        uv_raw = place("uv_raw", [P, HEADS, P], F32, convo_at + 2 * kb)
        qrt = place("qrt", [P, NT, 2, ROPE], F32, convo_at)
        xb_at = at[0]
        xb = place("xb", [P, 2, D], F32)
        uq_raw = place("uq_raw", [P, 2, HEADS, NOPE + ROPE], F32, xb_at)
        ws_raw = place("ws_raw", [P, HEADS, P], F32, xb_at + 6 * kb)
        acc = place("acc", [P, D], F32)
        A_bc = place("A_bc", [P, D], F32)
        S_bc = place("S_bc", [P, D], F32)
        Wq = place("Wq", [P, 2, HEADS, P], F32)
        uqr = place("uqr", [P, 2, HEADS, ROPE], F32)
        uv_hi = place("uv_hi", [P, HEADS, P], F32R)
        uv_lo = place("uv_lo", [P, HEADS, P], F32R)
        pw2 = place("pw2", [P, 2, CW], F32)
        wsT = place("wsT", [P, HEADS, P], F32)
        ident = place("ident", [P, P], F32)
        ident_r = place("ident_r", [P, P], F32R)
        ones = place("ones", [P, P], F32)
        mask = place("mask", [P, P], F32)
        mask_r = place("mask_r", [P, P], F32R)
        cosd = place("cosd", [P, NT, ROPE], F32)
        sind = place("sind", [P, NT, ROPE], F32)
        sgu_g = place("sgu_g", [P, CW], F32)
        sgu_b = place("sgu_b", [P, CW], F32)
        qtmp = place("qtmp", [P, 2, CW], F32)
        gtmp = place("gtmp", [P, 2, CW], F32)
        scr = place("scr", [P, BANK], F32)
        taps = place("taps", [P, 2, CONV_K], F32)
        cols = place("cols", [P, 24], F32)
        silu_c = place("silu_c", [P, 2 * KD], F32)
        st = place("st", [P, 64], F32)
        bst = place("bst", [P, NT, 6], F32)
        mv = place("mv", [P, NT, 2], F32)
        ssq = place("ssq", [P, 8], F32)
        rsum = place("rsum", [P, 2], F32)
        nmax = place("nmax", [P, 2], F32)
        posi = place("posi", [P, NT], I32)
        posf = place("posf", [P, NT], F32)
        freq = place("freq", [P, ROPE // 2], F32)
        assert at[0] <= nc.sbuf_usable_end if isinstance(nc.sbuf_usable_end, int) else True
        print("SBUF", at[0])

        GQ, GKV, CB, CLG, CLB, BS = 0, 2, 3, 5, 7, 9

        ps = ctx.enter_context(nc.psum_tensor("ps", [P, 8, BANK], F32))

        s_wraw = [sem(f"s_wraw{i}") for i in range(2)]
        s_araw = [sem(f"s_araw{i}") for i in range(2)]
        s_xin = [sem(f"s_xin{i}") for i in range(2)]
        s_prep = sem("s_prep")
        s_once = sem("s_once")
        s_store = [sem(f"s_store{i}") for i in range(2)]
        s_cst = sem("s_cst")
        s_hi = sem("s_hi")
        s_lo = sem("s_lo")
        s_araw_used = sem("s_araw_used")
        s_z = sem("s_z")
        s_zev = sem("s_zev")
        s_auxd = [sem(f"s_auxd{i}") for i in range(4)]
        s_auxf = [sem(f"s_auxf{i}") for i in range(4)]
        s_h = sem("s_h")
        s_hhi = sem("s_hhi")
        s_qn = sem("s_qn")
        s_kvn = sem("s_kvn")
        s_kvhi = sem("s_kvhi")
        s_vn = sem("s_vn")
        s_vg = sem("s_vg")
        s_mul = sem("s_mul")
        s_th = sem("s_th")
        s_conv = sem("s_conv")
        s_glu = sem("s_glu")
        s_cln = sem("s_cln")
        s_scaled = sem("s_scaled")
        s_wsT = sem("s_wsT")
        s_uvhi = sem("s_uvhi")
        s_acc = sem("s_acc")
        s_S = sem("s_S")
        s_nmax = sem("s_nmax")
        s_exp = sem("s_exp")
        s_pthi = sem("s_pthi")
        s_qhi = sem("s_qhi")
        s_qrhi = sem("s_qrhi")
        s_vhi = sem("s_vhi")
        s_yhi = sem("s_yhi")
        s_o = sem("s_o")
        s_osq = sem("s_osq")
        s_ofree = sem("s_ofree")
        s_x1 = sem("s_x1")
        s_xsq = sem("s_xsq")
        s_hn = sem("s_hn")
        s_silc = sem("s_silc")
        s_rope = sem("s_rope")
        s_dve = sem("s_dve")
        s_act = sem("s_act")

        ring = BankRing()
        block = ctx.enter_context(nc.Block())

        THIRD = {"shift": 0, "scale": 1, "gate": 2}
        NEED = {"scale": KD + 2, "shift": KD + 1, "gate": KD + 2}

        def ada_jobs():
            jobs = [(0, th, hf) for th in ("scale", "shift") for hf in range(2)]
            for l in range(DEPTH):
                if l + 1 < DEPTH:
                    jobs += [(l + 1, th, hf) for th in ("scale", "shift") for hf in range(2)]
                jobs += [(l, "gate", hf) for hf in range(2)]
            return jobs

        first_piece, n_ada = {}, 0
        for job in ada_jobs():
            first_piece[job] = n_ada
            n_ada += NEED[job[1]]
        ada_number = {job: i for i, job in enumerate(ada_jobs())}

        def piece_used(eng, n):
            job = max((j for j in first_piece if first_piece[j] <= n), key=first_piece.get)
            j = n - first_piece[job]
            others = sum(NEED[x[1]] - 2 for x in ada_jobs()[:ada_number[job]])
            if j == KD - 1:
                eng.wait_ge(s_acc, ada_number[job] + 1)
            elif j == KD:
                emptied(eng, ("ada", *job))
            else:
                eng.wait_ge(s_araw_used, others + (j + 1 if j < KD else KD))

        def aux_ready(eng, name):
            b, n = ring.uses[name]
            eng.wait_ge(s_auxd[b], n + 1)
            return ps[:, 4 + b, :]

        def emptied(eng, name):
            b, n = ring.uses[name]
            eng.wait_ge(s_auxf[b], n + 1)

        def aux_release(ins, name):
            return ins.then_inc(s_auxf[ring.uses[name][0]], 1)

        PREP = 14

        def prep_all(l):
            return (l + 1) * PREP * 16

        def conv_taps(l, ct, k, half):
            return ((l * 2 + ct) * CONV_K + k) * 2 + half + 1

        def pt_count(l, n, b):
            h, i = n // NT, n % NT
            per_head = NT + NT // 2
            before = i + max(0, i - 4)
            return (l * HEADS + h) * per_head + before + b + 1

        @block.tensor
        def _(pe):
            mm = nc.tensor.matmul

            def take(name):
                b, n = ring.take(name)
                if n:
                    pe.wait_ge(s_auxf[b], n)
                return ps[:, 4 + b, :], s_auxd[b]

            def three(out_, a_hi, a_lo, b_hi, b_lo, first=True, last=True):
                mm(out_, a_hi, b_hi, start=first, stop=False)
                mm(out_, a_hi, b_lo, start=False, stop=False)
                return mm(out_, a_lo, b_hi, start=False, stop=last)

            def ada(l, third, half):
                bank, done = take(("ada", l, third, half))
                pe.wait_ge(s_acc, ada_number[l, third, half] + 1)
                mm(bank, ones[:, :], acc[:, half * BANK:(half + 1) * BANK], start=True, stop=True).then_inc(done, 1)

            def h_transpose(l, t):
                for a_ in range(2):
                    bank, done = take(("hT", l, t, a_))
                    pe.wait_ge(s_h, l * NT + t + 1)
                    for j in range(4):
                        k = 4 * a_ + j
                        ins = nc.tensor.transpose(bank[:, j * P:(j + 1) * P], Y[:, t, k * P:(k + 1) * P], ident[:, :])
                    ins.then_inc(done, 1)

            def z(l, c, i):
                u = l * UNITS + unit(c, i)
                if u >= 4:
                    pe.wait_ge(s_zev, u - 3)
                if i == 0:
                    pe.wait_ge(s_lo, l * W_PIECES + 2 * c + 2)
                slot = (l * NCH + c) % 2
                width = CHUNKS[c][1]
                if c in (CONV_A, CONV_B):
                    ct, half = i // 2, i % 2
                    if c == CONV_A:
                        emptied(pe, ("hT", l, 4 * half + 3, 1))
                    o = ps[:, u % 4, :]
                    for k in range(KD):
                        cs = slice(ct * P, (ct + 1) * P)
                        ts = slice(half * BANK, (half + 1) * BANK)
                        ins = three(o, w_hi[:, slot, k, cs], w_lo[:, slot, k, cs], act_hi[:, k, ts], act_lo[:, k, ts],
                                    k == 0, k == KD - 1)
                else:
                    if c == Q:
                        emptied(pe, ("hT", l, i, 1))
                    o = ps[:, u % 4, 0:width]
                    for k in range(KD):
                        ts = slice(i * P, (i + 1) * P)
                        ins = three(o, act_hi[:, k, ts], act_lo[:, k, ts], w_hi[:, slot, k, 0:width],
                                    w_lo[:, slot, k, 0:width], k == 0, k == KD - 1)
                ins.then_inc(s_z, 1)

            def q_transpose(l, t):
                bank, done = take(("qT", l, t))
                pe.wait_ge(s_qn, l * NT + t + 1)
                for k in range(2):
                    ins = nc.tensor.transpose(bank[:, k * P:(k + 1) * P], qtmp[:, t % 2, k * P:(k + 1) * P], ident[:, :])
                ins.then_inc(done, 1)

            def kv_transpose(l, t):
                bank, done = take(("kvT", l, t))
                pe.wait_ge(s_kvn, l * NT + t + 1)
                nc.tensor.transpose(bank[:, 0:P], qtmp[:, t % 2, 0:P], ident[:, :])
                nc.tensor.transpose(bank[0:ROPE, P:2 * P], qtmp[:, t % 2, P:P + ROPE], ident[:, :]).then_inc(done, 1)

            def taps_transpose(l):
                bank, done = take(("taps", l))
                pe.wait_ge(s_prep, prep_all(l))
                for ct in range(2):
                    ins = nc.tensor.transpose(bank[:, ct * 32:ct * 32 + CONV_K], gtmp[0:CONV_K, 0, ct * P:(ct + 1) * P],
                                              ident[0:CONV_K, 0:CONV_K])
                ins.then_inc(done, 1)

            def ws_transpose(l):
                bank, done = take(("ws", l))
                for g in range(HEADS):
                    ins = nc.tensor.transpose(bank[:, g * P:(g + 1) * P], ws_raw[:, g, :], ident[:, :])
                ins.then_inc(done, 1)

            def u_transpose(l, h):
                bank, done = take(("uT", l, h))
                if h == 0:
                    pe.wait_ge(s_scaled, l + 1)
                for k in range(2):
                    nc.tensor.transpose(bank[:, k * P:(k + 1) * P], uq_raw[:, k, h, 0:NOPE], ident[:, :])
                nc.tensor.transpose(bank[:, 2 * P:3 * P], uk_raw[:, h, :], ident[:, :]).then_inc(done, 1)

            def absorb(l, h):
                bank, done = take(("Wq", l, h))
                emptied(pe, ("uT", l, h))
                g = gtmp[:, :, :].rearrange("p a b -> p (a b)")
                for k in range(2):
                    ins = mm(bank[:, k * P:(k + 1) * P], g[:, k * P:(k + 1) * P], g[:, 2 * P:3 * P], start=True, stop=True)
                ins.then_inc(done, 1)

            def spatial(l, t):
                bank, done = take(("sgu", l, t))
                pe.wait_ge(s_vg, l * NT + t + 1)
                if t == 0:
                    pe.wait_ge(s_wsT, l + 1)
                for g in range(HEADS):
                    ins = mm(bank[:, g * 64:(g + 1) * 64], wsT[:, g, :], gtmp[:, t % 2, g * 64:(g + 1) * 64],
                             start=True, stop=True)
                ins.then_inc(done, 1)

            def conv_to_token(l, ct):
                for half in range(2):
                    bank, done = take(("cT", l, ct, half))
                    pe.wait_ge(s_conv, conv_taps(l, ct, CONV_K - 1, half))
                    for j in range(4):
                        ins = nc.tensor.transpose(bank[:, j * P:(j + 1) * P], convo[:, half, j * P:(j + 1) * P], ident[:, :])
                    ins.then_inc(done, 1)

            def conv_to_feature(l, half):
                for ct in range(2):
                    bank, done = take(("cB", l, ct, half))
                    pe.wait_ge(s_cln, l * NT + 4 * half + 4)
                    for j in range(4):
                        cs = Y_CONV + ct * P
                        ins = nc.tensor.transpose(bank[:, j * P:(j + 1) * P], Y[:, 4 * half + j, cs:cs + P], ident[:, :])
                    ins.then_inc(done, 1)

            def pointwise(l, t):
                bank, done = take(("pw", l, t))
                emptied(pe, ("cB", l, 1, t // 4))
                for ct in range(2):
                    ins = mm(bank[:, 0:CW], convh[:, ct, HALO + t * P:HALO + (t + 1) * P], pw2[:, ct, :],
                             start=ct == 0, stop=ct == 1)
                ins.then_inc(done, 1)

            def q_rope(l, pair, b):
                bank, done = take(("RT", l, pair, b))
                emptied(pe, ("qT", l, NT - 1))
                for j in range(4):
                    t = 4 * b + j
                    for k in range(2):
                        ins = mm(bank[:, j * P:(j + 1) * P], qnT[:, k, t * P:(t + 1) * P],
                                 uqr[:, k, 2 * pair:2 * pair + 2, :], start=k == 0, stop=k == 1)
                ins.then_inc(done, 1)

            def queries(l, h):
                for b in range(2):
                    bank, done = take(("QA", l, h, b))
                    emptied(pe, ("Wq", l, HEADS - 1))
                    for k in range(2):
                        ins = mm(bank, Wq[:, k, h, :], qnT[:, k, b * BANK:(b + 1) * BANK], start=k == 0, stop=k == 1)
                    ins.then_inc(done, 1)
                for b in range(2):
                    bank, done = take(("qr", l, h, b))
                    emptied(pe, ("RT", l, h // 2, b))
                    for j in range(4):
                        ins = nc.tensor.transpose(bank[0:ROPE, j * P:(j + 1) * P], qrt[:, 4 * b + j, h % 2, :], ident[:, :])
                    ins.then_inc(done, 1)

            def values(l, h):
                for b in range(2):
                    bank, done = take(("V", l, h, b))
                    emptied(pe, ("kvT", l, NT - 1))
                    for j in range(4):
                        ts = slice((4 * b + j) * P, (4 * b + j + 1) * P)
                        ins = three(bank[:, j * P:(j + 1) * P], kv_hi[:, ts], kv_lo[:, ts], uv_hi[:, h, :], uv_lo[:, h, :])
                    ins.then_inc(done, 1)

            def scores(l, n):
                h, i = n // NT, n % NT
                g = l * STEPS + n
                if n >= 2:
                    pe.wait_ge(s_exp, g - 1)
                if n < 2:
                    pe.wait_ge(s_zev, (l + 1) * UNITS)
                if i == 0:
                    emptied(pe, ("QA", l, h, 1))
                    emptied(pe, ("qr", l, h, 1))
                qs = slice(i * P, (i + 1) * P)
                for b in range(i // 4 + 1):
                    n_keys = min(BANK, (i + 1) * P - b * BANK)
                    ks = slice(b * BANK, b * BANK + n_keys)
                    o = ps[:, 2 * (n % 2) + b, 0:n_keys]
                    three(o, q_hi[:, qs], q_lo[:, qs], kv_hi[:, ks], kv_lo[:, ks], True, False)
                    mm(o, qr_st[:, qs], kr_st[:, ks], start=False, stop=False)
                    diagonal = b == i // 4
                    ins = mm(o, qr_lo[:, qs], kr_st[0:ROPE, ks], start=False, stop=not diagonal)
                    if diagonal:
                        ins = mm(o[:, n_keys - P:n_keys], ident_r[:, :], mask_r[:, :], start=False, stop=True)
                ins.then_inc(s_S, 1)

            def p_transpose(l, n):
                i = n % NT
                for b in range(i // 4 + 1):
                    bank, done = take(("PT", l, n, b))
                    pe.wait_ge(s_exp, l * STEPS + n + 1)
                    for j in range(min(4, i + 1 - 4 * b)):
                        kbk = 4 * b + j
                        ins = nc.tensor.transpose(bank[:, j * P:(j + 1) * P], xb[:, n % 2, kbk * P:(kbk + 1) * P], ident[:, :])
                    ins.then_inc(done, 1)

            def pv(l, n):
                h, i = n // NT, n % NT
                bank, done = take(("O", l, n))
                if i == 0:
                    emptied(pe, ("V", l, h, 1))
                emptied(pe, ("PT", l, n, i // 4))
                for k in range(i + 1):
                    ins = three(bank[:, 0:P], pt_hi[:, k, :], pt_lo[:, k, :], v_hi[:, k, :], v_lo[:, k, :], k == 0, k == i)
                ins.then_inc(done, 1)

            def y_transpose(l, t):
                for a_ in range(2):
                    bank, done = take(("yT", l, t, a_))
                    if a_ == 0:
                        emptied(pe, ("O", l, (HEADS - 1) * NT + t))
                    else:
                        emptied(pe, ("pw", l, t))
                        pe.wait_ge(s_mul, (l * 2 + 1) * NT + t + 1)
                    for j in range(4):
                        k = 4 * a_ + j
                        ins = nc.tensor.transpose(bank[:, j * P:(j + 1) * P], Y[:, t, k * P:(k + 1) * P], ident[:, :])
                    ins.then_inc(done, 1)

            def out_proj(l, t):
                g = l * NT + t
                if t >= 2:
                    pe.wait_ge(s_ofree, g - 1)
                else:
                    pe.wait_ge(s_exp, (l + 1) * STEPS)
                emptied(pe, ("yT", l, t, 1))
                if t == 0:
                    pe.wait_ge(s_lo, (l + 1) * W_PIECES)
                for half in range(2):
                    o = ps[:, 2 * (t % 2) + half, :]
                    hs = slice(half * BANK, (half + 1) * BANK)
                    for k in range(KD):
                        ins = three(o, yT_hi[:, t % 2, k, :], yT_lo[:, t % 2, k, :], act_hi[:, k, hs], act_lo[:, k, hs],
                                    k == 0, k == KD - 1)
                ins.then_inc(s_o, 1)

            pe.wait_ge(s_cst, 6)
            for third in ("scale", "shift"):
                for half in range(2):
                    ada(0, third, half)
            for l in range(DEPTH):
                for t in range(3):
                    h_transpose(l, t)
                for t in range(NT):
                    z(l, Q, t)
                    if t + 3 < NT:
                        h_transpose(l, t + 3)
                    if t >= 2:
                        q_transpose(l, t - 2)
                z(l, CONV_A, 0)
                q_transpose(l, 6)
                q_transpose(l, 7)
                z(l, CONV_A, 1)
                taps_transpose(l)
                ws_transpose(l)
                z(l, CONV_A, 2)
                u_transpose(l, 0)
                z(l, CONV_A, 3)
                for i in range(4):
                    absorb(l, i)
                    if i < 3:
                        u_transpose(l, i + 1)
                    z(l, CONV_B, i)
                for t in range(NT):
                    z(l, KV, t)
                    if t >= 3:
                        kv_transpose(l, t - 3)
                    if t in (1, 2) and l + 1 < DEPTH:
                        ada(l + 1, "scale", t - 1)
                for t in range(NT):
                    z(l, SGU_V, t)
                    if t < 3:
                        kv_transpose(l, 5 + t)
                    if t >= 4:
                        spatial(l, t - 4)
                for t in range(NT):
                    z(l, SGU_U, t)
                    if t < 4:
                        spatial(l, 4 + t)
                for t in range(NT):
                    z(l, G_ATT0, t)
                    if t == 0:
                        conv_to_token(l, 0)
                for t in range(NT):
                    z(l, G_ATT1, t)
                for t in range(NT):
                    z(l, G_SGU, t)
                    if t == 1:
                        conv_to_token(l, 1)
                for t in range(NT):
                    z(l, G_CONV, t)
                    if t == 1:
                        conv_to_feature(l, 0)
                        conv_to_feature(l, 1)
                    if t in (4, 5):
                        q_rope(l, 0, t - 4)
                    if t in (6, 7) and l + 1 < DEPTH:
                        ada(l + 1, "shift", t - 6)
                queries(l, 0)
                values(l, 0)
                scores(l, 0)
                for n in range(STEPS):
                    i = n % NT
                    last_of_head = i == NT - 1
                    if last_of_head and n + 1 < STEPS:
                        queries(l, n // NT + 1)
                    elif n + 1 < STEPS:
                        scores(l, n + 1)
                    if i > 0:
                        pv(l, n - 1)
                    if n < NT:
                        pointwise(l, n)
                    p_transpose(l, n)
                    if n in (11, 12):
                        q_rope(l, 1, n - 11)
                    if n in (22, 30):
                        ada(l, "gate", (n - 22) // 8)
                    if last_of_head:
                        pv(l, n)
                        if n + 1 < STEPS:
                            values(l, n // NT + 1)
                            scores(l, n + 1)
                y_transpose(l, 0)
                for t in range(NT):
                    if t + 1 < NT:
                        y_transpose(l, t + 1)
                    out_proj(l, t)

        @block.sync
        def _(sp):
            for tile_, src in ((silu_c[:, KD:2 * KD], a["c"].rearrange("b (k p) -> p (b k)", p=P)),
                               (posi[:, :], a["positions"].rearrange("b (t p) -> p (b t)", p=P)),
                               (freq[:, :], a["inv_freq"].partition_broadcast(P))):
                sp.dma_start(tile_, src, allow_slow_non_contiguous=True).then_inc(s_once, 16)

            def ada_piece(job, j):
                l, third, half = job
                n = first_piece[job] + j
                if n >= 2:
                    piece_used(sp, n - 2)
                c0 = THIRD[third] * D + half * BANK
                if j < KD:
                    src = a["w_ada"][l, j * P:(j + 1) * P, c0:c0 + BANK]
                elif j == KD:
                    src = a["b_ada"][l, c0:c0 + BANK].partition_broadcast(P)
                else:
                    gain = a["g_pre"] if third == "scale" else a["g_post"]
                    src = gain[l, half * BANK:(half + 1) * BANK].partition_broadcast(P)
                sp.dma_start(araw[:, n % 2, :], src).then_inc(s_araw[n % 2], 16)

            def ada_job(*job):
                for j in range(NEED[job[1]]):
                    ada_piece(job, j)

            def w_piece(l, p):
                n = l * W_PIECES + p
                if n >= 2:
                    sp.wait_ge(s_lo, n - 1)
                if p < 2 * NCH:
                    c0, width = CHUNKS[p // 2]
                    k0 = 4 * (p % 2)
                    dst = wraw[:, n % 2, :].rearrange("p (k n) -> p k n", k=4)[:, :, 0:width]
                    src = a["w_in"][l, k0 * P:(k0 + 4) * P, c0:c0 + width].rearrange("(k p) n -> p k n", p=P)
                else:
                    k = p - 2 * NCH
                    dst, src = wraw[:, n % 2, :], a["w_out"][l, k * P:(k + 1) * P, :]
                sp.dma_start(dst, src).then_inc(s_wraw[n % 2], 16)

            def x_tile(l, m, t):
                if m == 0:
                    if t >= 2:
                        sp.wait_ge(s_hn, t - 1)
                    src = a["x"]
                else:
                    if t < 2:
                        emptied(sp, ("PT", l, STEPS - 1, 1))
                    if l > 0:
                        sp.wait_ge(s_store[t % 2], ((l - 1) * NT // 2 + t // 2 + 1) * 16)
                    if t >= 2:
                        sp.wait_ge(s_store[t % 2], (l * NT // 2 + t // 2) * 16)
                        if l + 1 < DEPTH:
                            sp.wait_ge(s_hn, (l + 1) * NT + t - 1)
                    src = a["x"] if l == 0 else x_mid
                sp.dma_start(xb[:, t % 2, :], src[t * P:(t + 1) * P, :]).then_inc(s_xin[t % 2], 16)

            def prep(l):
                if l > 0:
                    sp.wait_ge(s_x1, l * NT)
                    for i in range(2):
                        sp.wait_ge(s_store[i], l * NT // 2 * 16)
                    sp.wait_ge(s_hn, (l + 1) * NT)
                    emptied(sp, ("cB", l - 1, 1, 1))
                    emptied(sp, ("pw", l - 1, NT - 1))
                    emptied(sp, ("kvT", l - 1, NT - 1))
                else:
                    sp.wait_ge(s_hn, NT)
                for dst, src in (
                    (uq_raw[:, :, :, :], a["w_uq"][l].rearrange("(k p) (h n) -> p k h n", p=P, h=HEADS)),
                    (ws_raw[:, :, :], a["w_s"][l].rearrange("g t s -> t g s")),
                    (uk_raw[:, :, :], a["w_ukv"][l].rearrange("p (h n) -> p h n", h=HEADS)[:, :, 0:NOPE]),
                    (uv_raw[:, :, :], a["w_ukv"][l].rearrange("p (h n) -> p h n", h=HEADS)[:, :, NOPE:]),
                    (gtmp[0:CONV_K, 0, :], a["conv_w"][l]),
                    (pw2[:, :, :], a["w_pw2"][l].rearrange("(c p) n -> p c n", p=P)),
                    (sgu_g[:, :], a["sgu_ln_g"][l].partition_broadcast(P)),
                    (sgu_b[:, :], a["sgu_ln_b"][l].partition_broadcast(P)),
                    (cols[:, GQ:GQ + 2], a["q_norm_g"][l].rearrange("(c p) -> p c", p=P)),
                    (cols[:, GKV:GKV + 1], a["kv_norm_g"][l].rearrange("(c p) -> p c", p=P)),
                    (cols[:, CB:CB + 2], a["conv_b"][l].rearrange("(c p) -> p c", p=P)),
                    (cols[:, CLG:CLG + 2], a["conv_ln_g"][l].rearrange("(c p) -> p c", p=P)),
                    (cols[:, CLB:CLB + 2], a["conv_ln_b"][l].rearrange("(c p) -> p c", p=P)),
                    (cols[:, BS:BS + 4], a["b_s"][l].rearrange("g t -> t g")),
                ):
                    sp.dma_start(dst, src, allow_slow_non_contiguous=True).then_inc(s_prep, 16)

            for hf in range(2):
                x_tile(0, 0, hf)
            for third in ("scale", "shift"):
                for hf in range(2):
                    ada_job(0, third, hf)
                if third == "scale":
                    w_piece(0, 0)
                    w_piece(0, 1)
            for t in range(2, NT):
                x_tile(0, 0, t)
            w_piece(0, 2)
            w_piece(0, 3)
            for l in range(DEPTH):
                prep(l)
                for p in range(4, 8):
                    w_piece(l, p)
                for hf in range(2):
                    if l + 1 < DEPTH:
                        ada_job(l + 1, "scale", hf)
                    w_piece(l, 8 + hf)
                for p in range(10, 2 * NCH):
                    w_piece(l, p)
                if l + 1 < DEPTH:
                    for hf in range(2):
                        ada_job(l + 1, "shift", hf)
                gate = [((l, "gate", hf), j) for hf in range(2) for j in range(NEED["gate"])]
                for k, until in enumerate((0, 0, 0, 0, 5, 8, 14, 17)):
                    for job, j in gate[(0, 0, 0, 0, 0, 5, 8, 14)[k]:until]:
                        ada_piece(job, j)
                    w_piece(l, 2 * NCH + k)
                for job, j in gate[17:]:
                    ada_piece(job, j)
                for t in range(NT):
                    x_tile(l, l + 1, t)
                    if 2 <= t < 6 and l + 1 < DEPTH:
                        w_piece(l + 1, t - 2)

        @block.scalar
        def _(act):
            fn = nc.scalar.activation

            def hi_piece(l, p):
                n = l * W_PIECES + p
                act.wait_ge(s_wraw[n % 2], (n // 2 + 1) * 16)
                if p < 2 * NCH:
                    c = p // 2
                    cc = l * NCH + c
                    width = CHUNKS[c][1]
                    if c < 2:
                        if l > 0:
                            aux_ready(act, ("O", l - 1, STEPS - 1))
                    else:
                        act.wait_ge(s_z, l * UNITS + unit(c - 1, 0))
                    dst = w_hi[:, cc % 2, 4 * (p % 2):4 * (p % 2) + 4, 0:width]
                    src = wraw[:, n % 2, :].rearrange("p (k n) -> p k n", k=4)[:, :, 0:width]
                else:
                    act.wait_ge(s_z, (l + 1) * UNITS)
                    dst, src = act_hi[:, p - 2 * NCH, :], wraw[:, n % 2, :]
                fn(dst, src, ACT.Copy).then_inc(s_hi, 1)

            def kv_hi_copy(l, t):
                bank = aux_ready(act, ("kvT", l, t))
                nc.scalar.activation(kv_hi[:, t * P:(t + 1) * P], bank[:, 0:P], ACT.Copy)
                nc.scalar.activation(kr_st[0:ROPE, t * P:(t + 1) * P], bank[0:ROPE, P:2 * P], ACT.Copy).then_inc(s_kvhi, 1)

            def z_ready(l, c, i):
                u = l * UNITS + unit(c, i)
                act.wait_ge(s_z, u + 1)
                return ps[:, u % 4, :]

            def square_sum(src, junk, dst):
                return fn(junk, src, ACT.Square, accum_out=dst)

            def h_hi(l, t):
                for b in range(2):
                    bank = aux_ready(act, ("hT", l, t, b))
                    if l > 0:
                        act.wait_ge(s_o, l * NT)
                    fn(act_hi[:, 4 * b:4 * b + 4, t * P:(t + 1) * P], bank.rearrange("p (k n) -> p k n", k=4),
                       ACT.Copy).then_inc(s_hhi, 1)

            def evac_q(l, t):
                z_ = z_ready(l, Q, t)
                if t >= 2:
                    b, n = ring.uses["qT", l, t - 2]
                    act.wait_ge(s_auxd[b], n + 1)
                elif l > 0:
                    b, n = ring.uses["kvT", l - 1, NT - 1]
                    act.wait_ge(s_auxd[b], n + 1)
                fn(qtmp[:, t % 2, :], z_[:, 0:CW], ACT.Copy)
                if l * UNITS + t:
                    act.wait_ge(s_zev, l * UNITS + unit(Q, t))
                square_sum(z_[:, 0:CW], scr[:, 0:CW], ssq[:, t % 2:t % 2 + 1]).then_inc(s_zev, 1)

            def q_copy(l, t):
                bank = aux_ready(act, ("qT", l, t))
                if l > 0 and t == 0:
                    emptied(act, ("yT", l - 1, NT - 1, 1))
                    act.wait_ge(s_o, l * NT)
                aux_release(fn(qnT[:, :, t * P:(t + 1) * P], bank[:, 0:CW].rearrange("p (k n) -> p k n", k=2),
                               ACT.Copy), ("qT", l, t))

            act.wait_ge(s_once, 48)
            fn(silu_c[:, 0:KD], silu_c[:, KD:2 * KD], ACT.Silu).then_inc(s_silc, 1)
            act.wait_ge(s_rope, 1)
            fn(sind[:, :, ROPE // 2:ROPE], sind[:, :, ROPE // 2:ROPE], ACT.Sin).then_inc(s_act, 1)
            fn(cosd[:, :, 0:ROPE // 2], cosd[:, :, 0:ROPE // 2], ACT.Sin).then_inc(s_act, 1)
            for p in range(2):
                hi_piece(0, p)
            for t in range(NT):
                act.wait_ge(s_xin[t % 2], (t // 2 + 1) * 16)
                square_sum(xb[:, t % 2, :], Y[:, t, :], ssq[:, 4 + t % 2:5 + t % 2]).then_inc(s_xsq, 1)
            for p in range(2, 4):
                hi_piece(0, p)

            for l in range(DEPTH):
                for t in range(3):
                    h_hi(l, t)
                for t in range(NT):
                    evac_q(l, t)
                    if t + 3 < NT:
                        h_hi(l, t + 3)
                    if t >= 2:
                        q_copy(l, t - 2)
                for i in range(4):
                    if i in (1, 2):
                        q_copy(l, 5 + i)
                    z_ = z_ready(l, CONV_A, i)
                    if l > 0:
                        b, n = ring.uses["pw", l - 1, NT - 1]
                        act.wait_ge(s_auxd[b], n + 1)
                    ct, half = i // 2, i % 2
                    fn(convh[:, ct, HALO + half * BANK:HALO + (half + 1) * BANK], z_, ACT.Copy, scale=0.5).then_inc(s_zev, 1)
                    if i >= 2:
                        hi_piece(l, 4 + i - 2)
                for i in range(4):
                    z_ = z_ready(l, CONV_B, i)
                    act.wait_ge(s_glu, l * 4 + i) if l * 4 + i else None
                    if i == 0 and l > 0:
                        emptied(act, ("RT", l - 1, 1, 1))
                    fn(scr[:, :], z_, ACT.Tanh, scale=0.5).then_inc(s_zev, 1)
                    if i >= 2:
                        hi_piece(l, 6 + i - 2)
                for t in range(NT):
                    z_ = z_ready(l, KV, t)
                    if t >= 2:
                        b, n = ring.uses["kvT", l, t - 2]
                    else:
                        b, n = ring.uses["qT", l, NT - 2 + t]
                    act.wait_ge(s_auxd[b], n + 1)
                    fn(qtmp[:, t % 2, 0:KV_RANK + ROPE], z_[:, 0:KV_RANK + ROPE], ACT.Copy)
                    act.wait_ge(s_zev, l * UNITS + unit(KV, t))
                    if t == 0:
                        act.wait_ge(s_glu, l * 4 + 4)
                    square_sum(z_[:, 0:KV_RANK], scr[:, 0:KV_RANK], ssq[:, t % 2:t % 2 + 1]).then_inc(s_zev, 1)
                    if t >= 3:
                        kv_hi_copy(l, t - 3)
                    if t in (2, 5):
                        hi_piece(l, 8 + (t - 2) // 3)
                for t in range(NT):
                    z_ = z_ready(l, SGU_V, t)
                    if t >= 2:
                        b, n = ring.uses["sgu", l, t - 2]
                        act.wait_ge(s_auxd[b], n + 1)
                    else:
                        b, n = ring.uses["Wq", l, HEADS - 1]
                        act.wait_ge(s_auxd[b], n + 1)
                    fn(gtmp[:, t % 2, :], z_[:, 0:CW], ACT.Gelu).then_inc(s_zev, 1)
                    if t < 3:
                        kv_hi_copy(l, 5 + t)
                    if t in (2, 5):
                        hi_piece(l, 10 + (t - 2) // 3)
                for t in range(NT):
                    z_ = z_ready(l, SGU_U, t)
                    if t < 2:
                        b, n = ring.uses["sgu", l, NT - 2 + t]
                        act.wait_ge(s_auxd[b], n + 1)
                    else:
                        act.wait_ge(s_mul, l * 2 * NT + t - 1)
                    fn(gtmp[:, t % 2, :], z_[:, 0:CW], ACT.Gelu).then_inc(s_zev, 1)
                    if t in (2, 5):
                        hi_piece(l, 12 + (t - 2) // 3)
                for c in (G_ATT0, G_ATT1):
                    for t in range(NT):
                        z_ = z_ready(l, c, t)
                        y0 = Y_ATT + (c - G_ATT0) * CW
                        fn(Y[:, t, y0:y0 + CW], z_[:, 0:CW], ACT.Silu).then_inc(s_zev, 1)
                        if t in (2, 5):
                            hi_piece(l, 2 * (c + 1) + (t - 2) // 3)
                for t in range(NT):
                    z_ = z_ready(l, G_SGU, t)
                    act.wait_ge(s_mul, l * 2 * NT + (NT - 1 + t if t < 2 else NT + t - 1))
                    fn(gtmp[:, t % 2, :], z_[:, 0:CW], ACT.Silu).then_inc(s_zev, 1)
                    if t in (2, 5):
                        hi_piece(l, 18 + (t - 2) // 3)

                def conv_silu(half):
                    for ct in range(2):
                        bank = aux_ready(act, ("cB", l, ct, half))
                        act.wait_ge(s_conv, (l + 1) * 2 * 2 * CONV_K)
                        aux_release(fn(convh[:, ct, HALO + half * BANK:HALO + (half + 1) * BANK], bank, ACT.Silu,
                                       scale=cols[:, CLG + ct:CLG + ct + 1], bias=cols[:, CLB + ct:CLB + ct + 1]
                                       ), ("cB", l, ct, half))

                for t in range(NT):
                    z_ = z_ready(l, G_CONV, t)
                    if t in (0, 4):
                        conv_silu(t // 4)
                    fn(Y[:, t, Y_CONV:Y_CONV + CW], z_[:, 0:CW], ACT.Silu).then_inc(s_zev, 1)

                def q_split(h):
                    for b in range(2):
                        bank = aux_ready(act, ("QA", l, h, b))
                        if h == 0 and b == 0:
                            act.wait_ge(s_z, (l + 1) * UNITS)
                        if h > 0 and b == 0:
                            act.wait_ge(s_S, l * STEPS + h * NT)
                        fn(q_hi[:, b * BANK:(b + 1) * BANK], bank, ACT.Copy).then_inc(s_qhi, 1)
                    for b in range(2):
                        bank = aux_ready(act, ("qr", l, h, b))
                        for r in range(2):
                            ins = fn(qr_st[r * ROPE:(r + 1) * ROPE, b * BANK:(b + 1) * BANK], bank[0:ROPE, :], ACT.Copy)
                        ins.then_inc(s_qrhi, 1)

                def v_split(h):
                    for b in range(2):
                        bank = aux_ready(act, ("V", l, h, b))
                        fn(v_hi[:, 4 * b:4 * b + 4, :], bank.rearrange("p (k n) -> p k n", k=4), ACT.Copy).then_inc(s_vhi, 1)

                q_split(0)
                v_split(0)
                for n in range(STEPS):
                    i = n % NT
                    keys = (i + 1) * P
                    act.wait_ge(s_nmax, l * STEPS + n + 1)
                    if n >= 2:
                        emptied(act, ("PT", l, n - 2, (i - 2) // 4 if i >= 2 else 1))
                        emptied(act, ("O", l, n - 2))
                    src = ps[:, 2 * (n % 2):2 * (n % 2) + 2, :].rearrange("p a b -> p (a b)")[:, 0:keys]
                    fn(xb[:, n % 2, 0:keys], src, ACT.Exp, bias=nmax[:, n % 2:n % 2 + 1],
                       accum_out=rsum[:, n % 2:n % 2 + 1]).then_inc(s_exp, 1)
                    if i == NT - 1 and n + 1 < STEPS:
                        q_split(n // NT + 1)
                    for b in range(i // 4 + 1):
                        bank = aux_ready(act, ("PT", l, n, b))
                        if i > 0 and b == 0:
                            ob, on = ring.uses["O", l, n - 1]
                            act.wait_ge(s_auxd[ob], on + 1)
                        m = min(4, i + 1 - 4 * b)
                        fn(pt_hi[:, 4 * b:4 * b + m, :], bank[:, 0:m * P].rearrange("p (k n) -> p k n", k=m),
                           ACT.Copy).then_inc(s_pthi, 1)
                    if i == NT - 1 and n + 1 < STEPS:
                        v_split(n // NT + 1)
                    if i in (2, 5):
                        hi_piece(l, 2 * NCH + 2 * (n // NT) + (i - 2) // 3)

                def y_hi(t):
                    for b in range(2):
                        bank = aux_ready(act, ("yT", l, t, b))
                        if t >= 2:
                            act.wait_ge(s_o, l * NT + t - 1)
                        else:
                            act.wait_ge(s_S, (l + 1) * STEPS)
                        fn(yT_hi[:, t % 2, 4 * b:4 * b + 4, :], bank.rearrange("p (k n) -> p k n", k=4),
                           ACT.Copy).then_inc(s_yhi, 1)

                y_hi(0)
                for t in range(NT):
                    g = l * NT + t
                    if t + 1 < NT:
                        y_hi(t + 1)
                    act.wait_ge(s_o, g + 1)
                    src = ps[:, 2 * (t % 2):2 * (t % 2) + 2, :].rearrange("p a b -> p (a b)")
                    square_sum(src, Y[:, t, :], ssq[:, 2 + t % 2:3 + t % 2]).then_inc(s_osq, 1)
                    act.wait_ge(s_x1, g + 1)
                    dst = out if l + 1 == DEPTH else x_mid
                    act.dma_start(dst[t * P:(t + 1) * P, :], xb[:, t % 2, :]).then_inc(s_store[t % 2], 16)
                    if l + 1 < DEPTH:
                        square_sum(xb[:, t % 2, :], Y[:, t, :], ssq[:, 4 + t % 2:5 + t % 2]).then_inc(s_xsq, 1)
                        if 3 <= t < 7:
                            hi_piece(l + 1, t - 3)
            for i in range(2):
                act.wait_ge(s_store[i], DEPTH * NT // 2 * 16)

        @block.vector
        def _(dve):
            v = nc.vector
            chain = [0]

            def link(ins):
                chain[0] += 1
                ins.then_inc(s_dve, 1)
                dve.wait_ge(s_dve, chain[0])

            def r_sqrt(src, n, scale, y, tmp):
                link(v.tensor_scalar(tmp[:, 0:n], src, scale, EPS, ALU.mult, ALU.add))
                link(v.tensor_scalar(y.bitcast(I32), tmp[:, 0:n].bitcast(I32), -0.5, float(0x5F3759DF), ALU.mult, ALU.add))
                link(v.tensor_scalar(tmp[:, 0:n], tmp[:, 0:n], -0.5, None, ALU.mult))
                for _ in range(3):
                    if n == 1:
                        link(v.scalar_tensor_tensor(tmp[:, 8:9], y, y, tmp[:, 0:1], ALU.mult, ALU.mult))
                    else:
                        link(v.tensor_tensor(tmp[:, 8:8 + n], y, y, ALU.mult))
                        link(v.tensor_tensor(tmp[:, 8:8 + n], tmp[:, 8:8 + n], tmp[:, 0:n], ALU.mult))
                    link(v.scalar_tensor_tensor(y, tmp[:, 8:8 + n], 1.5, y, ALU.add, ALU.mult))

            TMP = st[:, 0:16]
            RS = st[:, 16:17]

            def lo_split(dst, bank, hi, s_from, value, name):
                dve.wait_ge(s_from, value)
                aux_release(v.tensor_tensor(dst, bank, hi.bitcast(F32), ALU.subtract), name)

            def ada_piece(job, j):
                l, third, half = job
                n = first_piece[job] + j
                dve.wait_ge(s_araw[n % 2], (n // 2 + 1) * 16)
                w = araw[:, n % 2, :]
                o = acc[:, half * BANK:(half + 1) * BANK]
                sc = silu_c[:, j:j + 1] if j < KD else None
                if j == 0:
                    if ada_number[job] >= 2:
                        prev = ada_jobs()[ada_number[job] - 2]
                        aux_ready(dve, ("ada", *prev))
                    ins = v.tensor_scalar(o, w, sc, None, ALU.mult).then_inc(s_araw_used, 1)
                else:
                    piece_used(dve, n - 1)
                    ins = v.scalar_tensor_tensor(o, w, sc, o, ALU.mult, ALU.add)
                    ins.then_inc(s_acc if j == KD - 1 else s_araw_used, 1)

            def ada_finish(job):
                l, third, half = job
                n = first_piece[job] + KD
                hs = slice(half * BANK, (half + 1) * BANK)
                dst = {"scale": A_bc, "shift": S_bc, "gate": acc}[third][:, hs]
                bank = aux_ready(dve, ("ada", *job))
                dve.wait_ge(s_araw[n % 2], (n // 2 + 1) * 16)
                aux_release(v.tensor_tensor(dst, bank, araw[:, n % 2, :], ALU.add), ("ada", *job))
                if third == "shift":
                    return
                n += 1
                dve.wait_ge(s_araw[n % 2], (n // 2 + 1) * 16)
                piece_used(dve, n - 1)
                v.scalar_tensor_tensor(dst, dst, 1.0 if third == "scale" else 0.0, araw[:, n % 2, :], ALU.add,
                                       ALU.mult).then_inc(s_araw_used, 1)

            def ada_job(*job):
                for j in range(KD):
                    ada_piece(job, j)
                ada_finish(job)

            def h_norm(g, t):
                dve.wait_ge(s_xsq, g * NT + t + 1)
                r_sqrt(ssq[:, 4 + t % 2:5 + t % 2], 1, 1.0 / D, RS, TMP)
                v.scalar_tensor_tensor(Y[:, t, :], xb[:, t % 2, :], RS, A_bc[:, :], ALU.mult, ALU.mult).then_inc(s_hn, 1)

            dve.wait_ge(s_once, 48)
            link(v.memset(st[:, :], 0.0))
            dve.wait_ge(s_silc, 1)
            for third in ("scale",):
                for half in range(2):
                    ada_job(0, third, half)
            link(v.tensor_copy(posf[:, :], posi[:, :]))
            half_ = ROPE // 2
            ang = sind[:, :, half_:ROPE]
            turns = sind[:, :, 0:half_]
            for t in range(NT):
                ins = v.tensor_scalar(sind[:, t, half_:ROPE], freq[:, :], posf[:, t:t + 1], None, ALU.mult)
            link(ins)
            TWO_PI = 6.283185307179586
            link(v.tensor_scalar(turns, ang, 1.0 / TWO_PI, None, ALU.mult))
            turns_i = cosd[:, :, half_:ROPE].bitcast(I32)
            link(v.tensor_copy(turns_i, turns))
            link(v.tensor_copy(turns, turns_i))
            rest = TWO_PI
            parts = []
            for bits in (5, 15, 24):
                q = round(rest * 2.0 ** bits) / 2.0 ** bits
                parts.append(q)
                rest -= q
            for part in parts + [rest]:
                link(v.scalar_tensor_tensor(ang, turns, -part, ang, ALU.mult, ALU.add))
            PI = 3.1415925
            link(v.tensor_scalar(ang, ang, PI, -PI, ALU.min, ALU.max))
            cosv = cosd[:, :, 0:half_]
            link(v.tensor_scalar(cosv, ang, -1.0, None, ALU.mult))
            link(v.tensor_tensor(cosv, cosv, ang, ALU.min))
            v.tensor_scalar(cosv, cosv, TWO_PI / 4, None, ALU.add).then_inc(s_rope, 1)
            for half in range(2):
                ada_job(0, "shift", half)
            dve.wait_ge(s_act, 2)
            v.tensor_scalar(sind[:, :, 0:half_], ang, -1.0, None, ALU.mult)
            link(v.tensor_copy(cosd[:, :, half_:ROPE], cosv))
            for t in range(NT):
                h_norm(0, t)

            def h_lo(l, t):
                for b in range(2):
                    name = ("hT", l, t, b)
                    bank = aux_ready(dve, name)
                    sl = (slice(None), slice(4 * b, 4 * b + 4), slice(t * P, (t + 1) * P))
                    lo_split(act_lo[sl], bank.rearrange("p (k n) -> p k n", k=4), act_hi[sl], s_hhi,
                             (l * NT + t) * 2 + b + 1, name)

            def q_norm(l, t):
                dve.wait_ge(s_zev, l * UNITS + unit(Q, t) + 1)
                r_sqrt(ssq[:, t % 2:t % 2 + 1], 1, 1.0 / Q_RANK, RS, TMP)
                v.tensor_scalar(qtmp[:, t % 2, :], qtmp[:, t % 2, :], RS, None, ALU.mult).then_inc(s_qn, 1)

            def rope(dst, src, cos, sin, t1, t2):
                h2 = ROPE // 2
                v.tensor_tensor(t1, src, cos, ALU.mult)
                v.tensor_tensor(t2[:, :, 0:h2], src[:, :, h2:ROPE], sin[:, :, 0:h2], ALU.mult)
                link(v.tensor_tensor(t2[:, :, h2:ROPE], src[:, :, 0:h2], sin[:, :, h2:ROPE], ALU.mult))
                return v.tensor_tensor(dst, t1, t2, ALU.add)

            def kv_norm(l, t):
                dve.wait_ge(s_zev, l * UNITS + unit(KV, t) + 1)
                r_sqrt(ssq[:, t % 2:t % 2 + 1], 1, 1.0 / KV_RANK, RS, TMP)
                v.tensor_scalar(qtmp[:, t % 2, 0:P], qtmp[:, t % 2, 0:P], RS, None, ALU.mult)
                kr = qtmp[:, t % 2:t % 2 + 1, P:P + ROPE]
                t1 = scr[:, 256:256 + ROPE].rearrange("p (a n) -> p a n", a=1)
                t2 = scr[:, 384:384 + ROPE].rearrange("p (a n) -> p a n", a=1)
                rope(kr, kr, cosd[:, t:t + 1, :], sind[:, t:t + 1, :], t1, t2).then_inc(s_kvn, 1)

            def kv_lo_split(l, t):
                name = ("kvT", l, t)
                bank = aux_ready(dve, name)
                ts = slice(t * P, (t + 1) * P)
                dve.wait_ge(s_kvhi, l * NT + t + 1)
                v.tensor_tensor(kv_lo[:, ts], bank[:, 0:P], kv_hi[:, ts].bitcast(F32), ALU.subtract)
                aux_release(v.tensor_tensor(kr_st[ROPE:P, ts], bank[0:ROPE, P:2 * P], kr_st[0:ROPE, ts].bitcast(F32),
                                            ALU.subtract), name)

            pairs = [(ct, k) for ct in range(2) for k in range(CONV_K)]

            def conv_pair(l, m):
                if m >= len(pairs):
                    return
                ct, k = pairs[m]
                for half in range(2):
                    n = conv_taps(l, ct, k, half)
                    src = convh[:, ct, k + half * BANK:k + (half + 1) * BANK]
                    o = convo[:, half, :]
                    if k == 0:
                        if ct == 1:
                            aux_ready(dve, ("cT", l, 0, half))
                        v.tensor_scalar(o, src, taps[:, ct, 0:1], cols[:, CB + ct:CB + ct + 1], ALU.mult,
                                        ALU.add).then_inc(s_conv, 1)
                    else:
                        dve.wait_ge(s_conv, n - 2)
                        v.scalar_tensor_tensor(o, src, taps[:, ct, k:k + 1], o, ALU.mult, ALU.add).then_inc(s_conv, 1)

            def small_weights(l):
                dve.wait_ge(s_prep, prep_all(l))
                link(v.tensor_scalar(cols[:, 16:18], cols[:, GQ:GQ + 2], SCALE, None, ALU.mult))
                for k in range(2):
                    ins = v.tensor_scalar(uq_raw[:, k, :, :], uq_raw[:, k, :, :], cols[:, 16 + k:17 + k], None, ALU.mult)
                v.tensor_scalar(uk_raw[:, :, :], uk_raw[:, :, :], cols[:, GKV:GKV + 1], None, ALU.mult)
                link(v.tensor_scalar(uv_raw[:, :, :], uv_raw[:, :, :], cols[:, GKV:GKV + 1], None, ALU.mult))
                link(v.tensor_copy(uv_hi[:, :, :], uv_raw[:, :, :]))
                v.tensor_tensor(uv_lo[:, :, :], uv_raw[:, :, :], uv_hi[:, :, :].bitcast(F32), ALU.subtract)
                v.tensor_copy(uqr[:, :, :, :], uq_raw[:, :, :, NOPE:NOPE + ROPE]).then_inc(s_scaled, 1)

            def sgu_norm(l, t):
                dve.wait_ge(s_zev, l * UNITS + unit(SGU_V, t) + 1)
                link(v.bn_stats(bst[:, 0, :], gtmp[:, t % 2, :]))
                link(v.bn_aggr(mv[:, 0, :], bst[:, 0, :]))
                r_sqrt(mv[:, 0, 1:2], 1, 1.0, RS, TMP)
                v.tensor_scalar(gtmp[:, t % 2, :], gtmp[:, t % 2, :], mv[:, 0, 0:1], RS, ALU.subtract,
                                ALU.mult).then_inc(s_vn, 1)

            def sgu_mix(l, t):
                name = ("sgu", l, t)
                bank = aux_ready(dve, name)
                bias = cols[:, BS:BS + 4].unsqueeze(2).to_broadcast([P, HEADS, 64])
                o = Y[:, t, Y_SGU:Y_SGU + CW].rearrange("p (g n) -> p g n", g=HEADS)
                aux_release(v.tensor_tensor(o, bank[:, 0:CW].rearrange("p (g n) -> p g n", g=HEADS), bias,
                                            ALU.add), name)

            def conv_token(l, ct):
                for half in range(2):
                    name = ("cT", l, ct, half)
                    bank = aux_ready(dve, name)
                    aux_release(v.tensor_copy(Y[:, 4 * half:4 * half + 4, Y_CONV + ct * P:Y_CONV + (ct + 1) * P],
                                              bank.rearrange("p (k n) -> p k n", k=4)), name)

            def conv_norm(l):
                emptied(dve, ("cT", l, 1, 1))
                for t in range(NT):
                    ins = v.bn_stats(bst[:, t, :], Y[:, t, Y_CONV:Y_CONV + CW])
                link(ins)
                for t in range(NT):
                    ins = v.bn_aggr(mv[:, t, :], bst[:, t, :])
                link(ins)
                r_sqrt(mv[:, :, 1], NT, 1.0, st[:, 24:24 + NT], TMP)
                for t in range(NT):
                    yc = Y[:, t, Y_CONV:Y_CONV + CW]
                    v.tensor_scalar(yc, yc, mv[:, t, 0:1], st[:, 24 + t:25 + t], ALU.subtract, ALU.mult).then_inc(s_cln, 1)

            def q_rotate(l, pair, b):
                name = ("RT", l, pair, b)
                bank = aux_ready(dve, name)
                if pair == 0:
                    aux_ready(dve, ("cT", l, 1, b))
                else:
                    aux_ready(dve, ("qr", l, 1, b))
                if b == 1:
                    emptied(dve, ("RT", l, pair, 0))
                for h in range(2):
                    src = bank.rearrange("p (t h n) -> p t h n", t=4, h=2)[:, :, h, :]
                    t1 = scr[:, 0:256].rearrange("p (a n) -> p a n", a=4)
                    t2 = scr[:, 256:512].rearrange("p (a n) -> p a n", a=4)
                    ins = rope(qrt[:, 4 * b:4 * b + 4, h, :], src, cosd[:, 4 * b:4 * b + 4, :],
                               sind[:, 4 * b:4 * b + 4, :], t1, t2)
                    if h == 0:
                        link(ins)
                aux_release(ins, name)

            def q_lo_split(l, h):
                for b in range(2):
                    name = ("QA", l, h, b)
                    bs = slice(b * BANK, (b + 1) * BANK)
                    lo_split(q_lo[:, bs], aux_ready(dve, name), q_hi[:, bs], s_qhi, (l * HEADS + h) * 2 + b + 1, name)
                for b in range(2):
                    name = ("qr", l, h, b)
                    bs = slice(b * BANK, (b + 1) * BANK)
                    lo_split(qr_lo[:, bs], aux_ready(dve, name)[0:ROPE, :], qr_st[0:ROPE, bs], s_qrhi,
                             (l * HEADS + h) * 2 + b + 1, name)

            def v_lo_split(l, h):
                for b in range(2):
                    name = ("V", l, h, b)
                    sl = (slice(None), slice(4 * b, 4 * b + 4), slice(None))
                    lo_split(v_lo[sl], aux_ready(dve, name).rearrange("p (k n) -> p k n", k=4), v_hi[sl], s_vhi,
                             (l * HEADS + h) * 2 + b + 1, name)

            def row_max(l, n):
                keys = (n % NT + 1) * P
                dve.wait_ge(s_S, l * STEPS + n + 1)
                if n >= 2:
                    dve.wait_ge(s_exp, l * STEPS + n - 1)
                src = ps[:, 2 * (n % 2):2 * (n % 2) + 2, :].rearrange("p a b -> p (a b)")[:, 0:keys]
                v.tensor_reduce(nmax[:, n % 2:n % 2 + 1], src, AX_X, ALU.max, negate=True).then_inc(s_nmax, 1)

            def p_lo_split(l, n):
                i = n % NT
                for b in range(i // 4 + 1):
                    name = ("PT", l, n, b)
                    m = min(4, i + 1 - 4 * b)
                    sl = (slice(None), slice(4 * b, 4 * b + m), slice(None))
                    lo_split(pt_lo[sl], aux_ready(dve, name)[:, 0:m * P].rearrange("p (k n) -> p k n", k=m), pt_hi[sl],
                             s_pthi, pt_count(l, n, b), name)

            def att_out(l, n):
                h, i = n // NT, n % NT
                name = ("O", l, n)
                link(v.reciprocal(st[:, 40 + n % 2:41 + n % 2], rsum[:, n % 2:n % 2 + 1]))
                bank = aux_ready(dve, name)
                y = Y[:, i, h * P:(h + 1) * P]
                aux_release(v.scalar_tensor_tensor(y, bank[:, 0:P], st[:, 40 + n % 2:41 + n % 2], y, ALU.mult,
                                                   ALU.mult), name)

            def y_lo(l, t):
                for b in range(2):
                    name = ("yT", l, t, b)
                    sl = (slice(None), t % 2, slice(4 * b, 4 * b + 4), slice(None))
                    lo_split(yT_lo[sl], aux_ready(dve, name).rearrange("p (k n) -> p k n", k=4), yT_hi[sl], s_yhi,
                             (l * NT + t) * 2 + b + 1, name)

            def conv_gate(l, t):
                name = ("pw", l, t)
                bank = aux_ready(dve, name)
                dve.wait_ge(s_zev, (l + 1) * UNITS)
                y = Y[:, t, Y_CONV:Y_CONV + CW]
                aux_release(v.tensor_tensor(y, bank[:, 0:CW], y, ALU.mult), name)

            for l in range(DEPTH):
                for t in range(3):
                    h_lo(l, t)
                for t in range(NT):
                    q_norm(l, t)
                    if t + 3 < NT:
                        h_lo(l, t + 3)
                small_weights(l)
                bank = aux_ready(dve, ("taps", l))
                aux_release(v.tensor_copy(taps[:, :, :], bank[:, 0:64].rearrange("p (c k) -> p c k", c=2)[:, :, 0:CONV_K]),
                            ("taps", l))
                bank = aux_ready(dve, ("ws", l))
                aux_release(v.tensor_copy(wsT[:, :, :], bank.rearrange("p (g n) -> p g n", g=HEADS)),
                            ("ws", l))
                for h in range(HEADS):
                    bank = aux_ready(dve, ("uT", l, h))
                    if h > 0:
                        aux_ready(dve, ("Wq", l, h - 1))
                    gt = gtmp[:, :, :].rearrange("p a b -> p (a b)")
                    aux_release(v.tensor_copy(gt[:, 0:3 * P], bank[:, 0:3 * P]), ("uT", l, h))
                    bank = aux_ready(dve, ("Wq", l, h))
                    aux_release(v.tensor_copy(Wq[:, :, h, :], bank[:, 0:2 * P].rearrange("p (k n) -> p k n", k=2)
                                              ), ("Wq", l, h))
                    dve.wait_ge(s_zev, l * UNITS + unit(CONV_B, h) + 1)
                    ct, half = h // 2, h % 2
                    ch = convh[:, ct, HALO + half * BANK:HALO + (half + 1) * BANK]
                    v.scalar_tensor_tensor(ch, scr[:, :], 1.0, ch, ALU.add, ALU.mult).then_inc(s_glu, 1)
                dve.wait_ge(s_glu, (l + 1) * 4)
                m = 0
                for t in range(NT):
                    conv_pair(l, m)
                    m += 1
                    kv_norm(l, t)
                    if t >= 3:
                        kv_lo_split(l, t - 3)
                    if l + 1 < DEPTH and t == 0:
                        ada_job(l + 1, "scale", 0)
                    if l + 1 < DEPTH and t == 1:
                        ada_job(l + 1, "scale", 1)
                for t in range(NT):
                    conv_pair(l, m)
                    m += 1
                    sgu_norm(l, t)
                    if t < 3:
                        kv_lo_split(l, 5 + t)
                    if t >= 4:
                        sgu_mix(l, t - 4)
                for t in range(NT):
                    for _ in range(2):
                        conv_pair(l, m)
                        m += 1
                    if t < 4:
                        sgu_mix(l, 4 + t)
                for c in (G_ATT0, G_ATT1):
                    for t in range(NT):
                        if c == G_ATT0 and t == 1:
                            conv_token(l, 0)
                        for _ in range(2):
                            conv_pair(l, m)
                            m += 1
                conv_token(l, 1)
                conv_norm(l)
                q_rotate(l, 0, 0)
                q_rotate(l, 0, 1)
                if l + 1 < DEPTH:
                    for half in range(2):
                        ada_job(l + 1, "shift", half)
                q_lo_split(l, 0)
                v_lo_split(l, 0)
                row_max(l, 0)
                for n in range(STEPS):
                    i = n % NT
                    last_of_head = i == NT - 1
                    if not last_of_head:
                        row_max(l, n + 1)
                    elif n + 1 < STEPS:
                        q_lo_split(l, n // NT + 1)
                    if i > 0:
                        att_out(l, n - 1)
                    if n < NT:
                        conv_gate(l, n)
                    p_lo_split(l, n)
                    if n in (11, 12):
                        q_rotate(l, 1, n - 11)
                    if 14 <= n < 22:
                        ada_piece((l, "gate", 0), n - 14)
                    if n == 22:
                        ada_finish((l, "gate", 0))
                    if 22 <= n < 30:
                        ada_piece((l, "gate", 1), n - 22)
                    if n == 30:
                        ada_finish((l, "gate", 1))
                    if last_of_head:
                        att_out(l, n)
                        if n + 1 < STEPS:
                            v_lo_split(l, n // NT + 1)
                            row_max(l, n + 1)
                y_lo(l, 0)
                for t in range(NT):
                    if t + 1 < NT:
                        y_lo(l, t + 1)
                    g = l * NT + t
                    dve.wait_ge(s_osq, g + 1)
                    r_sqrt(ssq[:, 2 + t % 2:3 + t % 2], 1, 1.0 / D, RS, TMP)
                    src = ps[:, 2 * (t % 2):2 * (t % 2) + 2, :].rearrange("p a b -> p (a b)")
                    v.scalar_tensor_tensor(Y[:, t, :], src, RS, acc[:, :], ALU.mult, ALU.mult).then_inc(s_ofree, 1)
                    dve.wait_ge(s_ofree, g + 1)
                    before = 4 if l == 0 else 4 + 4 * l
                    dve.wait_ge(s_xin[t % 2], (before + t // 2 + 1) * 16)
                    v.tensor_tensor(xb[:, t % 2, :], xb[:, t % 2, :], Y[:, t, :], ALU.add).then_inc(s_x1, 1)
                    if l + 1 < DEPTH:
                        h_norm(l + 1, t)

        @block.gpsimd
        def _(pool):
            g_ = nc.gpsimd
            chain = [0]
            g_.memset(ident[:, :], 0.0).then_inc(s_cst, 1)
            g_.memset(ones[:, :], 1.0).then_inc(s_cst, 1)
            g_.memset(mask[:, :], 0.0).then_inc(s_cst, 1)
            g_.memset(convh[:, :, 0:HALO], 0.0)
            pool.wait_ge(s_cst, 3)
            g_.affine_select(out=ident[:, :], in_=ident[:, :], compare_op=ALU.not_equal, fill=1.0, base=0,
                             pattern=[[-1, P]], channel_multiplier=1).then_inc(s_cst, 1)
            g_.affine_select(out=mask[:, :], in_=mask[:, :], compare_op=ALU.is_ge, fill=MASKED, base=0,
                             pattern=[[-1, P]], channel_multiplier=1).then_inc(s_cst, 1)
            pool.wait_ge(s_cst, 5)
            g_.tensor_copy(ident_r[:, :], ident[:, :])
            g_.tensor_copy(mask_r[:, :], mask[:, :]).then_inc(s_cst, 1)

            def lo_piece(l, p):
                n = l * W_PIECES + p
                pool.wait_ge(s_hi, n + 1)
                if p < 2 * NCH:
                    cc = l * NCH + p // 2
                    width = CHUNKS[p // 2][1]
                    sl = (slice(None), cc % 2, slice(4 * (p % 2), 4 * (p % 2) + 4), slice(0, width))
                    hi, lo = w_hi[sl], w_lo[sl]
                    src = wraw[:, n % 2, :].rearrange("p (k n) -> p k n", k=4)[:, :, 0:width]
                else:
                    k = p - 2 * NCH
                    hi, lo, src = act_hi[:, k, :], act_lo[:, k, :], wraw[:, n % 2, :]
                g_.tensor_tensor(lo, src, hi.bitcast(F32), ALU.subtract).then_inc(s_lo, 1)

            def add_shift(g, t):
                pool.wait_ge(s_hn, g * NT + t + 1)
                g_.tensor_tensor(Y[:, t, :], Y[:, t, :], S_bc[:, :], ALU.add).then_inc(s_h, 1)

            lo_piece(0, 0)
            lo_piece(0, 1)
            for t in range(NT):
                add_shift(0, t)
            lo_piece(0, 2)
            lo_piece(0, 3)
            for l in range(DEPTH):
                for p in range(4, 6):
                    lo_piece(l, p)
                emptied(pool, ("ws", l))
                g_.affine_select(out=wsT[:, :, :], in_=wsT[:, :, :], compare_op=ALU.is_ge, fill=0.0, base=0,
                                 pattern=[[0, HEADS], [1, P]], channel_multiplier=-1).then_inc(s_wsT, 1)
                for p in range(6, 10):
                    lo_piece(l, p)
                for t in range(NT):
                    pool.wait_ge(s_vn, l * NT + t + 1)
                    gv = gtmp[:, t % 2, :]
                    chain[0] += 1
                    g_.tensor_tensor(gv, gv, sgu_g[:, :], ALU.mult).then_inc(s_cst, 1)
                    pool.wait_ge(s_cst, 6 + chain[0])
                    g_.tensor_tensor(gv, gv, sgu_b[:, :], ALU.add).then_inc(s_vg, 1)
                    if t in (2, 5):
                        lo_piece(l, 10 + (t - 2) // 3)
                for t in range(NT):
                    emptied(pool, ("sgu", l, t))
                    pool.wait_ge(s_zev, l * UNITS + unit(SGU_U, t) + 1)
                    y = Y[:, t, Y_SGU:Y_SGU + CW]
                    g_.tensor_tensor(y, y, gtmp[:, t % 2, :], ALU.mult).then_inc(s_mul, 1)
                    if t in (2, 5):
                        lo_piece(l, 12 + (t - 2) // 3)
                for p in range(14, 18):
                    lo_piece(l, p)
                for t in range(NT):
                    pool.wait_ge(s_zev, l * UNITS + unit(G_SGU, t) + 1)
                    y = Y[:, t, Y_SGU:Y_SGU + CW]
                    g_.tensor_tensor(y, y, gtmp[:, t % 2, :], ALU.mult).then_inc(s_mul, 1)
                    if t in (2, 5):
                        lo_piece(l, 18 + (t - 2) // 3)
                for p in range(2 * NCH, W_PIECES):
                    lo_piece(l, p)
                if l + 1 < DEPTH:
                    for t in range(NT):
                        add_shift(l + 1, t)
                        if 3 <= t < 7:
                            lo_piece(l + 1, t - 3)


_INS = ["x", "c", "positions", "w_ada", "b_ada", "g_pre", "g_post", "w_in", "q_norm_g", "w_uq", "kv_norm_g", "w_ukv",
        "conv_w", "conv_b", "conv_ln_g", "conv_ln_b", "w_pw2", "sgu_ln_g", "sgu_ln_b", "w_s", "b_s", "w_out"]


def kernel(**inputs):
    import numpy as np
    import concourse.bacc as bacc
    from concourse import mybir as mb
    from concourse.bass_utils import run_bass_kernel_spmd

    nc = bacc.Bacc("TRN2", target_bir_lowering=False, num_devices=1, dynamic_dma_scratch_size=1024)
    arrays = {n: np.ascontiguousarray(inputs[n]) for n in _INS}
    arrays["x"] = arrays["x"].reshape(SEQ, D)
    arrays["inv_freq"] = (10000.0 ** (-np.arange(0, ROPE, 2) / ROPE)).astype(np.float32)
    aps, in_map = {}, {}
    for name, arr in arrays.items():
        in_map[f"in_{name}"] = arr
        aps[name] = nc.dram_tensor(f"in_{name}", arr.shape, mb.dt.from_np(arr.dtype), kind="ExternalInput").ap()
    x_mid = nc.dram_tensor("x_mid", (SEQ, D), mb.dt.float32).ap()
    out = nc.dram_tensor("out", (SEQ, D), mb.dt.float32, kind="ExternalOutput").ap()
    trunk(nc, aps, out, x_mid)
    r = run_bass_kernel_spmd(nc, [in_map], core_ids=[0])
    return r.results[0]["out"].reshape(1, SEQ, D)
```

```python
from contextlib import ExitStack

import concourse.bass as bass
from concourse import mybir

ALU = mybir.AluOpType
ACT = mybir.ActivationFunctionType
F32 = mybir.dt.float32
F32R = mybir.dt.float32r
I32 = mybir.dt.int32
AX_X = mybir.AxisListType.X

P = 128
D = 1024
SEQ = 1024
DEPTH = 2
NT = SEQ // P
KD = D // P
HEADS = 4
NOPE = 128
ROPE = 64
Q_RANK = 256
KV_RANK = 128
CONV_K = 31
HALO = CONV_K - 1
EPS = 1e-6
SCALE = (NOPE + ROPE) ** -0.5
MASKED = -1e30
BANK = 512
CW = 256

Q, CONV_A, CONV_B, KV, SGU_V, SGU_U, G_ATT0, G_ATT1, G_SGU, G_CONV = range(10)
CHUNKS = [(0, 256), (960, 256), (1216, 256), (256, 192), (1984, 256), (1728, 256),
          (448, 256), (704, 256), (2240, 256), (1472, 256)]
NCH = len(CHUNKS)
UNITS = 6 * 0 + 8 * 8 + 2 * 4


def unit(c, i):
    if c == Q:
        return i
    if c in (CONV_A, CONV_B):
        return 8 + 4 * (c - CONV_A) + i
    return 16 + 8 * (c - KV) + i


Y_ATT, Y_CONV, Y_SGU = 0, 512, 768
Y_Q, Y_U, Y_KV = 0, 0, 256
W_PIECES = 2 * NCH + KD
STEPS = HEADS * NT
ORDER = [7, 0, 6, 1, 5, 2, 4, 3]


class BankRing:

    def __init__(self):
        self.uses = {}

    def take(self, name):
        n = len(self.uses)
        self.uses[name] = (n % 4, n // 4)
        return self.uses[name]


def trunk(nc, a, out, x_mid):
    with ExitStack() as ctx:
        base = 1152
        at = [base]

        def place(name, shape, dt, offset=None):
            size = 4
            for s in shape[1:]:
                size *= s
            if offset is None:
                offset = at[0]
                at[0] += (size + 31) // 32 * 32
            return nc.alloc_sbuf_tensor_at(name, shape, dt, offset=offset)

        def sem(name):
            return ctx.enter_context(nc.semaphore(name))

        act_hi = place("act_hi", [P, KD, SEQ], F32R)
        act_lo = place("act_lo", [P, KD, SEQ], F32R)
        boot = place("boot", [P, 2, KD, D], F32, base)
        Y = place("Y", [P, NT, D], F32)
        w_at = at[0]
        w_hi = place("w_hi", [P, 2, KD, CW], F32R)
        w_lo = place("w_lo", [P, 2, KD, CW], F32R)
        kb = 1024
        q_hi = place("q_hi", [P, SEQ], F32R, w_at)
        q_lo = place("q_lo", [P, SEQ], F32R, w_at + 4 * kb)
        qr_st = place("qr_st", [P, SEQ], F32R, w_at + 8 * kb)
        qr_lo = place("qr_lo", [ROPE, SEQ], F32R, w_at + 12 * kb)
        v_hi = place("v_hi", [P, NT, P], F32R, w_at + 16 * kb)
        v_lo = place("v_lo", [P, NT, P], F32R, w_at + 20 * kb)
        pt_hi = place("pt_hi", [P, NT, P], F32R, w_at + 24 * kb)
        pt_lo = place("pt_lo", [P, NT, P], F32R, w_at + 28 * kb)
        wraw = place("wraw", [P, 2, 1024], F32)
        araw = place("araw", [P, 2, BANK], F32)
        qk_at = at[0]
        qnT = place("qnT", [P, 2, SEQ], F32)
        kv_hi = place("kv_hi", [P, SEQ], F32R)
        kv_lo = place("kv_lo", [P, SEQ], F32R)
        kr_st = place("kr_st", [P, SEQ], F32R)
        boot_bc = place("boot_bc", [P, 3, D], F32, qk_at)
        yT_hi = place("yT_hi", [P, 2, KD, P], F32R, qk_at)
        yT_lo = place("yT_lo", [P, 2, KD, P], F32R, qk_at + 8 * kb)
        convh = place("convh", [P, 2, HALO + SEQ], F32)
        convo_at = at[0]
        convo = place("convo", [P, 2, BANK], F32)
        uk_raw = place("uk_raw", [P, HEADS, NOPE], F32, convo_at)
        uv_raw = place("uv_raw", [P, HEADS, P], F32, convo_at + 2 * kb)
        qrt = place("qrt", [P, NT, 2, ROPE], F32, convo_at)
        xb_at = at[0]
        xb = place("xb", [P, 2, D], F32)
        uq_raw = place("uq_raw", [P, 2, HEADS, NOPE + ROPE], F32, xb_at)
        ws_raw = place("ws_raw", [P, HEADS, P], F32, xb_at + 6 * kb)
        acc = place("acc", [P, D], F32)
        A_bc = place("A_bc", [P, D], F32)
        S_bc = place("S_bc", [P, D], F32)
        Wq = place("Wq", [P, 2, HEADS, P], F32)
        uqr = place("uqr", [P, 2, HEADS, ROPE], F32)
        uv_hi = place("uv_hi", [P, HEADS, P], F32R)
        uv_lo = place("uv_lo", [P, HEADS, P], F32R)
        pw2 = place("pw2", [P, 2, CW], F32)
        wsT = place("wsT", [P, HEADS, P], F32)
        ident = place("ident", [P, P], F32)
        ident_r = place("ident_r", [P, P], F32R)
        ones = place("ones", [P, P], F32)
        mask = place("mask", [P, P], F32)
        mask_r = place("mask_r", [P, P], F32R)
        cosd = place("cosd", [P, NT, ROPE], F32)
        sind = place("sind", [P, NT, ROPE], F32)
        sgu_g = place("sgu_g", [P, CW], F32)
        sgu_b = place("sgu_b", [P, CW], F32)
        qtmp = place("qtmp", [P, 2, CW], F32)
        gtmp = place("gtmp", [P, 2, CW], F32)
        scr = place("scr", [P, BANK], F32)
        taps = place("taps", [P, 2, CONV_K], F32)
        cols = place("cols", [P, 24], F32)
        silu_c = place("silu_c", [P, 2 * KD], F32)
        st = place("st", [P, 64], F32)
        bst = place("bst", [P, NT, 6], F32)
        mv = place("mv", [P, NT, 2], F32)
        ssq = place("ssq", [P, 32], F32)
        rsum = place("rsum", [P, 4], F32)
        nmax = place("nmax", [P, 2], F32)
        posi = place("posi", [P, NT], I32)
        posf = place("posf", [P, NT], F32)
        freq = place("freq", [P, ROPE // 2], F32)
        assert at[0] <= nc.sbuf_usable_end if isinstance(nc.sbuf_usable_end, int) else True
        print("SBUF", at[0])

        GQ, GKV, CB, CLG, CLB, BS = 0, 2, 3, 5, 7, 9

        ps = ctx.enter_context(nc.psum_tensor("ps", [P, 8, BANK], F32))

        s_wraw = [sem(f"s_wraw{i}") for i in range(2)]
        s_araw = [sem(f"s_araw{i}") for i in range(2)]
        s_xin = [sem(f"s_xin{i}") for i in range(2)]
        s_prep = sem("s_prep")
        s_h0 = sem("s_h0")
        s_boot = [sem(f"s_boot{i}") for i in range(4)]
        s_bootbc = sem("s_bootbc")
        s_x0 = [sem(f"s_x0{i}") for i in range(2)]
        s_once = sem("s_once")
        s_store = [sem(f"s_store{i}") for i in range(2)]
        s_cst = sem("s_cst")
        s_hi = sem("s_hi")
        s_lo = sem("s_lo")
        s_araw_used = sem("s_araw_used")
        s_z = sem("s_z")
        s_zev = sem("s_zev")
        s_auxd = [sem(f"s_auxd{i}") for i in range(4)]
        s_auxf = [sem(f"s_auxf{i}") for i in range(4)]
        s_h = sem("s_h")
        s_hhi = sem("s_hhi")
        s_qn = sem("s_qn")
        s_kvn = sem("s_kvn")
        s_kvhi = sem("s_kvhi")
        s_vn = sem("s_vn")
        s_vg = sem("s_vg")
        s_mul = sem("s_mul")
        s_th = sem("s_th")
        s_conv = sem("s_conv")
        s_glu = sem("s_glu")
        s_cln = sem("s_cln")
        s_scaled = sem("s_scaled")
        s_wsT = sem("s_wsT")
        s_uvhi = sem("s_uvhi")
        s_acc = sem("s_acc")
        s_S = sem("s_S")
        s_nmax = sem("s_nmax")
        s_exp = sem("s_exp")
        s_pthi = sem("s_pthi")
        s_qhi = sem("s_qhi")
        s_qrhi = sem("s_qrhi")
        s_vhi = sem("s_vhi")
        s_yhi = sem("s_yhi")
        s_o = sem("s_o")
        s_osq = sem("s_osq")
        s_ofree = sem("s_ofree")
        s_x1 = sem("s_x1")
        s_xsq = sem("s_xsq")
        s_hn = sem("s_hn")
        s_silc = sem("s_silc")
        s_rope = sem("s_rope")
        s_dve = sem("s_dve")
        s_act = sem("s_act")

        ring = BankRing()
        block = ctx.enter_context(nc.Block())

        ATT = "attention"
        THIRD = {"shift": 0, "scale": 1, "gate": 2}
        STAGE_AT = {c: (0, 8, 16, 24, 32, 40, 48, 56, 64, 72)[c] for c in range(NCH)}
        LAYER_TIME = 180

        def when(l, stage, i):
            if stage == ATT:
                return l * LAYER_TIME + 80 + 2 * i
            return l * LAYER_TIME + STAGE_AT[stage] + (2 if stage in (CONV_A, CONV_B) else 1) * i

        def ada_plan():
            plan = []
            for l in range(DEPTH):
                if l + 1 < DEPTH:
                    job = [(l + 1, third, half) for third in ("scale", "shift") for half in range(2)]
                    plan += [(l, CONV_A, (0, 0, 1, 1, 2, 2, 3, 3)[j], job[0], j) for j in range(KD)]
                    for i in range(4):
                        if i == 1:
                            plan += [(l, CONV_B, i, job[0], j) for j in (KD, KD + 1)]
                        plan += [(l, CONV_B, i, job[1], j) for j in (2 * i, 2 * i + 1)]
                    plan += [(l, KV, 1, job[1], j) for j in (KD, KD + 1)]
                    plan += [(l, G_SGU, j, job[2], j) for j in range(KD)]
                    for i in range(NT):
                        if i == 1:
                            plan.append((l, G_CONV, i, job[2], KD))
                        plan.append((l, G_CONV, i, job[3], i))
                    plan.append((l, ATT, 1, job[3], KD))
                for half in range(2):
                    job = (l, "gate", half)
                    first = 2 + 10 * half
                    plan += [(l, ATT, first + j, job, j) for j in range(KD)]
                    plan += [(l, ATT, first + KD + 1, job, j) for j in (KD, KD + 1)]
            return plan

        ada_order = [(job, j) for _, _, _, job, j in ada_plan()]
        ada_jobs = [job for job, j in ada_order if j == KD - 1]

        def piece_used(eng, n):
            job, j = ada_order[n]
            if j == KD - 1:
                eng.wait_ge(s_acc, 2 + ada_jobs.index(job) + 1)
            elif j == KD:
                emptied(eng, ("ada", *job))
            else:
                eng.wait_ge(s_araw_used, sum(j_ not in (KD - 1, KD) for _, j_ in ada_order[:n + 1]))

        def aux_ready(eng, name):
            b, n = ring.uses[name]
            eng.wait_ge(s_auxd[b], n + 1)
            return ps[:, 4 + b, :]

        def emptied(eng, name):
            b, n = ring.uses[name]
            eng.wait_ge(s_auxf[b], n + 1)

        def h_ready(eng, l, t):
            if l == 0 and t < H0:
                eng.wait_ge(s_h0, t + 1)
            else:
                eng.wait_ge(s_h, l * NT + t + 1 - H0)

        def aux_release(ins, name):
            return ins.then_inc(s_auxf[ring.uses[name][0]], 1)

        H0 = 3
        PREP = 14

        def prep_all(l):
            return (l + 1) * PREP * 16

        def conv_taps(l, ct, k, half):
            return ((l * 2 + ct) * CONV_K + k) * 2 + half + 1

        def pt_count(l, n, b):
            banks = [i // 4 + 1 for i in ORDER]
            return (l * HEADS + n // NT) * sum(banks) + sum(banks[:n % NT]) + b + 1

        @block.tensor
        def _(pe):
            mm = nc.tensor.matmul

            def take(name):
                b, n = ring.take(name)
                if n:
                    pe.wait_ge(s_auxf[b], n)
                return ps[:, 4 + b, :], s_auxd[b]

            def three(out_, a_hi, a_lo, b_hi, b_lo, first=True, last=True):
                mm(out_, a_hi, b_hi, start=first, stop=False)
                mm(out_, a_hi, b_lo, start=False, stop=False)
                return mm(out_, a_lo, b_hi, start=False, stop=last)

            def ada(l, third, half):
                bank, done = take(("ada", l, third, half))
                pe.wait_ge(s_acc, 2 + ada_jobs.index((l, third, half)) + 1)
                mm(bank, ones[:, :], acc[:, half * BANK:(half + 1) * BANK], start=True, stop=True).then_inc(done, 1)

            def h_transpose(l, t):
                for a_ in range(2):
                    bank, done = take(("hT", l, t, a_))
                    h_ready(pe, l, t)
                    for j in range(4):
                        k = 4 * a_ + j
                        ins = nc.tensor.transpose(bank[:, j * P:(j + 1) * P], Y[:, t, k * P:(k + 1) * P], ident[:, :])
                    ins.then_inc(done, 1)

            def z(l, c, i):
                u = l * UNITS + unit(c, i)
                if u >= 4:
                    pe.wait_ge(s_zev, u - 3)
                if i == 0:
                    pe.wait_ge(s_lo, l * W_PIECES + 2 * c + 2)
                slot = (l * NCH + c) % 2
                width = CHUNKS[c][1]
                if c in (CONV_A, CONV_B):
                    ct, half = i // 2, i % 2
                    if c == CONV_A:
                        emptied(pe, ("hT", l, 4 * half + 3, 1))
                    o = ps[:, u % 4, :]
                    for k in range(KD):
                        cs = slice(ct * P, (ct + 1) * P)
                        ts = slice(half * BANK, (half + 1) * BANK)
                        ins = three(o, w_hi[:, slot, k, cs], w_lo[:, slot, k, cs], act_hi[:, k, ts], act_lo[:, k, ts],
                                    k == 0, k == KD - 1)
                else:
                    if c == Q:
                        emptied(pe, ("hT", l, i, 1))
                    o = ps[:, u % 4, 0:width]
                    for k in range(KD):
                        ts = slice(i * P, (i + 1) * P)
                        ins = three(o, act_hi[:, k, ts], act_lo[:, k, ts], w_hi[:, slot, k, 0:width],
                                    w_lo[:, slot, k, 0:width], k == 0, k == KD - 1)
                ins.then_inc(s_z, 1)

            def q_transpose(l, t):
                bank, done = take(("qT", l, t))
                pe.wait_ge(s_qn, l * NT + t + 1)
                for k in range(2):
                    ins = nc.tensor.transpose(bank[:, k * P:(k + 1) * P], Y[:, t, k * P:(k + 1) * P], ident[:, :])
                ins.then_inc(done, 1)

            def kv_transpose(l, t):
                bank, done = take(("kvT", l, t))
                pe.wait_ge(s_kvn, l * NT + t + 1)
                nc.tensor.transpose(bank[:, 0:P], Y[:, t, Y_KV:Y_KV + P], ident[:, :])
                nc.tensor.transpose(bank[0:ROPE, P:2 * P], Y[:, t, Y_KV + P:Y_KV + P + ROPE], ident[:, :]).then_inc(done, 1)

            def taps_transpose(l):
                bank, done = take(("taps", l))
                pe.wait_ge(s_prep, prep_all(l))
                for ct in range(2):
                    ins = nc.tensor.transpose(bank[:, ct * 32:ct * 32 + CONV_K], gtmp[0:CONV_K, 0, ct * P:(ct + 1) * P],
                                              ident[0:CONV_K, 0:CONV_K])
                ins.then_inc(done, 1)

            def ws_transpose(l):
                bank, done = take(("ws", l))
                for g in range(HEADS):
                    ins = nc.tensor.transpose(bank[:, g * P:(g + 1) * P], ws_raw[:, g, :], ident[:, :])
                ins.then_inc(done, 1)

            def u_transpose(l, h):
                bank, done = take(("uT", l, h))
                if h == 0:
                    pe.wait_ge(s_scaled, l + 1)
                for k in range(2):
                    nc.tensor.transpose(bank[:, k * P:(k + 1) * P], uq_raw[:, k, h, 0:NOPE], ident[:, :])
                nc.tensor.transpose(bank[:, 2 * P:3 * P], uk_raw[:, h, :], ident[:, :]).then_inc(done, 1)

            def absorb(l, h):
                bank, done = take(("Wq", l, h))
                emptied(pe, ("uT", l, h))
                g = (gtmp, qtmp)[h % 2][:, :, :].rearrange("p a b -> p (a b)")
                for k in range(2):
                    ins = mm(bank[:, k * P:(k + 1) * P], g[:, k * P:(k + 1) * P], g[:, 2 * P:3 * P], start=True, stop=True)
                ins.then_inc(done, 1)

            def spatial(l, t):
                bank, done = take(("sgu", l, t))
                pe.wait_ge(s_vg, l * NT + t + 1)
                if t == 0:
                    pe.wait_ge(s_wsT, l + 1)
                for g in range(HEADS):
                    ins = mm(bank[:, g * 64:(g + 1) * 64], wsT[:, g, :], Y[:, t, Y_SGU + g * 64:Y_SGU + (g + 1) * 64],
                             start=True, stop=True)
                ins.then_inc(done, 1)

            def conv_to_token(l, ct):
                for half in range(2):
                    bank, done = take(("cT", l, ct, half))
                    pe.wait_ge(s_conv, conv_taps(l, ct, CONV_K - 1, half))
                    for j in range(4):
                        src = convo[:, half, j * P:(j + 1) * P] if ct == 0 else Y[:, 4 * half + j, Y_CONV + P:Y_CONV + CW]
                        ins = nc.tensor.transpose(bank[:, j * P:(j + 1) * P], src, ident[:, :])
                    ins.then_inc(done, 1)

            def conv_to_feature(l, half):
                for ct in range(2):
                    bank, done = take(("cB", l, ct, half))
                    pe.wait_ge(s_cln, l * NT + 4 * half + 4)
                    for j in range(4):
                        cs = Y_CONV + ct * P
                        ins = nc.tensor.transpose(bank[:, j * P:(j + 1) * P], Y[:, 4 * half + j, cs:cs + P], ident[:, :])
                    ins.then_inc(done, 1)

            def pointwise(l, t):
                bank, done = take(("pw", l, t))
                emptied(pe, ("cB", l, 1, t // 4))
                for ct in range(2):
                    ins = mm(bank[:, 0:CW], convh[:, ct, HALO + t * P:HALO + (t + 1) * P], pw2[:, ct, :],
                             start=ct == 0, stop=ct == 1)
                ins.then_inc(done, 1)

            def q_rope(l, pair, b):
                bank, done = take(("RT", l, pair, b))
                emptied(pe, ("qT", l, NT - 1))
                for j in range(4):
                    t = 4 * b + j
                    for k in range(2):
                        ins = mm(bank[:, j * P:(j + 1) * P], qnT[:, k, t * P:(t + 1) * P],
                                 uqr[:, k, 2 * pair:2 * pair + 2, :], start=k == 0, stop=k == 1)
                ins.then_inc(done, 1)

            def queries_nope(l, h):
                for b in range(2):
                    bank, done = take(("QA", l, h, b))
                    emptied(pe, ("Wq", l, HEADS - 1))
                    for k in range(2):
                        ins = mm(bank, Wq[:, k, h, :], qnT[:, k, b * BANK:(b + 1) * BANK], start=k == 0, stop=k == 1)
                    ins.then_inc(done, 1)

            def queries_rope(l, h):
                for b in range(2):
                    bank, done = take(("qr", l, h, b))
                    emptied(pe, ("RT", l, h // 2, b))
                    for j in range(4):
                        ins = nc.tensor.transpose(bank[0:ROPE, j * P:(j + 1) * P], qrt[:, 4 * b + j, h % 2, :], ident[:, :])
                    ins.then_inc(done, 1)

            def values(l, h):
                for b in range(2):
                    bank, done = take(("V", l, h, b))
                    emptied(pe, ("kvT", l, NT - 1))
                    for j in range(4):
                        ts = slice((4 * b + j) * P, (4 * b + j + 1) * P)
                        ins = three(bank[:, j * P:(j + 1) * P], kv_hi[:, ts], kv_lo[:, ts], uv_hi[:, h, :], uv_lo[:, h, :])
                    ins.then_inc(done, 1)

            def scores(l, n):
                h, i = n // NT, ORDER[n % NT]
                g = l * STEPS + n
                if n >= 2:
                    pe.wait_ge(s_exp, g - 1)
                if n < 2:
                    pe.wait_ge(s_zev, (l + 1) * UNITS)
                if n % NT == 0:
                    emptied(pe, ("QA", l, h, 1))
                    emptied(pe, ("qr", l, h, 1))
                qs = slice(i * P, (i + 1) * P)
                for b in range(i // 4 + 1):
                    n_keys = min(BANK, (i + 1) * P - b * BANK)
                    ks = slice(b * BANK, b * BANK + n_keys)
                    o = ps[:, 2 * (n % 2) + b, 0:n_keys]
                    three(o, q_hi[:, qs], q_lo[:, qs], kv_hi[:, ks], kv_lo[:, ks], True, False)
                    mm(o, qr_st[:, qs], kr_st[:, ks], start=False, stop=False)
                    diagonal = b == i // 4
                    ins = mm(o, qr_lo[:, qs], kr_st[0:ROPE, ks], start=False, stop=not diagonal)
                    if diagonal:
                        ins = mm(o[:, n_keys - P:n_keys], ident_r[:, :], mask_r[:, :], start=False, stop=True)
                ins.then_inc(s_S, 1)

            def p_transpose(l, n):
                i = ORDER[n % NT]
                for b in range(i // 4 + 1):
                    bank, done = take(("PT", l, n, b))
                    pe.wait_ge(s_exp, l * STEPS + n + 1)
                    for j in range(min(4, i + 1 - 4 * b)):
                        kbk = 4 * b + j
                        ins = nc.tensor.transpose(bank[:, j * P:(j + 1) * P], xb[:, n % 2, kbk * P:(kbk + 1) * P], ident[:, :])
                    ins.then_inc(done, 1)

            def pv(l, n):
                h, i = n // NT, ORDER[n % NT]
                bank, done = take(("O", l, n))
                if n % NT == 0:
                    emptied(pe, ("V", l, h, 1))
                for k in range(i + 1):
                    if k % 4 == 0:
                        emptied(pe, ("PT", l, n, k // 4))
                    ins = three(bank[:, 0:P], pt_hi[:, k, :], pt_lo[:, k, :], v_hi[:, k, :], v_lo[:, k, :], k == 0, k == i)
                ins.then_inc(done, 1)

            def y_transpose(l, t):
                for a_ in range(2):
                    bank, done = take(("yT", l, t, a_))
                    if a_ == 0:
                        emptied(pe, ("O", l, (HEADS - 1) * NT + ORDER.index(t)))
                    else:
                        emptied(pe, ("pw", l, t))
                        pe.wait_ge(s_mul, (l * 2 + 1) * NT + t + 1)
                    for j in range(4):
                        k = 4 * a_ + j
                        ins = nc.tensor.transpose(bank[:, j * P:(j + 1) * P], Y[:, t, k * P:(k + 1) * P], ident[:, :])
                    ins.then_inc(done, 1)

            def out_proj(l, t):
                g = l * NT + t
                if t >= 2:
                    pe.wait_ge(s_ofree, g - 1)
                else:
                    pe.wait_ge(s_exp, (l + 1) * STEPS)
                emptied(pe, ("yT", l, t, 1))
                if t == 0:
                    pe.wait_ge(s_lo, (l + 1) * W_PIECES)
                for half in range(2):
                    o = ps[:, 2 * (t % 2) + half, :]
                    hs = slice(half * BANK, (half + 1) * BANK)
                    for k in range(KD):
                        ins = three(o, yT_hi[:, t % 2, k, :], yT_lo[:, t % 2, k, :], act_hi[:, k, hs], act_lo[:, k, hs],
                                    k == 0, k == KD - 1)
                ins.then_inc(s_o, 1)

            pe.wait_ge(s_cst, 6)
            for part in range(2):
                for half in range(2):
                    bank, done = take(("boot", part, half))
                    pe.wait_ge(s_acc, part + 1)
                    mm(bank, ones[:, :], acc[:, half * BANK:(half + 1) * BANK], start=True, stop=True).then_inc(done, 1)
            for l in range(DEPTH):
                for t in range(3):
                    h_transpose(l, t)
                for t in range(NT):
                    z(l, Q, t)
                    if t + 3 < NT:
                        h_transpose(l, t + 3)
                z(l, CONV_A, 0)
                for t in range(4):
                    q_transpose(l, t)
                z(l, CONV_A, 1)
                for t in range(4, NT):
                    q_transpose(l, t)
                taps_transpose(l)
                ws_transpose(l)
                z(l, CONV_A, 2)
                u_transpose(l, 0)
                u_transpose(l, 1)
                z(l, CONV_A, 3)
                absorb(l, 0)
                absorb(l, 1)
                u_transpose(l, 2)
                u_transpose(l, 3)
                for i in range(4):
                    z(l, CONV_B, i)
                    if i == 0:
                        absorb(l, 2)
                        absorb(l, 3)
                    if i == 0 and l + 1 < DEPTH:
                        ada(l + 1, "scale", 0)
                for t in range(NT):
                    z(l, KV, t)
                    if t == 0 and l + 1 < DEPTH:
                        ada(l + 1, "scale", 1)
                for t in range(NT):
                    z(l, SGU_V, t)
                    if t >= 4:
                        kv_transpose(l, 2 * (t - 4))
                        kv_transpose(l, 2 * (t - 4) + 1)
                for t in range(NT):
                    z(l, SGU_U, t)
                    if t >= 4:
                        spatial(l, 2 * (t - 4))
                        spatial(l, 2 * (t - 4) + 1)
                for t in range(NT):
                    z(l, G_ATT0, t)
                    if t == 1:
                        conv_to_token(l, 0)
                for t in range(NT):
                    z(l, G_ATT1, t)
                for t in range(NT):
                    z(l, G_SGU, t)
                    if t == 2:
                        conv_to_token(l, 1)
                for t in range(NT):
                    z(l, G_CONV, t)
                    if t == 1:
                        conv_to_feature(l, 0)
                        conv_to_feature(l, 1)
                    if t in (4, 5):
                        q_rope(l, 0, t - 4)
                    if t == 0 and l + 1 < DEPTH:
                        ada(l + 1, "shift", 0)
                queries_nope(l, 0)
                queries_rope(l, 0)
                values(l, 0)
                scores(l, 0)
                scores(l, 1)
                for n in range(STEPS):
                    pos, h = n % NT, n // NT
                    p_transpose(l, n)
                    if n + 2 < STEPS and pos != NT - 2:
                        scores(l, n + 2)
                    if pos == NT - 3 and h + 1 < HEADS:
                        queries_nope(l, h + 1)
                    if pos == NT - 2 and h + 1 < HEADS:
                        queries_rope(l, h + 1)
                    if n < NT:
                        pointwise(l, n)
                    pv(l, n)
                    if pos == NT - 2 and n + 2 < STEPS:
                        scores(l, n + 2)
                    if n in (11, 12):
                        q_rope(l, 1, n - 11)
                    if n == 0 and l + 1 < DEPTH:
                        ada(l + 1, "shift", 1)
                    if n in (10, 20):
                        ada(l, "gate", n // 10 - 1)
                    if pos == NT - 1 and h + 1 < HEADS:
                        values(l, h + 1)
                y_transpose(l, 0)
                for t in range(NT):
                    if t + 1 < NT:
                        y_transpose(l, t + 1)
                    out_proj(l, t)

        @block.sync
        def _(sp):
            for tile_, src in ((silu_c[:, KD:2 * KD], a["c"].rearrange("b (k p) -> p (b k)", p=P)),
                               (posi[:, :], a["positions"].rearrange("b (t p) -> p (b t)", p=P)),
                               (freq[:, :], a["inv_freq"].partition_broadcast(P))):
                sp.dma_start(tile_, src, allow_slow_non_contiguous=True).then_inc(s_once, 16)

            def ada_piece(n):
                (l, third, half), j = ada_order[n]
                if n >= 2:
                    piece_used(sp, n - 2)
                c0 = THIRD[third] * D + half * BANK
                if j < KD:
                    src = a["w_ada"][l, j * P:(j + 1) * P, c0:c0 + BANK]
                elif j == KD:
                    src = a["b_ada"][l, c0:c0 + BANK].partition_broadcast(P)
                else:
                    gain = a["g_pre"] if third == "scale" else a["g_post"]
                    src = gain[l, half * BANK:(half + 1) * BANK].partition_broadcast(P)
                sp.dma_start(araw[:, n % 2, :], src).then_inc(s_araw[n % 2], 16)

            def w_piece(l, p):
                n = l * W_PIECES + p
                if n >= 2:
                    sp.wait_ge(s_lo, n - 1)
                if p < 2 * NCH:
                    c0, width = CHUNKS[p // 2]
                    k0 = 4 * (p % 2)
                    dst = wraw[:, n % 2, :].rearrange("p (k n) -> p k n", k=4)[:, :, 0:width]
                    src = a["w_in"][l, k0 * P:(k0 + 4) * P, c0:c0 + width].rearrange("(k p) n -> p k n", p=P)
                else:
                    k = p - 2 * NCH
                    dst, src = wraw[:, n % 2, :], a["w_out"][l, k * P:(k + 1) * P, :]
                sp.dma_start(dst, src).then_inc(s_wraw[n % 2], 16)

            def x_tile(l, t):
                if t < 2:
                    emptied(sp, ("PT", l, STEPS - 1, ORDER[-1] // 4))
                if l > 0:
                    sp.wait_ge(s_store[t % 2], ((l - 1) * NT // 2 + t // 2 + 1) * 16)
                if t >= 2:
                    sp.wait_ge(s_store[t % 2], (l * NT // 2 + t // 2) * 16)
                    if l + 1 < DEPTH:
                        sp.wait_ge(s_hn, (l + 1) * NT + t - 1)
                src = a["x"] if l == 0 else x_mid
                sp.dma_start(xb[:, t % 2, :], src[t * P:(t + 1) * P, :]).then_inc(s_xin[t % 2], 16)

            def prep(l):
                if l > 0:
                    sp.wait_ge(s_x1, l * NT)
                    for i in range(2):
                        sp.wait_ge(s_store[i], l * NT // 2 * 16)
                    sp.wait_ge(s_hn, (l + 1) * NT)
                    emptied(sp, ("cB", l - 1, 1, 1))
                    emptied(sp, ("pw", l - 1, NT - 1))
                    emptied(sp, ("kvT", l - 1, NT - 1))
                else:
                    sp.wait_ge(s_xsq, NT)
                for dst, src in (
                    (uq_raw[:, :, :, :], a["w_uq"][l].rearrange("(k p) (h n) -> p k h n", p=P, h=HEADS)),
                    (ws_raw[:, :, :], a["w_s"][l].rearrange("g t s -> t g s")),
                    (uk_raw[:, :, :], a["w_ukv"][l].rearrange("p (h n) -> p h n", h=HEADS)[:, :, 0:NOPE]),
                    (uv_raw[:, :, :], a["w_ukv"][l].rearrange("p (h n) -> p h n", h=HEADS)[:, :, NOPE:]),
                    (gtmp[0:CONV_K, 0, :], a["conv_w"][l]),
                    (pw2[:, :, :], a["w_pw2"][l].rearrange("(c p) n -> p c n", p=P)),
                    (sgu_g[:, :], a["sgu_ln_g"][l].partition_broadcast(P)),
                    (sgu_b[:, :], a["sgu_ln_b"][l].partition_broadcast(P)),
                    (cols[:, GQ:GQ + 2], a["q_norm_g"][l].rearrange("(c p) -> p c", p=P)),
                    (cols[:, GKV:GKV + 1], a["kv_norm_g"][l].rearrange("(c p) -> p c", p=P)),
                    (cols[:, CB:CB + 2], a["conv_b"][l].rearrange("(c p) -> p c", p=P)),
                    (cols[:, CLG:CLG + 2], a["conv_ln_g"][l].rearrange("(c p) -> p c", p=P)),
                    (cols[:, CLB:CLB + 2], a["conv_ln_b"][l].rearrange("(c p) -> p c", p=P)),
                    (cols[:, BS:BS + 4], a["b_s"][l].rearrange("g t -> t g")),
                ):
                    sp.dma_start(dst, src, allow_slow_non_contiguous=True).then_inc(s_prep, 16)

            def boot_piece(part, half):
                c0 = (THIRD["scale"], THIRD["shift"])[part] * D
                src = a["w_ada"][0, 4 * half * P:4 * (half + 1) * P, c0:c0 + D].rearrange("(k p) n -> p k n", p=P)
                sp.dma_start(boot[:, part, 4 * half:4 * half + 4, :], src).then_inc(s_boot[2 * part + half], 16)

            for half in range(2):
                boot_piece(0, half)
            for i, src in enumerate((a["b_ada"][0, D:2 * D], a["b_ada"][0, 0:D], a["g_pre"][0])):
                sp.dma_start(boot_bc[:, i, :], src.partition_broadcast(P)).then_inc(s_bootbc, 16)
            for half in range(2):
                src = a["x"][4 * half * P:4 * (half + 1) * P, :].rearrange("(t p) n -> p t n", p=P)
                sp.dma_start(Y[:, 4 * half:4 * half + 4, :], src).then_inc(s_x0[half], 16)
            w_piece(0, 0)
            w_piece(0, 1)
            for half in range(2):
                boot_piece(1, half)
            w_piece(0, 2)
            w_piece(0, 3)
            prep(0)
            w_times = [when(l, p // 2 - 1, (2 + p % 2) if p < 8 else (2, 5)[p % 2]) if 4 <= p < 2 * NCH else
                       when(l, ATT, 8 * ((p - 2 * NCH) // 2) + (2, 4)[p % 2]) if p >= 4 else
                       when(l - 1, ATT, STEPS) + 4 * (p + 3)
                       for l in range(DEPTH) for p in range(W_PIECES)]
            loads = [(w_times[n - 2], w_piece, (n // W_PIECES, n % W_PIECES)) for n in range(4, len(w_times))]
            ada_times = [when(l, stage, i if stage != CONV_A else 0) for l, stage, i, _, _ in ada_plan()]
            loads += [(ada_times[n - 2] if n >= 2 else 0, ada_piece, (n,)) for n in range(len(ada_order))]
            for l in range(DEPTH):
                out_at = when(l, ATT, STEPS)
                loads += [(out_at + (4 * (t - 2) + 3 if t >= 2 else 0), x_tile, (l, t)) for t in range(NT)]
                if l > 0:
                    loads.append((when(l, Q, 0) - 1, prep, (l,)))
            for _, load, which in sorted(loads, key=lambda e: e[0]):
                load(*which)

        @block.scalar
        def _(act):
            fn = nc.scalar.activation

            def hi_piece(l, p):
                n = l * W_PIECES + p
                act.wait_ge(s_wraw[n % 2], (n // 2 + 1) * 16)
                if p < 2 * NCH:
                    c = p // 2
                    cc = l * NCH + c
                    width = CHUNKS[c][1]
                    if c < 2:
                        if l > 0:
                            aux_ready(act, ("O", l - 1, STEPS - 1))
                    else:
                        act.wait_ge(s_z, l * UNITS + unit(c - 1, 0))
                    dst = w_hi[:, cc % 2, 4 * (p % 2):4 * (p % 2) + 4, 0:width]
                    src = wraw[:, n % 2, :].rearrange("p (k n) -> p k n", k=4)[:, :, 0:width]
                else:
                    act.wait_ge(s_z, (l + 1) * UNITS)
                    dst, src = act_hi[:, p - 2 * NCH, :], wraw[:, n % 2, :]
                fn(dst, src, ACT.Copy).then_inc(s_hi, 1)

            def kv_hi_copy(l, t):
                bank = aux_ready(act, ("kvT", l, t))
                nc.scalar.activation(kv_hi[:, t * P:(t + 1) * P], bank[:, 0:P], ACT.Copy)
                nc.scalar.activation(kr_st[0:ROPE, t * P:(t + 1) * P], bank[0:ROPE, P:2 * P], ACT.Copy).then_inc(s_kvhi, 1)

            def z_ready(l, c, i):
                u = l * UNITS + unit(c, i)
                act.wait_ge(s_z, u + 1)
                return ps[:, u % 4, :]

            def square_sum(src, junk, dst):
                return fn(junk, src, ACT.Square, accum_out=dst)

            def h_hi(l, t):
                for b in range(2):
                    bank = aux_ready(act, ("hT", l, t, b))
                    if l > 0:
                        act.wait_ge(s_o, l * NT)
                    fn(act_hi[:, 4 * b:4 * b + 4, t * P:(t + 1) * P], bank.rearrange("p (k n) -> p k n", k=4),
                       ACT.Copy).then_inc(s_hhi, 1)

            def evac_q(l, t):
                z_ = z_ready(l, Q, t)
                fn(Y[:, t, Y_Q:Y_Q + CW], z_[:, 0:CW], ACT.Copy)
                if l * UNITS + t:
                    act.wait_ge(s_zev, l * UNITS + unit(Q, t))
                square_sum(z_[:, 0:CW], scr[:, 0:CW], ssq[:, 16 + t:17 + t]).then_inc(s_zev, 1)

            def q_copy(l, t):
                bank = aux_ready(act, ("qT", l, t))
                if l > 0 and t == 0:
                    emptied(act, ("yT", l - 1, NT - 1, 1))
                    act.wait_ge(s_o, l * NT)
                aux_release(fn(qnT[:, :, t * P:(t + 1) * P], bank[:, 0:CW].rearrange("p (k n) -> p k n", k=2),
                               ACT.Copy), ("qT", l, t))

            act.wait_ge(s_once, 48)
            fn(silu_c[:, 0:KD], silu_c[:, KD:2 * KD], ACT.Silu).then_inc(s_silc, 1)
            act.wait_ge(s_rope, 1)
            fn(sind[:, :, ROPE // 2:ROPE], sind[:, :, ROPE // 2:ROPE], ACT.Sin).then_inc(s_act, 1)
            fn(cosd[:, :, 0:ROPE // 2], cosd[:, :, 0:ROPE // 2], ACT.Sin).then_inc(s_act, 1)
            for t in range(NT):
                act.wait_ge(s_x0[t // 4], 16)
                if t >= 2:
                    act.wait_ge(s_xsq, t - 1)
                square_sum(Y[:, t, :], xb[:, t % 2, :], ssq[:, 8 + t:9 + t]).then_inc(s_xsq, 1)
            for p in range(4):
                hi_piece(0, p)

            for l in range(DEPTH):
                for t in range(3):
                    h_hi(l, t)
                for t in range(NT):
                    evac_q(l, t)
                    if t + 3 < NT:
                        h_hi(l, t + 3)
                for i in range(4):
                    if i in (1, 2):
                        for t in range(4):
                            q_copy(l, 4 * (i - 1) + t)
                    z_ = z_ready(l, CONV_A, i)
                    if l > 0:
                        b, n = ring.uses["pw", l - 1, NT - 1]
                        act.wait_ge(s_auxd[b], n + 1)
                    ct, half = i // 2, i % 2
                    fn(convh[:, ct, HALO + half * BANK:HALO + (half + 1) * BANK], z_, ACT.Copy, scale=0.5).then_inc(s_zev, 1)
                    if i >= 2:
                        hi_piece(l, 4 + i - 2)
                for i in range(4):
                    z_ = z_ready(l, CONV_B, i)
                    act.wait_ge(s_glu, l * 4 + i) if l * 4 + i else None
                    if i == 0 and l > 0:
                        emptied(act, ("RT", l - 1, 1, 1))
                    fn(scr[:, :], z_, ACT.Tanh, scale=0.5).then_inc(s_zev, 1)
                    if i >= 2:
                        hi_piece(l, 6 + i - 2)
                for t in range(NT):
                    z_ = z_ready(l, KV, t)
                    fn(Y[:, t, Y_KV:Y_KV + KV_RANK + ROPE], z_[:, 0:KV_RANK + ROPE], ACT.Copy)
                    act.wait_ge(s_zev, l * UNITS + unit(KV, t))
                    if t == 0:
                        act.wait_ge(s_glu, l * 4 + 4)
                    square_sum(z_[:, 0:KV_RANK], scr[:, 0:KV_RANK], ssq[:, 24 + t:25 + t]).then_inc(s_zev, 1)
                    if t in (2, 5):
                        hi_piece(l, 8 + (t - 2) // 3)
                for t in range(NT):
                    z_ = z_ready(l, SGU_V, t)
                    fn(Y[:, t, Y_SGU:Y_SGU + CW], z_[:, 0:CW], ACT.Gelu).then_inc(s_zev, 1)
                    if t >= 5:
                        kv_hi_copy(l, 2 * (t - 5))
                        kv_hi_copy(l, 2 * (t - 5) + 1)
                    if t in (2, 5):
                        hi_piece(l, 10 + (t - 2) // 3)
                for t in range(NT):
                    z_ = z_ready(l, SGU_U, t)
                    if t == 0:
                        kv_hi_copy(l, 6)
                        kv_hi_copy(l, 7)
                        emptied(act, ("qT", l, NT - 1))
                    fn(Y[:, t, Y_U:Y_U + CW], z_[:, 0:CW], ACT.Gelu).then_inc(s_zev, 1)
                    if t in (2, 5):
                        hi_piece(l, 12 + (t - 2) // 3)
                for c in (G_ATT0, G_ATT1):
                    for t in range(NT):
                        z_ = z_ready(l, c, t)
                        y0 = Y_ATT + (c - G_ATT0) * CW
                        if c == G_ATT0:
                            act.wait_ge(s_mul, l * 2 * NT + t + 1)
                        fn(Y[:, t, y0:y0 + CW], z_[:, 0:CW], ACT.Silu).then_inc(s_zev, 1)
                        if t in (2, 5):
                            hi_piece(l, 2 * (c + 1) + (t - 2) // 3)
                for t in range(NT):
                    z_ = z_ready(l, G_SGU, t)
                    if t >= 2:
                        act.wait_ge(s_mul, l * 2 * NT + NT + t - 1)
                    fn(gtmp[:, t % 2, :], z_[:, 0:CW], ACT.Silu).then_inc(s_zev, 1)
                    if t in (2, 5):
                        hi_piece(l, 18 + (t - 2) // 3)

                def conv_silu(half):
                    for ct in range(2):
                        bank = aux_ready(act, ("cB", l, ct, half))
                        act.wait_ge(s_conv, (l + 1) * 2 * 2 * CONV_K)
                        aux_release(fn(convh[:, ct, HALO + half * BANK:HALO + (half + 1) * BANK], bank, ACT.Silu,
                                       scale=cols[:, CLG + ct:CLG + ct + 1], bias=cols[:, CLB + ct:CLB + ct + 1]
                                       ), ("cB", l, ct, half))

                for t in range(NT):
                    z_ = z_ready(l, G_CONV, t)
                    if t in (0, 4):
                        conv_silu(t // 4)
                    fn(Y[:, t, Y_CONV:Y_CONV + CW], z_[:, 0:CW], ACT.Silu).then_inc(s_zev, 1)

                def q_hi_copy(h):
                    for b in range(2):
                        bank = aux_ready(act, ("QA", l, h, b))
                        if h == 0 and b == 0:
                            act.wait_ge(s_z, (l + 1) * UNITS)
                        if h > 0 and b == 0:
                            act.wait_ge(s_S, l * STEPS + h * NT)
                        fn(q_hi[:, b * BANK:(b + 1) * BANK], bank, ACT.Copy).then_inc(s_qhi, 1)

                def q_rope_hi(h):
                    for b in range(2):
                        bank = aux_ready(act, ("qr", l, h, b))
                        for r in range(2):
                            ins = fn(qr_st[r * ROPE:(r + 1) * ROPE, b * BANK:(b + 1) * BANK], bank[0:ROPE, :], ACT.Copy)
                        ins.then_inc(s_qrhi, 1)

                def v_split(h):
                    for b in range(2):
                        bank = aux_ready(act, ("V", l, h, b))
                        fn(v_hi[:, 4 * b:4 * b + 4, :], bank.rearrange("p (k n) -> p k n", k=4), ACT.Copy).then_inc(s_vhi, 1)

                def exp(n):
                    keys = (ORDER[n % NT] + 1) * P
                    act.wait_ge(s_nmax, l * STEPS + n + 1)
                    if n >= 2:
                        emptied(act, ("PT", l, n - 2, ORDER[(n - 2) % NT] // 4))
                    if n >= 4:
                        emptied(act, ("O", l, n - 4))
                    src = ps[:, 2 * (n % 2):2 * (n % 2) + 2, :].rearrange("p a b -> p (a b)")[:, 0:keys]
                    fn(xb[:, n % 2, 0:keys], src, ACT.Exp, bias=nmax[:, n % 2:n % 2 + 1],
                       accum_out=rsum[:, n % 4:n % 4 + 1]).then_inc(s_exp, 1)

                def p_hi(n):
                    i = ORDER[n % NT]
                    for b in range(i // 4 + 1):
                        bank = aux_ready(act, ("PT", l, n, b))
                        if n > 0 and b == 0:
                            aux_ready(act, ("O", l, n - 1))
                        m = min(4, i + 1 - 4 * b)
                        fn(pt_hi[:, 4 * b:4 * b + m, :], bank[:, 0:m * P].rearrange("p (k n) -> p k n", k=m),
                           ACT.Copy).then_inc(s_pthi, 1)

                q_hi_copy(0)
                q_rope_hi(0)
                v_split(0)
                exp(0)
                for n in range(STEPS):
                    pos, h = n % NT, n // NT
                    if pos == 0 and h > 0:
                        v_split(h)
                    if pos == NT - 2 and h + 1 < HEADS:
                        q_hi_copy(h + 1)
                    p_hi(n)
                    if pos == NT - 2 and h + 1 < HEADS:
                        q_rope_hi(h + 1)
                    if n + 1 < STEPS:
                        exp(n + 1)
                    if pos in (2, 4):
                        hi_piece(l, 2 * NCH + 2 * h + (pos - 2) // 2)

                def y_hi(t):
                    for b in range(2):
                        bank = aux_ready(act, ("yT", l, t, b))
                        if t >= 2:
                            act.wait_ge(s_o, l * NT + t - 1)
                        else:
                            act.wait_ge(s_S, (l + 1) * STEPS)
                        fn(yT_hi[:, t % 2, 4 * b:4 * b + 4, :], bank.rearrange("p (k n) -> p k n", k=4),
                           ACT.Copy).then_inc(s_yhi, 1)

                y_hi(0)
                for t in range(NT):
                    g = l * NT + t
                    if t + 1 < NT:
                        y_hi(t + 1)
                    act.wait_ge(s_o, g + 1)
                    src = ps[:, 2 * (t % 2):2 * (t % 2) + 2, :].rearrange("p a b -> p (a b)")
                    square_sum(src, Y[:, t, :], ssq[:, 2 + t % 2:3 + t % 2]).then_inc(s_osq, 1)
                    act.wait_ge(s_x1, g + 1)
                    dst = out if l + 1 == DEPTH else x_mid
                    act.dma_start(dst[t * P:(t + 1) * P, :], xb[:, t % 2, :]).then_inc(s_store[t % 2], 16)
                    if l + 1 < DEPTH:
                        square_sum(xb[:, t % 2, :], Y[:, t, :], ssq[:, 4 + t % 2:5 + t % 2]).then_inc(s_xsq, 1)
                        if 3 <= t < 7:
                            hi_piece(l + 1, t - 3)
            for i in range(2):
                act.wait_ge(s_store[i], DEPTH * NT // 2 * 16)

        @block.vector
        def _(dve):
            v = nc.vector
            chain = [0]

            def link(ins):
                chain[0] += 1
                ins.then_inc(s_dve, 1)
                dve.wait_ge(s_dve, chain[0])

            def r_sqrt(src, n, scale, y, tmp):
                link(v.tensor_scalar(tmp[:, 0:n], src, scale, EPS, ALU.mult, ALU.add))
                link(v.tensor_scalar(y.bitcast(I32), tmp[:, 0:n].bitcast(I32), -0.5, float(0x5F3759DF), ALU.mult, ALU.add))
                link(v.tensor_scalar(tmp[:, 0:n], tmp[:, 0:n], -0.5, None, ALU.mult))
                for _ in range(3):
                    if n == 1:
                        link(v.scalar_tensor_tensor(tmp[:, 8:9], y, y, tmp[:, 0:1], ALU.mult, ALU.mult))
                    else:
                        link(v.tensor_tensor(tmp[:, 8:8 + n], y, y, ALU.mult))
                        link(v.tensor_tensor(tmp[:, 8:8 + n], tmp[:, 8:8 + n], tmp[:, 0:n], ALU.mult))
                    link(v.scalar_tensor_tensor(y, tmp[:, 8:8 + n], 1.5, y, ALU.add, ALU.mult))

            TMP = st[:, 0:16]
            RS = st[:, 16:17]

            def lo_split(dst, bank, hi, s_from, value, name):
                dve.wait_ge(s_from, value)
                aux_release(v.tensor_tensor(dst, bank, hi.bitcast(F32), ALU.subtract), name)

            def ada_step(l, stage, i):
                for n, (l_, stage_, i_, job, j) in enumerate(ada_plan()):
                    if (l_, stage_, i_) == (l, stage, i):
                        ada_piece(n, job, j)

            def ada_piece(n, job, j):
                l, third, half = job
                hs = slice(half * BANK, (half + 1) * BANK)
                o, w = acc[:, hs], araw[:, n % 2, :]
                dst = {"scale": A_bc, "shift": S_bc, "gate": acc}[third][:, hs]
                dve.wait_ge(s_araw[n % 2], (n // 2 + 1) * 16)
                if j == 0:
                    k = ada_jobs.index(job)
                    aux_ready(dve, ("ada", *ada_jobs[k - 2]) if k >= 2 else ("boot", 1, half))
                    v.tensor_scalar(o, w, silu_c[:, 0:1], None, ALU.mult).then_inc(s_araw_used, 1)
                elif j < KD:
                    piece_used(dve, n - 1 if ada_order[n - 1][0] == job else ada_order.index((job, j - 1)))
                    ins = v.scalar_tensor_tensor(o, w, silu_c[:, j:j + 1], o, ALU.mult, ALU.add)
                    ins.then_inc(s_acc if j == KD - 1 else s_araw_used, 1)
                elif j == KD:
                    bank = aux_ready(dve, ("ada", *job))
                    aux_release(v.tensor_tensor(dst, bank, w, ALU.add), ("ada", *job))
                else:
                    emptied(dve, ("ada", *job))
                    v.scalar_tensor_tensor(dst, dst, 1.0 if third == "scale" else 0.0, w, ALU.add,
                                           ALU.mult).then_inc(s_araw_used, 1)

            def boot_sum(part):
                for k in range(KD):
                    if k % 4 == 0:
                        dve.wait_ge(s_boot[2 * part + k // 4], 16)
                    w, sc = boot[:, part, k, :], silu_c[:, k:k + 1]
                    if k == 0:
                        if part == 1:
                            emptied(dve, ("boot", 0, 1))
                        ins = v.tensor_scalar(acc[:, :], w, sc, None, ALU.mult)
                    else:
                        ins = v.scalar_tensor_tensor(acc[:, :], w, sc, acc[:, :], ALU.mult, ALU.add)
                    if k < KD - 1:
                        link(ins)
                ins.then_inc(s_acc, 1)

            def h_norm(g, t):
                dve.wait_ge(s_xsq, g * NT + t + 1)
                r_sqrt(ssq[:, 4 + t % 2:5 + t % 2], 1, 1.0 / D, RS, TMP)
                v.scalar_tensor_tensor(Y[:, t, :], xb[:, t % 2, :], RS, A_bc[:, :], ALU.mult, ALU.mult).then_inc(s_hn, 1)

            dve.wait_ge(s_once, 48)
            link(v.memset(st[:, :], 0.0))
            dve.wait_ge(s_silc, 1)
            boot_sum(0)
            link(v.tensor_copy(posf[:, :], posi[:, :]))
            half_ = ROPE // 2
            ang = sind[:, :, half_:ROPE]
            turns = sind[:, :, 0:half_]
            for t in range(NT):
                ins = v.tensor_scalar(sind[:, t, half_:ROPE], freq[:, :], posf[:, t:t + 1], None, ALU.mult)
            link(ins)
            TWO_PI = 6.283185307179586
            link(v.tensor_scalar(turns, ang, 1.0 / TWO_PI, None, ALU.mult))
            turns_i = cosd[:, :, half_:ROPE].bitcast(I32)
            link(v.tensor_copy(turns_i, turns))
            link(v.tensor_copy(turns, turns_i))
            rest = TWO_PI
            parts = []
            for bits in (5, 15, 24):
                q = round(rest * 2.0 ** bits) / 2.0 ** bits
                parts.append(q)
                rest -= q
            for part in parts + [rest]:
                link(v.scalar_tensor_tensor(ang, turns, -part, ang, ALU.mult, ALU.add))
            PI = 3.1415925
            link(v.tensor_scalar(ang, ang, PI, -PI, ALU.min, ALU.max))
            cosv = cosd[:, :, 0:half_]
            link(v.tensor_scalar(cosv, ang, -1.0, None, ALU.mult))
            link(v.tensor_tensor(cosv, cosv, ang, ALU.min))
            v.tensor_scalar(cosv, cosv, TWO_PI / 4, None, ALU.add).then_inc(s_rope, 1)
            dve.wait_ge(s_bootbc, 48)
            for half in range(2):
                hs = slice(half * BANK, (half + 1) * BANK)
                bank = aux_ready(dve, ("boot", 0, half))
                aux_release(v.scalar_tensor_tensor(A_bc[:, hs], bank, 1.0, boot_bc[:, 0, hs], ALU.add, ALU.add),
                            ("boot", 0, half))
            emptied(dve, ("boot", 0, 1))
            link(v.tensor_tensor(A_bc[:, :], A_bc[:, :], boot_bc[:, 2, :], ALU.mult))
            dve.wait_ge(s_act, 2)
            v.tensor_scalar(sind[:, :, 0:half_], ang, -1.0, None, ALU.mult)
            link(v.tensor_copy(cosd[:, :, half_:ROPE], cosv))
            dve.wait_ge(s_xsq, NT)
            r_sqrt(ssq[:, 8:16], NT, 1.0 / D, st[:, 48:56], TMP)
            for t in range(NT):
                v.scalar_tensor_tensor(Y[:, t, :], Y[:, t, :], st[:, 48 + t:49 + t], A_bc[:, :], ALU.mult,
                                       ALU.mult).then_inc(s_hn, 1)
            boot_sum(1)
            for half in range(2):
                hs = slice(half * BANK, (half + 1) * BANK)
                bank = aux_ready(dve, ("boot", 1, half))
                aux_release(v.tensor_tensor(S_bc[:, hs], bank, boot_bc[:, 1, hs], ALU.add), ("boot", 1, half))
            emptied(dve, ("boot", 1, 1))
            for t in range(H0):
                dve.wait_ge(s_hn, t + 1)
                v.tensor_tensor(Y[:, t, :], Y[:, t, :], S_bc[:, :], ALU.add).then_inc(s_h0, 1)

            def h_lo(l, t):
                for b in range(2):
                    name = ("hT", l, t, b)
                    bank = aux_ready(dve, name)
                    sl = (slice(None), slice(4 * b, 4 * b + 4), slice(t * P, (t + 1) * P))
                    lo_split(act_lo[sl], bank.rearrange("p (k n) -> p k n", k=4), act_hi[sl], s_hhi,
                             (l * NT + t) * 2 + b + 1, name)

            def q_norm(l):
                dve.wait_ge(s_zev, l * UNITS + unit(Q, NT - 1) + 1)
                r_sqrt(ssq[:, 16:24], NT, 1.0 / Q_RANK, st[:, 32:40], TMP)
                for t in range(NT):
                    y = Y[:, t, Y_Q:Y_Q + CW]
                    v.tensor_scalar(y, y, st[:, 32 + t:33 + t], None, ALU.mult).then_inc(s_qn, 1)

            def rope(dst, src, cos, sin, t1, t2):
                h2 = ROPE // 2
                v.tensor_tensor(t1, src, cos, ALU.mult)
                v.tensor_tensor(t2[:, :, 0:h2], src[:, :, h2:ROPE], sin[:, :, 0:h2], ALU.mult)
                link(v.tensor_tensor(t2[:, :, h2:ROPE], src[:, :, 0:h2], sin[:, :, h2:ROPE], ALU.mult))
                return v.tensor_tensor(dst, t1, t2, ALU.add)

            def kv_norm(l):
                dve.wait_ge(s_zev, l * UNITS + unit(KV, NT - 1) + 1)
                kr = Y[:, :, Y_KV + P:Y_KV + P + ROPE]
                t1 = scr[:, :].rearrange("p (a n) -> p a n", a=NT)
                t2 = qtmp[:, :, :].rearrange("p a b -> p (a b)").rearrange("p (a n) -> p a n", a=NT)
                rope(kr, kr, cosd[:, :, :], sind[:, :, :], t1, t2)
                r_sqrt(ssq[:, 24:32], NT, 1.0 / KV_RANK, st[:, 32:40], TMP)
                for t in range(NT):
                    y = Y[:, t, Y_KV:Y_KV + P]
                    v.tensor_scalar(y, y, st[:, 32 + t:33 + t], None, ALU.mult).then_inc(s_kvn, 1)

            def kv_lo_split(l, t):
                name = ("kvT", l, t)
                bank = aux_ready(dve, name)
                ts = slice(t * P, (t + 1) * P)
                dve.wait_ge(s_kvhi, l * NT + t + 1)
                v.tensor_tensor(kv_lo[:, ts], bank[:, 0:P], kv_hi[:, ts].bitcast(F32), ALU.subtract)
                aux_release(v.tensor_tensor(kr_st[ROPE:P, ts], bank[0:ROPE, P:2 * P], kr_st[0:ROPE, ts].bitcast(F32),
                                            ALU.subtract), name)

            pairs = [(ct, k) for ct in range(2) for k in range(CONV_K)]

            def conv_pair(l, m):
                if m >= len(pairs):
                    return
                ct, k = pairs[m]
                for half in range(2):
                    n = conv_taps(l, ct, k, half)
                    src = convh[:, ct, k + half * BANK:k + (half + 1) * BANK]
                    o = convo[:, half, :]
                    if ct == 1:
                        o = Y[:, 4 * half:4 * half + 4, Y_CONV + P:Y_CONV + CW]
                        src = src.rearrange("p (t n) -> p t n", t=4)
                    if k == 0:
                        if m == 0 and half == 0:
                            emptied(dve, ("taps", l))
                            emptied(dve, ("uT", l, HEADS - 1))
                        v.tensor_scalar(o, src, taps[:, ct, 0:1], cols[:, CB + ct:CB + ct + 1], ALU.mult,
                                        ALU.add).then_inc(s_conv, 1)
                    else:
                        dve.wait_ge(s_conv, n - 2)
                        v.scalar_tensor_tensor(o, src, taps[:, ct, k:k + 1], o, ALU.mult, ALU.add).then_inc(s_conv, 1)

            def absorb_operands(l, h):
                bank = aux_ready(dve, ("uT", l, h))
                if h >= 2:
                    aux_ready(dve, ("Wq", l, h - 2))
                place_ = (gtmp, qtmp)[h % 2][:, :, :].rearrange("p a b -> p (a b)")
                aux_release(v.tensor_copy(place_[:, 0:3 * P], bank[:, 0:3 * P]), ("uT", l, h))

            def absorbed(l, h):
                bank = aux_ready(dve, ("Wq", l, h))
                aux_release(v.tensor_copy(Wq[:, :, h, :], bank[:, 0:2 * P].rearrange("p (k n) -> p k n", k=2)),
                            ("Wq", l, h))

            def small_weights(l):
                dve.wait_ge(s_prep, prep_all(l))
                link(v.tensor_scalar(cols[:, 16:18], cols[:, GQ:GQ + 2], SCALE, None, ALU.mult))
                for k in range(2):
                    ins = v.tensor_scalar(uq_raw[:, k, :, :], uq_raw[:, k, :, :], cols[:, 16 + k:17 + k], None, ALU.mult)
                v.tensor_scalar(uk_raw[:, :, :], uk_raw[:, :, :], cols[:, GKV:GKV + 1], None, ALU.mult)
                link(v.tensor_scalar(uv_raw[:, :, :], uv_raw[:, :, :], cols[:, GKV:GKV + 1], None, ALU.mult))
                link(v.tensor_copy(uv_hi[:, :, :], uv_raw[:, :, :]))
                v.tensor_tensor(uv_lo[:, :, :], uv_raw[:, :, :], uv_hi[:, :, :].bitcast(F32), ALU.subtract)
                v.tensor_copy(uqr[:, :, :, :], uq_raw[:, :, :, NOPE:NOPE + ROPE]).then_inc(s_scaled, 1)

            def sgu_stats(l, t):
                dve.wait_ge(s_zev, l * UNITS + unit(SGU_V, t) + 1)
                ins = v.bn_stats(bst[:, t, :], Y[:, t, Y_SGU:Y_SGU + CW])
                if t == NT - 1:
                    link(ins)

            def sgu_norm(l):
                for t in range(NT):
                    ins = v.bn_aggr(mv[:, t, :], bst[:, t, :])
                link(ins)
                r_sqrt(mv[:, :, 1], NT, 1.0, st[:, 24:24 + NT], TMP)
                for t in range(NT):
                    y = Y[:, t, Y_SGU:Y_SGU + CW]
                    v.tensor_scalar(y, y, mv[:, t, 0:1], st[:, 24 + t:25 + t], ALU.subtract, ALU.mult).then_inc(s_vn, 1)

            def sgu_mix(l, t):
                name = ("sgu", l, t)
                bank = aux_ready(dve, name)
                bias = cols[:, BS:BS + 4].unsqueeze(2).to_broadcast([P, HEADS, 64])
                o = Y[:, t, Y_SGU:Y_SGU + CW].rearrange("p (g n) -> p g n", g=HEADS)
                aux_release(v.tensor_tensor(o, bank[:, 0:CW].rearrange("p (g n) -> p g n", g=HEADS), bias,
                                            ALU.add), name)

            def conv_token(l, ct):
                for half in range(2):
                    name = ("cT", l, ct, half)
                    bank = aux_ready(dve, name)
                    aux_release(v.tensor_copy(Y[:, 4 * half:4 * half + 4, Y_CONV + ct * P:Y_CONV + (ct + 1) * P],
                                              bank.rearrange("p (k n) -> p k n", k=4)), name)

            def conv_norm(l):
                emptied(dve, ("cT", l, 1, 1))
                for t in range(NT):
                    ins = v.bn_stats(bst[:, t, :], Y[:, t, Y_CONV:Y_CONV + CW])
                link(ins)
                for t in range(NT):
                    ins = v.bn_aggr(mv[:, t, :], bst[:, t, :])
                link(ins)
                r_sqrt(mv[:, :, 1], NT, 1.0, st[:, 24:24 + NT], TMP)
                for t in range(NT):
                    yc = Y[:, t, Y_CONV:Y_CONV + CW]
                    v.tensor_scalar(yc, yc, mv[:, t, 0:1], st[:, 24 + t:25 + t], ALU.subtract, ALU.mult).then_inc(s_cln, 1)

            def q_rotate(l, pair, b):
                name = ("RT", l, pair, b)
                bank = aux_ready(dve, name)
                if pair == 0:
                    aux_ready(dve, ("cT", l, 1, b))
                else:
                    aux_ready(dve, ("qr", l, 1, b))
                if b == 1:
                    emptied(dve, ("RT", l, pair, 0))
                for h in range(2):
                    src = bank.rearrange("p (t h n) -> p t h n", t=4, h=2)[:, :, h, :]
                    t1 = scr[:, 0:256].rearrange("p (a n) -> p a n", a=4)
                    t2 = scr[:, 256:512].rearrange("p (a n) -> p a n", a=4)
                    ins = rope(qrt[:, 4 * b:4 * b + 4, h, :], src, cosd[:, 4 * b:4 * b + 4, :],
                               sind[:, 4 * b:4 * b + 4, :], t1, t2)
                    if h == 0:
                        link(ins)
                aux_release(ins, name)

            def q_nope_lo(l, h):
                for b in range(2):
                    name = ("QA", l, h, b)
                    bs = slice(b * BANK, (b + 1) * BANK)
                    lo_split(q_lo[:, bs], aux_ready(dve, name), q_hi[:, bs], s_qhi, (l * HEADS + h) * 2 + b + 1, name)

            def q_rope_lo(l, h):
                for b in range(2):
                    name = ("qr", l, h, b)
                    bs = slice(b * BANK, (b + 1) * BANK)
                    lo_split(qr_lo[:, bs], aux_ready(dve, name)[0:ROPE, :], qr_st[0:ROPE, bs], s_qrhi,
                             (l * HEADS + h) * 2 + b + 1, name)

            def v_lo_split(l, h):
                for b in range(2):
                    name = ("V", l, h, b)
                    sl = (slice(None), slice(4 * b, 4 * b + 4), slice(None))
                    lo_split(v_lo[sl], aux_ready(dve, name).rearrange("p (k n) -> p k n", k=4), v_hi[sl], s_vhi,
                             (l * HEADS + h) * 2 + b + 1, name)

            def row_max(l, n):
                keys = (ORDER[n % NT] + 1) * P
                dve.wait_ge(s_S, l * STEPS + n + 1)
                if n >= 2:
                    dve.wait_ge(s_exp, l * STEPS + n - 1)
                src = ps[:, 2 * (n % 2):2 * (n % 2) + 2, :].rearrange("p a b -> p (a b)")[:, 0:keys]
                v.tensor_reduce(nmax[:, n % 2:n % 2 + 1], src, AX_X, ALU.max, negate=True).then_inc(s_nmax, 1)

            def p_lo_split(l, n):
                i = ORDER[n % NT]
                for b in range(i // 4 + 1):
                    name = ("PT", l, n, b)
                    m = min(4, i + 1 - 4 * b)
                    sl = (slice(None), slice(4 * b, 4 * b + m), slice(None))
                    lo_split(pt_lo[sl], aux_ready(dve, name)[:, 0:m * P].rearrange("p (k n) -> p k n", k=m), pt_hi[sl],
                             s_pthi, pt_count(l, n, b), name)

            def att_out(l, n):
                h, i = n // NT, ORDER[n % NT]
                name = ("O", l, n)
                link(v.reciprocal(st[:, 40 + n % 2:41 + n % 2], rsum[:, n % 4:n % 4 + 1]))
                bank = aux_ready(dve, name)
                y = Y[:, i, h * P:(h + 1) * P]
                aux_release(v.scalar_tensor_tensor(y, bank[:, 0:P], st[:, 40 + n % 2:41 + n % 2], y, ALU.mult,
                                                   ALU.mult), name)

            def y_lo(l, t):
                for b in range(2):
                    name = ("yT", l, t, b)
                    sl = (slice(None), t % 2, slice(4 * b, 4 * b + 4), slice(None))
                    lo_split(yT_lo[sl], aux_ready(dve, name).rearrange("p (k n) -> p k n", k=4), yT_hi[sl], s_yhi,
                             (l * NT + t) * 2 + b + 1, name)

            def conv_gate(l, t):
                name = ("pw", l, t)
                bank = aux_ready(dve, name)
                dve.wait_ge(s_zev, (l + 1) * UNITS)
                y = Y[:, t, Y_CONV:Y_CONV + CW]
                aux_release(v.tensor_tensor(y, bank[:, 0:CW], y, ALU.mult), name)

            for l in range(DEPTH):
                for t in range(3):
                    h_lo(l, t)
                for t in range(NT):
                    if t + 3 < NT:
                        h_lo(l, t + 3)
                q_norm(l)
                small_weights(l)
                ada_step(l, CONV_A, 0)
                ada_step(l, CONV_A, 1)
                bank = aux_ready(dve, ("taps", l))
                aux_release(v.tensor_copy(taps[:, :, :], bank[:, 0:64].rearrange("p (c k) -> p c k", c=2)[:, :, 0:CONV_K]),
                            ("taps", l))
                bank = aux_ready(dve, ("ws", l))
                aux_release(v.tensor_copy(wsT[:, :, :], bank.rearrange("p (g n) -> p g n", g=HEADS)),
                            ("ws", l))
                ada_step(l, CONV_A, 2)
                for h in range(2):
                    absorb_operands(l, h)
                ada_step(l, CONV_A, 3)
                for h in range(2):
                    absorbed(l, h)
                for h in range(2, 4):
                    absorb_operands(l, h)
                for i in range(4):
                    dve.wait_ge(s_zev, l * UNITS + unit(CONV_B, i) + 1)
                    ct, half = i // 2, i % 2
                    ch = convh[:, ct, HALO + half * BANK:HALO + (half + 1) * BANK]
                    v.scalar_tensor_tensor(ch, scr[:, :], 1.0, ch, ALU.add, ALU.mult).then_inc(s_glu, 1)
                    if i == 0:
                        absorbed(l, 2)
                        absorbed(l, 3)
                    if i >= 2:
                        dve.wait_ge(s_glu, l * 4 + i)
                        for m in (0, 1, 2):
                            conv_pair(l, 3 * (i - 2) + m)
                    ada_step(l, CONV_B, i)
                dve.wait_ge(s_glu, (l + 1) * 4)
                m = 6
                for t in range(NT):
                    for _ in range(2 if t % 3 == 2 else 1):
                        conv_pair(l, m)
                        m += 1
                    ada_step(l, KV, t)
                kv_norm(l)
                for t in range(NT):
                    sgu_stats(l, t)
                    if t >= 2:
                        conv_pair(l, m)
                        m += 1
                    if t >= 5:
                        kv_lo_split(l, 2 * (t - 5))
                        kv_lo_split(l, 2 * (t - 5) + 1)
                sgu_norm(l)
                kv_lo_split(l, 6)
                kv_lo_split(l, 7)
                for t in range(NT):
                    if t >= 5:
                        sgu_mix(l, 2 * (t - 5))
                        sgu_mix(l, 2 * (t - 5) + 1)
                    if t >= 1:
                        conv_pair(l, m)
                        m += 1
                sgu_mix(l, 6)
                sgu_mix(l, 7)
                for t in range(2 * NT):
                    for _ in range(2):
                        conv_pair(l, m)
                        m += 1
                    if t == 2:
                        conv_token(l, 0)
                while m < len(pairs):
                    conv_pair(l, m)
                    m += 1
                for t in range(NT):
                    ada_step(l, G_SGU, t)
                    if t == 2:
                        conv_token(l, 1)
                        conv_norm(l)
                for t in range(NT):
                    ada_step(l, G_CONV, t)
                    if t in (4, 5):
                        q_rotate(l, 0, t - 4)
                q_nope_lo(l, 0)
                q_rope_lo(l, 0)
                v_lo_split(l, 0)
                row_max(l, 0)
                row_max(l, 1)
                for n in range(STEPS):
                    pos, h = n % NT, n // NT
                    if pos == 0 and h > 0:
                        v_lo_split(l, h)
                    if pos == NT - 2 and h + 1 < HEADS:
                        q_nope_lo(l, h + 1)
                    if n > 0:
                        att_out(l, n - 1)
                    p_lo_split(l, n)
                    if pos == NT - 2 and h + 1 < HEADS:
                        q_rope_lo(l, h + 1)
                    if n < NT:
                        conv_gate(l, n)
                    if n + 2 < STEPS:
                        row_max(l, n + 2)
                    if n in (11, 12):
                        q_rotate(l, 1, n - 11)
                    ada_step(l, ATT, n)
                att_out(l, STEPS - 1)
                y_lo(l, 0)
                for t in range(NT):
                    if t + 1 < NT:
                        y_lo(l, t + 1)
                    g = l * NT + t
                    dve.wait_ge(s_osq, g + 1)
                    r_sqrt(ssq[:, 2 + t % 2:3 + t % 2], 1, 1.0 / D, RS, TMP)
                    src = ps[:, 2 * (t % 2):2 * (t % 2) + 2, :].rearrange("p a b -> p (a b)")
                    v.scalar_tensor_tensor(Y[:, t, :], src, RS, acc[:, :], ALU.mult, ALU.mult).then_inc(s_ofree, 1)
                    dve.wait_ge(s_ofree, g + 1)
                    before = 4 * l
                    dve.wait_ge(s_xin[t % 2], (before + t // 2 + 1) * 16)
                    v.tensor_tensor(xb[:, t % 2, :], xb[:, t % 2, :], Y[:, t, :], ALU.add).then_inc(s_x1, 1)
                    if l + 1 < DEPTH:
                        h_norm(l + 1, t)

        @block.gpsimd
        def _(pool):
            g_ = nc.gpsimd
            chain = [0]
            g_.memset(ident[:, :], 0.0).then_inc(s_cst, 1)
            g_.memset(ones[:, :], 1.0).then_inc(s_cst, 1)
            g_.memset(mask[:, :], 0.0).then_inc(s_cst, 1)
            g_.memset(convh[:, :, 0:HALO], 0.0)
            pool.wait_ge(s_cst, 3)
            g_.affine_select(out=ident[:, :], in_=ident[:, :], compare_op=ALU.not_equal, fill=1.0, base=0,
                             pattern=[[-1, P]], channel_multiplier=1).then_inc(s_cst, 1)
            g_.affine_select(out=mask[:, :], in_=mask[:, :], compare_op=ALU.is_ge, fill=MASKED, base=0,
                             pattern=[[-1, P]], channel_multiplier=1).then_inc(s_cst, 1)
            pool.wait_ge(s_cst, 5)
            g_.tensor_copy(ident_r[:, :], ident[:, :])
            g_.tensor_copy(mask_r[:, :], mask[:, :]).then_inc(s_cst, 1)

            def lo_piece(l, p):
                n = l * W_PIECES + p
                pool.wait_ge(s_hi, n + 1)
                if p < 2 * NCH:
                    cc = l * NCH + p // 2
                    width = CHUNKS[p // 2][1]
                    sl = (slice(None), cc % 2, slice(4 * (p % 2), 4 * (p % 2) + 4), slice(0, width))
                    hi, lo = w_hi[sl], w_lo[sl]
                    src = wraw[:, n % 2, :].rearrange("p (k n) -> p k n", k=4)[:, :, 0:width]
                else:
                    k = p - 2 * NCH
                    hi, lo, src = act_hi[:, k, :], act_lo[:, k, :], wraw[:, n % 2, :]
                g_.tensor_tensor(lo, src, hi.bitcast(F32), ALU.subtract).then_inc(s_lo, 1)

            def add_shift(g, t):
                if g == 0:
                    for half in range(2):
                        emptied(pool, ("boot", 1, half))
                pool.wait_ge(s_hn, g * NT + t + 1)
                g_.tensor_tensor(Y[:, t, :], Y[:, t, :], S_bc[:, :], ALU.add).then_inc(s_h, 1)

            lo_piece(0, 0)
            lo_piece(0, 1)
            for t in range(H0, NT):
                add_shift(0, t)
            lo_piece(0, 2)
            lo_piece(0, 3)
            for l in range(DEPTH):
                for p in range(4, 6):
                    lo_piece(l, p)
                emptied(pool, ("ws", l))
                g_.affine_select(out=wsT[:, :, :], in_=wsT[:, :, :], compare_op=ALU.is_ge, fill=0.0, base=0,
                                 pattern=[[0, HEADS], [1, P]], channel_multiplier=-1).then_inc(s_wsT, 1)
                for p in range(6, 12):
                    lo_piece(l, p)
                for t in range(NT):
                    pool.wait_ge(s_vn, l * NT + t + 1)
                    gv = Y[:, t, Y_SGU:Y_SGU + CW]
                    chain[0] += 1
                    g_.tensor_tensor(gv, gv, sgu_g[:, :], ALU.mult).then_inc(s_cst, 1)
                    pool.wait_ge(s_cst, 6 + chain[0])
                    g_.tensor_tensor(gv, gv, sgu_b[:, :], ALU.add).then_inc(s_vg, 1)
                    if t in (4, 7):
                        lo_piece(l, 12 + (t - 4) // 3)
                for t in range(NT):
                    emptied(pool, ("sgu", l, t))
                    pool.wait_ge(s_zev, l * UNITS + unit(SGU_U, t) + 1)
                    y = Y[:, t, Y_SGU:Y_SGU + CW]
                    g_.tensor_tensor(y, y, Y[:, t, Y_U:Y_U + CW], ALU.mult).then_inc(s_mul, 1)
                for p in range(14, 18):
                    lo_piece(l, p)
                for t in range(NT):
                    pool.wait_ge(s_zev, l * UNITS + unit(G_SGU, t) + 1)
                    y = Y[:, t, Y_SGU:Y_SGU + CW]
                    g_.tensor_tensor(y, y, gtmp[:, t % 2, :], ALU.mult).then_inc(s_mul, 1)
                    if t in (2, 5):
                        lo_piece(l, 18 + (t - 2) // 3)
                for p in range(2 * NCH, W_PIECES):
                    lo_piece(l, p)
                if l + 1 < DEPTH:
                    for t in range(NT):
                        add_shift(l + 1, t)
                        if 3 <= t < 7:
                            lo_piece(l + 1, t - 3)


_INS = ["x", "c", "positions", "w_ada", "b_ada", "g_pre", "g_post", "w_in", "q_norm_g", "w_uq", "kv_norm_g", "w_ukv",
        "conv_w", "conv_b", "conv_ln_g", "conv_ln_b", "w_pw2", "sgu_ln_g", "sgu_ln_b", "w_s", "b_s", "w_out"]


def kernel(**inputs):
    import numpy as np
    import concourse.bacc as bacc
    from concourse import mybir as mb
    from concourse.bass_utils import run_bass_kernel_spmd

    nc = bacc.Bacc("TRN2", target_bir_lowering=False, num_devices=1, dynamic_dma_scratch_size=1024)
    arrays = {n: np.ascontiguousarray(inputs[n]) for n in _INS}
    arrays["x"] = arrays["x"].reshape(SEQ, D)
    arrays["inv_freq"] = (10000.0 ** (-np.arange(0, ROPE, 2) / ROPE)).astype(np.float32)
    aps, in_map = {}, {}
    for name, arr in arrays.items():
        in_map[f"in_{name}"] = arr
        aps[name] = nc.dram_tensor(f"in_{name}", arr.shape, mb.dt.from_np(arr.dtype), kind="ExternalInput").ap()
    x_mid = nc.dram_tensor("x_mid", (SEQ, D), mb.dt.float32).ap()
    out = nc.dram_tensor("out", (SEQ, D), mb.dt.float32, kind="ExternalOutput").ap()
    trunk(nc, aps, out, x_mid)
    r = run_bass_kernel_spmd(nc, [in_map], core_ids=[0])
    return r.results[0]["out"].reshape(1, SEQ, D)
```

```python
from contextlib import ExitStack

import concourse.bass as bass
from concourse import mybir

ALU = mybir.AluOpType
ACT = mybir.ActivationFunctionType
F32 = mybir.dt.float32
F32R = mybir.dt.float32r
I32 = mybir.dt.int32
AX_X = mybir.AxisListType.X

P = 128
D = 1024
SEQ = 1024
DEPTH = 2
NT = SEQ // P
KD = D // P
HEADS = 4
NOPE = 128
ROPE = 64
Q_RANK = 256
KV_RANK = 128
CONV_K = 31
HALO = CONV_K - 1
EPS = 1e-6
SCALE = (NOPE + ROPE) ** -0.5
MASKED = -1e30
BANK = 512
CW = 256

Q, CONV_A, CONV_B, KV, SGU_V, SGU_U, G_ATT0, G_ATT1, G_SGU, G_CONV = range(10)
CHUNKS = [(0, 256), (960, 256), (1216, 256), (256, 192), (1984, 256), (1728, 256),
          (448, 256), (704, 256), (2240, 256), (1472, 256)]
NCH = len(CHUNKS)
UNITS = (NCH - 2) * NT + 2 * 4


def unit(c, i):
    if c == Q:
        return i
    if c in (CONV_A, CONV_B):
        return 8 + 4 * (c - CONV_A) + i
    return 16 + 8 * (c - KV) + i


Y_ATT, Y_CONV, Y_SGU = 0, 512, 768
Y_Q, Y_U, Y_KV = 0, 0, 256
W_PIECES = 2 * NCH + KD
STEPS = HEADS * NT
ORDER = [4, 0, 7, 1, 6, 2, 5, 3]


class BankRing:

    def __init__(self):
        self.uses = {}

    def take(self, name):
        n = len(self.uses)
        self.uses[name] = (n % 4, n // 4)
        return self.uses[name]


def trunk(nc, a, out, x_mid):
    with ExitStack() as ctx:
        base = 1152
        at = [base]

        def place(name, shape, dt, offset=None):
            size = 4
            for s in shape[1:]:
                size *= s
            if offset is None:
                offset = at[0]
                at[0] += (size + 31) // 32 * 32
            return nc.alloc_sbuf_tensor_at(name, shape, dt, offset=offset)

        def sem(name):
            return ctx.enter_context(nc.semaphore(name))

        act_hi = place("act_hi", [P, KD, SEQ], F32R)
        act_lo = place("act_lo", [P, KD, SEQ], F32R)
        boot = place("boot", [P, 2, KD, D], F32, base)
        Y = place("Y", [P, NT, D], F32)
        w_at = at[0]
        w_hi = place("w_hi", [P, 2, KD, CW], F32R)
        w_lo = place("w_lo", [P, 2, KD, CW], F32R)
        kb = 1024
        q_hi = place("q_hi", [P, SEQ], F32R, w_at)
        q_lo = place("q_lo", [P, SEQ], F32R, w_at + 4 * kb)
        qr_st = place("qr_st", [P, SEQ], F32R, w_at + 8 * kb)
        qr_lo = place("qr_lo", [ROPE, SEQ], F32R, w_at + 12 * kb)
        v_hl = place("v_hl", [P, NT, 2, P], F32R, w_at + 16 * kb)
        pt_hi = place("pt_hi", [P, NT, P], F32R, w_at + 24 * kb)
        pt_lo = place("pt_lo", [P, NT, P], F32R, w_at + 28 * kb)
        wraw = place("wraw", [P, 2, 1024], F32)
        araw = place("araw", [P, 2, BANK], F32)
        qk_at = at[0]
        qnT = place("qnT", [P, 2, SEQ], F32)
        kv_hi = place("kv_hi", [P, SEQ], F32R)
        kv_lo = place("kv_lo", [P, SEQ], F32R)
        kr_st = place("kr_st", [P, SEQ], F32R)
        boot_row = place("boot_row", [1, 3, D], F32, qk_at)
        yT_hi = place("yT_hi", [P, 2, KD, P], F32R, qk_at)
        yT_lo = place("yT_lo", [P, 2, KD, P], F32R, qk_at + 8 * kb)
        convh = place("convh", [P, 2, HALO + SEQ], F32)
        convo_at = at[0]
        convo = place("convo", [P, 2, BANK], F32)
        uk_raw = place("uk_raw", [P, HEADS, NOPE], F32, convo_at)
        uv_raw = place("uv_raw", [P, HEADS, P], F32, convo_at + 2 * kb)
        qrt = place("qrt", [P, NT, 2, ROPE], F32, convo_at)
        xb_at = at[0]
        xb = place("xb", [P, 2, D], F32)
        uq_raw = place("uq_raw", [P, 2, HEADS, NOPE + ROPE], F32, xb_at)
        ws_raw = place("ws_raw", [P, HEADS, P], F32, xb_at + 6 * kb)
        acc = place("acc", [P, D], F32)
        A_bc = place("A_bc", [P, D], F32)
        S_bc = place("S_bc", [P, D], F32)
        Wq = place("Wq", [P, 2, HEADS, P], F32)
        silu_bc = place("silu_bc", [P, KD, P], F32, at[0] - 2 * HEADS * P * 4)
        uqr = place("uqr", [P, 2, HEADS, ROPE], F32)
        uv_hi = place("uv_hi", [P, HEADS, P], F32R)
        uv_lo = place("uv_lo", [P, HEADS, P], F32R)
        pw2 = place("pw2", [P, 2, CW], F32)
        wsT = place("wsT", [P, HEADS, P], F32)
        ident = place("ident", [P, P], F32)
        ident_r = place("ident_r", [P, P], F32R)
        ones = place("ones", [P, P], F32)
        mask = place("mask", [P, P], F32)
        mask_r = place("mask_r", [P, P], F32R)
        cosd = place("cosd", [P, NT, ROPE], F32)
        sind = place("sind", [P, NT, ROPE], F32)
        sgu_g = place("sgu_g", [P, CW], F32)
        sgu_b = place("sgu_b", [P, CW], F32)
        qtmp = place("qtmp", [P, 2, CW], F32)
        gtmp = place("gtmp", [P, 2, CW], F32)
        scr = place("scr", [P, BANK], F32)
        taps = place("taps", [P, 2, CONV_K], F32)
        cols = place("cols", [P, 24], F32)
        silu_c = place("silu_c", [P, 2 * KD], F32)
        st = place("st", [P, 64], F32)
        bst = place("bst", [P, NT, 6], F32)
        mv = place("mv", [P, NT, 2], F32)
        ssq = place("ssq", [P, 32], F32)
        rsum = place("rsum", [P, 4], F32)
        nmax = place("nmax", [P, 2], F32)
        posi = place("posi", [P, NT], I32)
        posf = place("posf", [P, NT], F32)
        freq = place("freq", [P, ROPE // 2], F32)

        GQ, GKV, CB, CLG, CLB, BS = 0, 2, 3, 5, 7, 9

        ps = ctx.enter_context(nc.psum_tensor("ps", [P, 8, BANK], F32))

        w_arrived = [sem(f"w_arrived{i}") for i in range(2)]
        ada_arrived = [sem(f"ada_arrived{i}") for i in range(2)]
        x_arrived = [sem(f"x_arrived{i}") for i in range(2)]
        small_arrived = sem("small_arrived")
        first_h_ready = sem("first_h_ready")
        boot_arrived = [sem(f"boot_arrived{i}") for i in range(4)]
        boot_row_arrived = sem("boot_row_arrived")
        first_x_arrived = [sem(f"first_x_arrived{i}") for i in range(4)]
        silu_bc_ready = sem("silu_bc_ready")
        once_arrived = sem("once_arrived")
        result_stored = [sem(f"result_stored{i}") for i in range(2)]
        pool_done = sem("pool_done")
        w_hi_ready = sem("w_hi_ready")
        w_split = sem("w_split")
        ada_used = sem("ada_used")
        z_done = sem("z_done")
        z_read = sem("z_read")
        aux_done = [sem(f"aux_done{i}") for i in range(4)]
        aux_read = [sem(f"aux_read{i}") for i in range(4)]
        h_ready = sem("h_ready")
        h_hi_ready = sem("h_hi_ready")
        q_normed = sem("q_normed")
        kv_normed = sem("kv_normed")
        kv_hi_ready = sem("kv_hi_ready")
        v_normed = sem("v_normed")
        v_scaled = sem("v_scaled")
        sgu_multiplied = sem("sgu_multiplied")
        conv_done = sem("conv_done")
        glu_done = sem("glu_done")
        conv_normed = sem("conv_normed")
        small_scaled = sem("small_scaled")
        ws_masked = sem("ws_masked")
        ada_summed = sem("ada_summed")
        scores_ready = sem("scores_ready")
        max_ready = sem("max_ready")
        probs_ready = sem("probs_ready")
        p_hi_ready = sem("p_hi_ready")
        q_hi_ready = sem("q_hi_ready")
        qr_hi_ready = sem("qr_hi_ready")
        v_hi_ready = sem("v_hi_ready")
        y_hi_ready = sem("y_hi_ready")
        pv_lo_copied = sem("pv_lo_copied")
        out_ready = sem("out_ready")
        out_squared = sem("out_squared")
        out_read = sem("out_read")
        x_updated = sem("x_updated")
        x_squared = sem("x_squared")
        h_normed = sem("h_normed")
        silu_ready = sem("silu_ready")
        angles_ready = sem("angles_ready")
        dve_chain = sem("dve_chain")
        sines_ready = sem("sines_ready")

        ring = BankRing()
        block = ctx.enter_context(nc.Block())

        ATT = "attention"
        THIRD = {"shift": 0, "scale": 1, "gate": 2}
        STAGE_AT = {c: (0, 8, 16, 24, 32, 40, 48, 56, 64, 72)[c] for c in range(NCH)}
        LAYER_TIME = 180

        def when(l, stage, i):
            if stage == ATT:
                return l * LAYER_TIME + 80 + 2 * i
            return l * LAYER_TIME + STAGE_AT[stage] + (2 if stage in (CONV_A, CONV_B) else 1) * i

        def ada_plan():
            plan = []
            for l in range(DEPTH):
                if l + 1 < DEPTH:
                    job = [(l + 1, third, half) for third in ("scale", "shift") for half in range(2)]
                    plan += [(l, CONV_A, (0, 0, 1, 1, 2, 2, 3, 3)[j], job[0], j) for j in range(KD)]
                    for i in range(4):
                        if i == 1:
                            plan += [(l, CONV_B, i, job[0], j) for j in (KD, KD + 1)]
                        plan += [(l, CONV_B, i, job[1], j) for j in (2 * i, 2 * i + 1)]
                    plan += [(l, KV, 5, job[1], j) for j in (KD, KD + 1)]
                    plan += [(l, G_SGU, j, job[2], j) for j in range(KD)]
                    for i in range(NT):
                        if i == 3:
                            plan.append((l, G_CONV, i, job[2], KD))
                        plan.append((l, G_CONV, i, job[3], i))
                    plan.append((l, ATT, 0, job[3], KD))
                for half in range(2):
                    job = (l, "gate", half)
                    first = 8 + 10 * half
                    plan += [(l, ATT, first + j, job, j) for j in range(KD)]
                    plan += [(l, ATT, first + KD + 1, job, j) for j in (KD, KD + 1)]
            return plan

        ada_order = [(job, j) for _, _, _, job, j in ada_plan()]
        ada_jobs = [job for job, j in ada_order if j == KD - 1]

        def piece_used(eng, n):
            job, j = ada_order[n]
            if j == KD - 1:
                eng.wait_ge(ada_summed, 1 + ada_jobs.index(job) + 1)
            elif j == KD:
                emptied(eng, ("ada", *job))
            else:
                eng.wait_ge(ada_used, sum(j_ not in (KD - 1, KD) for _, j_ in ada_order[:n + 1]))

        def aux_ready(eng, name):
            b, n = ring.uses[name]
            eng.wait_ge(aux_done[b], n + 1)
            return ps[:, 4 + b, :]

        def emptied(eng, name):
            b, n = ring.uses[name]
            eng.wait_ge(aux_read[b], n + 1)

        def wait_h(eng, l, t):
            if l == 0 and t < H0:
                eng.wait_ge(first_h_ready, t + 1)
            else:
                eng.wait_ge(h_ready, l * NT + t + 1 - H0)

        def aux_release(ins, name):
            return ins.then_inc(aux_read[ring.uses[name][0]], 1)

        H0 = 2
        PREP = 14

        def prep_all(l):
            return (l + 1) * PREP * 16

        def conv_taps(l, ct, k, half):
            return ((l * 2 + ct) * CONV_K + k) * 2 + half + 1

        def pt_count(l, n, b):
            banks = [i // 4 + 1 for i in ORDER]
            return (l * HEADS + n // NT) * sum(banks) + sum(banks[:n % NT]) + b + 1

        @block.tensor
        def _(pe):
            mm = nc.tensor.matmul

            def take(name):
                b, n = ring.take(name)
                if n:
                    pe.wait_ge(aux_read[b], n)
                return ps[:, 4 + b, :], aux_done[b]

            def three(out_, a_hi, a_lo, b_hi, b_lo, first=True, last=True):
                mm(out_, a_hi, b_hi, start=first, stop=False)
                mm(out_, a_hi, b_lo, start=False, stop=False)
                return mm(out_, a_lo, b_hi, start=False, stop=last)

            def ada(l, third, half):
                bank, done = take(("ada", l, third, half))
                pe.wait_ge(ada_summed, 1 + ada_jobs.index((l, third, half)) + 1)
                mm(bank, ones[:, :], acc[:, half * BANK:(half + 1) * BANK], start=True, stop=True).then_inc(done, 1)

            def h_transpose(l, t):
                for a_ in range(2):
                    bank, done = take(("hT", l, t, a_))
                    wait_h(pe, l, t)
                    for j in range(4):
                        k = 4 * a_ + j
                        ins = nc.tensor.transpose(bank[:, j * P:(j + 1) * P], Y[:, t, k * P:(k + 1) * P], ident[:, :])
                    ins.then_inc(done, 1)

            def z(l, c, i):
                u = l * UNITS + unit(c, i)
                if u >= 4:
                    pe.wait_ge(z_read, u - 3)
                if l > 0 and c == Q and i < 4:
                    pe.wait_ge(out_read, l * NT - 1 + i // 2)
                if i == 0:
                    pe.wait_ge(w_split, l * W_PIECES + 2 * c + 2)
                slot = (l * NCH + c) % 2
                width = CHUNKS[c][1]
                if c in (CONV_A, CONV_B):
                    ct, half = i // 2, i % 2
                    if c == CONV_A:
                        emptied(pe, ("hT", l, 4 * half + 3, 1))
                    o = ps[:, u % 4, :]
                    for k in range(KD):
                        cs = slice(ct * P, (ct + 1) * P)
                        ts = slice(half * BANK, (half + 1) * BANK)
                        ins = three(o, w_hi[:, slot, k, cs], w_lo[:, slot, k, cs], act_hi[:, k, ts], act_lo[:, k, ts],
                                    k == 0, k == KD - 1)
                else:
                    if c == Q:
                        emptied(pe, ("hT", l, i, 1))
                    o = ps[:, u % 4, 0:width]
                    for k in range(KD):
                        ts = slice(i * P, (i + 1) * P)
                        ins = three(o, act_hi[:, k, ts], act_lo[:, k, ts], w_hi[:, slot, k, 0:width],
                                    w_lo[:, slot, k, 0:width], k == 0, k == KD - 1)
                ins.then_inc(z_done, 1)

            def q_transpose(l, t):
                bank, done = take(("qT", l, t))
                pe.wait_ge(q_normed, l * NT + t + 1)
                for k in range(2):
                    ins = nc.tensor.transpose(bank[:, k * P:(k + 1) * P], Y[:, t, k * P:(k + 1) * P], ident[:, :])
                ins.then_inc(done, 1)

            def kv_transpose(l, t):
                bank, done = take(("kvT", l, t))
                pe.wait_ge(kv_normed, l * NT + t + 1)
                nc.tensor.transpose(bank[:, 0:P], Y[:, t, Y_KV:Y_KV + P], ident[:, :])
                nc.tensor.transpose(bank[0:ROPE, P:2 * P], Y[:, t, Y_KV + P:Y_KV + P + ROPE], ident[:, :]).then_inc(done, 1)

            def taps_transpose(l):
                bank, done = take(("taps", l))
                pe.wait_ge(small_arrived, prep_all(l))
                for ct in range(2):
                    ins = nc.tensor.transpose(bank[:, ct * 32:ct * 32 + CONV_K], gtmp[0:CONV_K, 0, ct * P:(ct + 1) * P],
                                              ident[0:CONV_K, 0:CONV_K])
                ins.then_inc(done, 1)

            def ws_transpose(l):
                bank, done = take(("ws", l))
                for g in range(HEADS):
                    ins = nc.tensor.transpose(bank[:, g * P:(g + 1) * P], ws_raw[:, g, :], ident[:, :])
                ins.then_inc(done, 1)

            def u_transpose(l, h):
                bank, done = take(("uT", l, h))
                if h == 0:
                    pe.wait_ge(small_scaled, l + 1)
                for k in range(2):
                    nc.tensor.transpose(bank[:, k * P:(k + 1) * P], uq_raw[:, k, h, 0:NOPE], ident[:, :])
                nc.tensor.transpose(bank[:, 2 * P:3 * P], uk_raw[:, h, :], ident[:, :]).then_inc(done, 1)

            def absorb(l, h):
                bank, done = take(("Wq", l, h))
                emptied(pe, ("uT", l, h))
                g = (gtmp, qtmp)[h % 2][:, :, :].rearrange("p a b -> p (a b)")
                for k in range(2):
                    ins = mm(bank[:, k * P:(k + 1) * P], g[:, k * P:(k + 1) * P], g[:, 2 * P:3 * P], start=True, stop=True)
                ins.then_inc(done, 1)

            def spatial(l, half):
                for pair in range(2):
                    bank, done = take(("sgu", l, half, pair))
                    pe.wait_ge(v_scaled, l * NT + 4 * half + 4)
                    pe.wait_ge(ws_masked, l + 1)
                    for i in range(2):
                        g = 2 * pair + i
                        ins = mm(bank[:, i * 256:(i + 1) * 256], wsT[:, g, :],
                                 Y[:, 4 * half:4 * half + 4, Y_SGU + g * 64:Y_SGU + (g + 1) * 64], start=True, stop=True)
                    ins.then_inc(done, 1)

            def conv_to_token(l, ct):
                for half in range(2):
                    bank, done = take(("cT", l, ct, half))
                    pe.wait_ge(conv_done, conv_taps(l, ct, CONV_K - 1, half))
                    for j in range(4):
                        src = convo[:, half, j * P:(j + 1) * P] if ct == 0 else Y[:, 4 * half + j, Y_CONV + P:Y_CONV + CW]
                        ins = nc.tensor.transpose(bank[:, j * P:(j + 1) * P], src, ident[:, :])
                    ins.then_inc(done, 1)

            def conv_to_feature(l, half):
                for ct in range(2):
                    bank, done = take(("cB", l, ct, half))
                    pe.wait_ge(conv_normed, l * NT + 4 * half + 4)
                    for j in range(4):
                        cs = Y_CONV + ct * P
                        ins = nc.tensor.transpose(bank[:, j * P:(j + 1) * P], Y[:, 4 * half + j, cs:cs + P], ident[:, :])
                    ins.then_inc(done, 1)

            def pointwise(l, t):
                bank, done = take(("pw", l, t))
                emptied(pe, ("cB", l, 1, t // 4))
                for ct in range(2):
                    ins = mm(bank[:, 0:CW], convh[:, ct, HALO + t * P:HALO + (t + 1) * P], pw2[:, ct, :],
                             start=ct == 0, stop=ct == 1)
                ins.then_inc(done, 1)

            def q_rope(l, pair, b):
                bank, done = take(("RT", l, pair, b))
                emptied(pe, ("qT", l, NT - 1))
                for j in range(4):
                    t = 4 * b + j
                    for k in range(2):
                        ins = mm(bank[:, j * P:(j + 1) * P], qnT[:, k, t * P:(t + 1) * P],
                                 uqr[:, k, 2 * pair:2 * pair + 2, :], start=k == 0, stop=k == 1)
                ins.then_inc(done, 1)

            def queries_nope(l, h):
                for b in range(2):
                    bank, done = take(("QA", l, h, b))
                    emptied(pe, ("Wq", l, HEADS - 1))
                    for k in range(2):
                        ins = mm(bank, Wq[:, k, h, :], qnT[:, k, b * BANK:(b + 1) * BANK], start=k == 0, stop=k == 1)
                    ins.then_inc(done, 1)

            def queries_rope(l, h):
                for b in range(2):
                    bank, done = take(("qr", l, h, b))
                    emptied(pe, ("RT", l, h // 2, b))
                    for j in range(4):
                        ins = nc.tensor.transpose(bank[0:ROPE, j * P:(j + 1) * P], qrt[:, 4 * b + j, h % 2, :], ident[:, :])
                    ins.then_inc(done, 1)

            def values(l, h):
                for b in range(2):
                    bank, done = take(("V", l, h, b))
                    emptied(pe, ("kvT", l, NT - 1))
                    for j in range(4):
                        ts = slice((4 * b + j) * P, (4 * b + j + 1) * P)
                        ins = three(bank[:, j * P:(j + 1) * P], kv_hi[:, ts], kv_lo[:, ts], uv_hi[:, h, :], uv_lo[:, h, :])
                    ins.then_inc(done, 1)

            def scores(l, n):
                h, i = n // NT, ORDER[n % NT]
                g = l * STEPS + n
                if n >= 2:
                    pe.wait_ge(probs_ready, g - 1)
                if n < 2:
                    pe.wait_ge(z_read, (l + 1) * UNITS)
                if n % NT == 0:
                    emptied(pe, ("QA", l, h, 1))
                    emptied(pe, ("qr", l, h, 1))
                qs = slice(i * P, (i + 1) * P)
                for b in range(i // 4 + 1):
                    n_keys = min(BANK, (i + 1) * P - b * BANK)
                    ks = slice(b * BANK, b * BANK + n_keys)
                    o = ps[:, 2 * (n % 2) + b, 0:n_keys]
                    three(o, q_hi[:, qs], q_lo[:, qs], kv_hi[:, ks], kv_lo[:, ks], True, False)
                    mm(o, qr_st[:, qs], kr_st[:, ks], start=False, stop=False)
                    diagonal = b == i // 4
                    ins = mm(o, qr_lo[:, qs], kr_st[0:ROPE, ks], start=False, stop=not diagonal)
                    if diagonal:
                        ins = mm(o[:, n_keys - P:n_keys], ident_r[:, :], mask_r[:, :], start=False, stop=True)
                ins.then_inc(scores_ready, 1)

            def p_transpose(l, n):
                i = ORDER[n % NT]
                for b in range(i // 4 + 1):
                    bank, done = take(("PT", l, n, b))
                    pe.wait_ge(probs_ready, l * STEPS + n + 1)
                    for j in range(min(4, i + 1 - 4 * b)):
                        kbk = 4 * b + j
                        ins = nc.tensor.transpose(bank[:, j * P:(j + 1) * P], xb[:, n % 2, kbk * P:(kbk + 1) * P],
                                                  ident[:, :])
                    ins.then_inc(done, 1)

            def pv(l, n):
                h, i = n // NT, ORDER[n % NT]
                bank, done = take(("O", l, n))
                if n % NT == 0:
                    emptied(pe, ("V", l, h, 1))
                for k in range(i + 1):
                    if k % 4 == 0:
                        emptied(pe, ("PT", l, n, k // 4))
                    mm(bank[:, 0:2 * P], pt_hi[:, k, :], v_hl[:, k, :, :], start=k == 0, stop=False)
                    ins = mm(bank[:, 0:P], pt_lo[:, k, :], v_hl[:, k, 0, :], start=False, stop=k == i)
                ins.then_inc(done, 1)

            def y_transpose(l, t):
                for a_ in range(2):
                    bank, done = take(("yT", l, t, a_))
                    if a_ == 0:
                        emptied(pe, ("O", l, (HEADS - 1) * NT + ORDER.index(t)))
                    else:
                        emptied(pe, ("pw", l, t))
                        pe.wait_ge(sgu_multiplied, (l * 2 + 1) * NT + t + 1)
                    for j in range(4):
                        k = 4 * a_ + j
                        ins = nc.tensor.transpose(bank[:, j * P:(j + 1) * P], Y[:, t, k * P:(k + 1) * P], ident[:, :])
                    ins.then_inc(done, 1)

            def out_proj(l, t):
                g = l * NT + t
                if t >= 2:
                    pe.wait_ge(out_read, g - 1)
                else:
                    pe.wait_ge(probs_ready, (l + 1) * STEPS)
                emptied(pe, ("yT", l, t, 1))
                if t == 0:
                    pe.wait_ge(w_split, (l + 1) * W_PIECES)
                for half in range(2):
                    o = ps[:, 2 * (t % 2) + half, :]
                    hs = slice(half * BANK, (half + 1) * BANK)
                    for k in range(KD):
                        ins = three(o, yT_hi[:, t % 2, k, :], yT_lo[:, t % 2, k, :], act_hi[:, k, hs], act_lo[:, k, hs],
                                    k == 0, k == KD - 1)
                ins.then_inc(out_ready, 1)

            pe.wait_ge(pool_done, 6)
            pe.wait_ge(silu_bc_ready, 1)
            pe.wait_ge(boot_row_arrived, 48)
            halves = [slice(half * BANK, (half + 1) * BANK) for half in range(2)]
            for half in range(2):
                bank, done = take(("boot", "g_pre", half))
                mm(bank, ones[0:1, :], boot_row[0:1, 2, halves[half]], start=True, stop=True).then_inc(done, 1)
            banks = [take(("boot", 0, half)) for half in range(2)]
            for half in range(2):
                mm(banks[half][0], ones[0:1, :], boot_row[0:1, 0, halves[half]], start=True, stop=False)
            for k in range(KD):
                if k % 4 == 0:
                    pe.wait_ge(boot_arrived[k // 4], 16)
                for half in range(2):
                    bank, done = banks[half]
                    ins = mm(bank, silu_bc[:, k, :], boot[:, 0, k, halves[half]], start=False, stop=k == KD - 1)
                    if k == KD - 1:
                        ins.then_inc(done, 1)
            banks = [take(("boot", 1, half)) for half in range(2)]
            for half in range(2):
                mm(banks[half][0], ones[0:1, :], boot_row[0:1, 1, halves[half]], start=True, stop=False)
            pe.wait_ge(ada_summed, 1)
            for half in range(2):
                mm(banks[half][0], ones[:, :], acc[:, halves[half]], start=False, stop=False)
            pe.wait_ge(boot_arrived[3], 16)
            for k in range(4, KD):
                for half in range(2):
                    bank, done = banks[half]
                    ins = mm(bank, silu_bc[:, k, :], boot[:, 1, k, halves[half]], start=False, stop=k == KD - 1)
                    if k == KD - 1:
                        ins.then_inc(done, 1)
            for l in range(DEPTH):
                if l == 0:
                    h_transpose(l, 0)
                    h_transpose(l, 1)
                for t in range(NT):
                    z(l, Q, t)
                    if t + 2 < NT:
                        h_transpose(l, t + 2)
                z(l, CONV_A, 0)
                for t in range(4):
                    q_transpose(l, t)
                z(l, CONV_A, 1)
                for t in range(4, NT):
                    q_transpose(l, t)
                taps_transpose(l)
                ws_transpose(l)
                z(l, CONV_A, 2)
                u_transpose(l, 0)
                u_transpose(l, 1)
                z(l, CONV_A, 3)
                absorb(l, 0)
                absorb(l, 1)
                u_transpose(l, 2)
                u_transpose(l, 3)
                for i in range(4):
                    z(l, CONV_B, i)
                    if i == 0:
                        absorb(l, 2)
                        absorb(l, 3)
                    if i == 0 and l + 1 < DEPTH:
                        ada(l + 1, "scale", 0)
                for t in range(NT):
                    z(l, KV, t)
                    if t == 4 and l + 1 < DEPTH:
                        ada(l + 1, "scale", 1)
                for t in range(NT):
                    z(l, SGU_V, t)
                    if t >= 4:
                        kv_transpose(l, 2 * (t - 4))
                        kv_transpose(l, 2 * (t - 4) + 1)
                for t in range(NT):
                    z(l, SGU_U, t)
                    if t == 5:
                        spatial(l, 0)
                for t in range(NT):
                    z(l, G_ATT0, t)
                    if t == 0:
                        spatial(l, 1)
                    if t == 1:
                        conv_to_token(l, 0)
                for t in range(NT):
                    z(l, G_ATT1, t)
                for t in range(NT):
                    z(l, G_SGU, t)
                    if t == 2:
                        conv_to_token(l, 1)
                for t in range(NT):
                    z(l, G_CONV, t)
                    if t == 1:
                        conv_to_feature(l, 0)
                        conv_to_feature(l, 1)
                    if t in (4, 5):
                        q_rope(l, 0, t - 4)
                    if t == 2 and l + 1 < DEPTH:
                        ada(l + 1, "shift", 0)
                queries_nope(l, 0)
                queries_rope(l, 0)
                values(l, 0)
                scores(l, 0)
                scores(l, 1)
                if l + 1 < DEPTH:
                    ada(l + 1, "shift", 1)
                pointwise(l, 0)
                for n in range(STEPS):
                    pos, h = n % NT, n // NT
                    p_transpose(l, n)
                    if n + 2 < STEPS and pos != NT - 2:
                        scores(l, n + 2)
                    if pos == NT - 3 and h + 1 < HEADS:
                        queries_nope(l, h + 1)
                    if pos == NT - 2 and h + 1 < HEADS:
                        queries_rope(l, h + 1)
                    if n + 1 < NT:
                        pointwise(l, n + 1)
                    if n >= STEPS - 2:
                        y_transpose(l, n - (STEPS - 2))
                    if pos == NT - 1 and h + 1 < HEADS:
                        values(l, h + 1)
                    pv(l, n)
                    if pos == NT - 2 and n + 2 < STEPS:
                        scores(l, n + 2)
                    if n in (9, 11):
                        q_rope(l, 1, (n - 9) // 2)
                    if n in (16, 26):
                        ada(l, "gate", (n - 16) // 10)
                for t in range(NT):
                    if 2 <= t + 1 < NT:
                        y_transpose(l, t + 1)
                    if t == NT - 1 and l + 1 < DEPTH:
                        h_transpose(l + 1, 0)
                        h_transpose(l + 1, 1)
                    out_proj(l, t)

        @block.sync
        def _(sp):
            for tile_, src in ((silu_c[:, KD:2 * KD], a["c"].rearrange("b (k p) -> p (b k)", p=P)),
                               (posi[:, :], a["positions"].rearrange("b (t p) -> p (b t)", p=P)),
                               (freq[:, :], a["inv_freq"].partition_broadcast(P))):
                sp.dma_start(tile_, src, allow_slow_non_contiguous=True).then_inc(once_arrived, 16)

            def ada_piece(n):
                (l, third, half), j = ada_order[n]
                if n >= 2:
                    piece_used(sp, n - 2)
                c0 = THIRD[third] * D + half * BANK
                if j < KD:
                    src = a["w_ada"][l, j * P:(j + 1) * P, c0:c0 + BANK]
                elif j == KD:
                    src = a["b_ada"][l, c0:c0 + BANK].partition_broadcast(P)
                else:
                    gain = a["g_pre"] if third == "scale" else a["g_post"]
                    src = gain[l, half * BANK:(half + 1) * BANK].partition_broadcast(P)
                sp.dma_start(araw[:, n % 2, :], src).then_inc(ada_arrived[n % 2], 16)

            def w_piece(l, p):
                n = l * W_PIECES + p
                if n >= 2:
                    sp.wait_ge(w_split, n - 1)
                if p < 2 * NCH:
                    c0, width = CHUNKS[p // 2]
                    k0 = 4 * (p % 2)
                    dst = wraw[:, n % 2, :].rearrange("p (k n) -> p k n", k=4)[:, :, 0:width]
                    src = a["w_in"][l, k0 * P:(k0 + 4) * P, c0:c0 + width].rearrange("(k p) n -> p k n", p=P)
                else:
                    k = p - 2 * NCH
                    dst, src = wraw[:, n % 2, :], a["w_out"][l, k * P:(k + 1) * P, :]
                sp.dma_start(dst, src).then_inc(w_arrived[n % 2], 16)

            def x_tile(l, t):
                if t < 2:
                    emptied(sp, ("PT", l, STEPS - 1, ORDER[-1] // 4))
                if l > 0:
                    sp.wait_ge(result_stored[t % 2], ((l - 1) * NT // 2 + t // 2 + 1) * 16)
                if t >= 2:
                    sp.wait_ge(result_stored[t % 2], (l * NT // 2 + t // 2) * 16)
                    if l + 1 < DEPTH:
                        sp.wait_ge(h_normed, (l + 1) * NT + t - 1)
                src = a["x"] if l == 0 else x_mid
                sp.dma_start(xb[:, t % 2, :], src[t * P:(t + 1) * P, :]).then_inc(x_arrived[t % 2], 16)

            def prep(l):
                if l > 0:
                    sp.wait_ge(x_updated, l * NT)
                    for i in range(2):
                        sp.wait_ge(result_stored[i], l * NT // 2 * 16)
                    sp.wait_ge(h_normed, (l + 1) * NT)
                    emptied(sp, ("cB", l - 1, 1, 1))
                    emptied(sp, ("pw", l - 1, NT - 1))
                    emptied(sp, ("kvT", l - 1, NT - 1))
                else:
                    sp.wait_ge(x_squared, NT)
                for dst, src in (
                    (uq_raw[:, :, :, :], a["w_uq"][l].rearrange("(k p) (h n) -> p k h n", p=P, h=HEADS)),
                    (ws_raw[:, :, :], a["w_s"][l].rearrange("g t s -> t g s")),
                    (uk_raw[:, :, :], a["w_ukv"][l].rearrange("p (h n) -> p h n", h=HEADS)[:, :, 0:NOPE]),
                    (uv_raw[:, :, :], a["w_ukv"][l].rearrange("p (h n) -> p h n", h=HEADS)[:, :, NOPE:]),
                    (gtmp[0:CONV_K, 0, :], a["conv_w"][l]),
                    (pw2[:, :, :], a["w_pw2"][l].rearrange("(c p) n -> p c n", p=P)),
                    (sgu_g[:, :], a["sgu_ln_g"][l].partition_broadcast(P)),
                    (sgu_b[:, :], a["sgu_ln_b"][l].partition_broadcast(P)),
                    (cols[:, GQ:GQ + 2], a["q_norm_g"][l].rearrange("(c p) -> p c", p=P)),
                    (cols[:, GKV:GKV + 1], a["kv_norm_g"][l].rearrange("(c p) -> p c", p=P)),
                    (cols[:, CB:CB + 2], a["conv_b"][l].rearrange("(c p) -> p c", p=P)),
                    (cols[:, CLG:CLG + 2], a["conv_ln_g"][l].rearrange("(c p) -> p c", p=P)),
                    (cols[:, CLB:CLB + 2], a["conv_ln_b"][l].rearrange("(c p) -> p c", p=P)),
                    (cols[:, BS:BS + 4], a["b_s"][l].rearrange("g t -> t g")),
                ):
                    sp.dma_start(dst, src, allow_slow_non_contiguous=True).then_inc(small_arrived, 16)

            def boot_piece(part, half):
                c0 = (THIRD["scale"], THIRD["shift"])[part] * D
                src = a["w_ada"][0, 4 * half * P:4 * (half + 1) * P, c0:c0 + D].rearrange("(k p) n -> p k n", p=P)
                sp.dma_start(boot[:, part, 4 * half:4 * half + 4, :], src).then_inc(boot_arrived[2 * part + half], 16)

            for i, src in enumerate((a["b_ada"][0:1, D:2 * D], a["b_ada"][0:1, 0:D], a["g_pre"][0:1, :])):
                sp.dma_start(boot_row[0:1, i, :], src).then_inc(boot_row_arrived, 16)
            for part in range(2):
                for half in range(2):
                    boot_piece(part, half)
            for i in range(4):
                src = a["x"][2 * i * P:2 * (i + 1) * P, :].rearrange("(t p) n -> p t n", p=P)
                sp.dma_start(Y[:, 2 * i:2 * i + 2, :], src).then_inc(first_x_arrived[i], 16)
                if i == 1:
                    w_piece(0, 0)
                    w_piece(0, 1)
            w_piece(0, 2)
            w_piece(0, 3)
            prep(0)
            w_times = [when(l, p // 2 - 1, (1 + p % 2) if p < 8 else (2, 5)[p % 2]) if 4 <= p < 2 * NCH else
                       when(l, ATT, 8 * ((p - 2 * NCH) // 2) + (2, 4)[p % 2]) if p >= 4 else
                       when(l - 1, ATT, STEPS) + 4 * (p + 3)
                       for l in range(DEPTH) for p in range(W_PIECES)]
            loads = [(w_times[n - 2], w_piece, (n // W_PIECES, n % W_PIECES)) for n in range(4, len(w_times))]
            ada_times = [when(l, stage, i if stage != CONV_A else 0) for l, stage, i, _, _ in ada_plan()]
            loads += [(ada_times[n - 2] if n >= 2 else 0, ada_piece, (n,)) for n in range(len(ada_order))]
            for l in range(DEPTH):
                out_at = when(l, ATT, STEPS)
                loads += [(out_at + (4 * (t - 2) + 3 if t >= 2 else 0), x_tile, (l, t)) for t in range(NT)]
                if l > 0:
                    loads.append((when(l, Q, 0) - 1, prep, (l,)))
            for _, load, which in sorted(loads, key=lambda e: e[0]):
                load(*which)

        @block.scalar
        def _(act):
            fn = nc.scalar.activation

            def hi_piece(l, p):
                n = l * W_PIECES + p
                act.wait_ge(w_arrived[n % 2], (n // 2 + 1) * 16)
                if p < 2 * NCH:
                    c = p // 2
                    cc = l * NCH + c
                    width = CHUNKS[c][1]
                    if c < 2:
                        if l > 0:
                            aux_ready(act, ("O", l - 1, STEPS - 1))
                    else:
                        act.wait_ge(z_done, l * UNITS + unit(c - 1, 0))
                    dst = w_hi[:, cc % 2, 4 * (p % 2):4 * (p % 2) + 4, 0:width]
                    src = wraw[:, n % 2, :].rearrange("p (k n) -> p k n", k=4)[:, :, 0:width]
                else:
                    act.wait_ge(z_done, (l + 1) * UNITS)
                    dst, src = act_hi[:, p - 2 * NCH, :], wraw[:, n % 2, :]
                fn(dst, src, ACT.Copy).then_inc(w_hi_ready, 1)

            def kv_hi_copy(l, t):
                bank = aux_ready(act, ("kvT", l, t))
                fn(kv_hi[:, t * P:(t + 1) * P], bank[:, 0:P], ACT.Copy)
                fn(kr_st[0:ROPE, t * P:(t + 1) * P], bank[0:ROPE, P:2 * P], ACT.Copy).then_inc(kv_hi_ready, 1)

            def z_ready(l, c, i):
                u = l * UNITS + unit(c, i)
                act.wait_ge(z_done, u + 1)
                return ps[:, u % 4, :]

            def square_sum(src, junk, dst):
                return fn(junk, src, ACT.Square, accum_out=dst)

            def h_hi(l, t):
                for b in range(2):
                    bank = aux_ready(act, ("hT", l, t, b))
                    if l > 0:
                        act.wait_ge(out_ready, l * NT)
                    fn(act_hi[:, 4 * b:4 * b + 4, t * P:(t + 1) * P], bank.rearrange("p (k n) -> p k n", k=4),
                       ACT.Copy).then_inc(h_hi_ready, 1)

            def evac_q(l, t):
                z_ = z_ready(l, Q, t)
                fn(Y[:, t, Y_Q:Y_Q + CW], z_[:, 0:CW], ACT.Copy)
                if l * UNITS + t:
                    act.wait_ge(z_read, l * UNITS + unit(Q, t))
                square_sum(z_[:, 0:CW], scr[:, 0:CW], ssq[:, 16 + t:17 + t]).then_inc(z_read, 1)

            def q_copy(l, t):
                bank = aux_ready(act, ("qT", l, t))
                if l > 0 and t == 0:
                    emptied(act, ("yT", l - 1, NT - 1, 1))
                    act.wait_ge(out_ready, l * NT)
                aux_release(fn(qnT[:, :, t * P:(t + 1) * P], bank[:, 0:CW].rearrange("p (k n) -> p k n", k=2),
                               ACT.Copy), ("qT", l, t))

            act.wait_ge(once_arrived, 48)
            fn(silu_c[:, 0:KD], silu_c[:, KD:2 * KD], ACT.Silu).then_inc(silu_ready, 1)
            act.wait_ge(angles_ready, 1)
            fn(sind[:, :, ROPE // 2:ROPE], sind[:, :, ROPE // 2:ROPE], ACT.Sin).then_inc(sines_ready, 1)
            fn(cosd[:, :, 0:ROPE // 2], cosd[:, :, 0:ROPE // 2], ACT.Sin).then_inc(sines_ready, 1)
            for half in range(2):
                fn(A_bc[:, half * BANK:(half + 1) * BANK], aux_ready(act, ("boot", "g_pre", half)), ACT.Copy
                   ).then_inc(aux_read[ring.uses["boot", "g_pre", half][0]], 1)

            def first_squares(t0, t1):
                for t in range(t0, t1):
                    act.wait_ge(first_x_arrived[t // 2], 16)
                    if t >= 2:
                        act.wait_ge(x_squared, t - 1)
                    square_sum(Y[:, t, :], xb[:, t % 2, :], ssq[:, 8 + t:9 + t]).then_inc(x_squared, 1)

            first_squares(0, 4)
            hi_piece(0, 0)
            hi_piece(0, 1)

            for l in range(DEPTH):
                if l == 0:
                    h_hi(l, 0)
                    h_hi(l, 1)
                    first_squares(4, NT)
                for t in range(NT):
                    evac_q(l, t)
                    if l == 0 and t in (1, 2):
                        hi_piece(l, 1 + t)
                    if t + 2 < NT and (l == 0 or t > 0):
                        h_hi(l, t + 2)
                for i in range(4):
                    if i in (1, 2):
                        for t in range(4):
                            q_copy(l, 4 * (i - 1) + t)
                    z_ = z_ready(l, CONV_A, i)
                    if l > 0:
                        b, n = ring.uses["pw", l - 1, NT - 1]
                        act.wait_ge(aux_done[b], n + 1)
                    ct, half = i // 2, i % 2
                    dst = convh[:, ct, HALO + half * BANK:HALO + (half + 1) * BANK]
                    fn(dst, z_, ACT.Copy, scale=0.5).then_inc(z_read, 1)
                    if i in (1, 2):
                        hi_piece(l, 4 + i - 1)
                for i in range(4):
                    z_ = z_ready(l, CONV_B, i)
                    if l * 4 + i:
                        act.wait_ge(glu_done, l * 4 + i)
                    if i == 0 and l > 0:
                        emptied(act, ("RT", l - 1, 1, 1))
                    fn(scr[:, :], z_, ACT.Tanh, scale=0.5).then_inc(z_read, 1)
                    if i in (1, 2):
                        hi_piece(l, 6 + i - 1)
                for t in range(NT):
                    z_ = z_ready(l, KV, t)
                    fn(Y[:, t, Y_KV:Y_KV + KV_RANK + ROPE], z_[:, 0:KV_RANK + ROPE], ACT.Copy)
                    act.wait_ge(z_read, l * UNITS + unit(KV, t))
                    if t == 0:
                        act.wait_ge(glu_done, l * 4 + 4)
                    square_sum(z_[:, 0:KV_RANK], scr[:, 0:KV_RANK], ssq[:, 24 + t:25 + t]).then_inc(z_read, 1)
                    if t in (2, 5):
                        hi_piece(l, 8 + (t - 2) // 3)
                for t in range(NT):
                    z_ = z_ready(l, SGU_V, t)
                    fn(Y[:, t, Y_SGU:Y_SGU + CW], z_[:, 0:CW], ACT.Gelu).then_inc(z_read, 1)
                    if t >= 5:
                        kv_hi_copy(l, 2 * (t - 5))
                        kv_hi_copy(l, 2 * (t - 5) + 1)
                    if t in (2, 5):
                        hi_piece(l, 10 + (t - 2) // 3)
                for t in range(NT):
                    z_ = z_ready(l, SGU_U, t)
                    if t == 0:
                        kv_hi_copy(l, 6)
                        kv_hi_copy(l, 7)
                        emptied(act, ("qT", l, NT - 1))
                    fn(Y[:, t, Y_U:Y_U + CW], z_[:, 0:CW], ACT.Gelu).then_inc(z_read, 1)
                    if t in (2, 5):
                        hi_piece(l, 12 + (t - 2) // 3)
                for c in (G_ATT0, G_ATT1):
                    for t in range(NT):
                        z_ = z_ready(l, c, t)
                        y0 = Y_ATT + (c - G_ATT0) * CW
                        if c == G_ATT0:
                            act.wait_ge(sgu_multiplied, l * 2 * NT + t + 1)
                        fn(Y[:, t, y0:y0 + CW], z_[:, 0:CW], ACT.Silu).then_inc(z_read, 1)
                        if t in (2, 5):
                            hi_piece(l, 2 * (c + 1) + (t - 2) // 3)
                for t in range(NT):
                    z_ = z_ready(l, G_SGU, t)
                    if t >= 2:
                        act.wait_ge(sgu_multiplied, l * 2 * NT + NT + t - 1)
                    fn(gtmp[:, t % 2, :], z_[:, 0:CW], ACT.Silu).then_inc(z_read, 1)
                    if t in (2, 5):
                        hi_piece(l, 18 + (t - 2) // 3)

                def conv_silu(half):
                    for ct in range(2):
                        bank = aux_ready(act, ("cB", l, ct, half))
                        act.wait_ge(conv_done, (l + 1) * 2 * 2 * CONV_K)
                        aux_release(fn(convh[:, ct, HALO + half * BANK:HALO + (half + 1) * BANK], bank, ACT.Silu,
                                       scale=cols[:, CLG + ct:CLG + ct + 1], bias=cols[:, CLB + ct:CLB + ct + 1]
                                       ), ("cB", l, ct, half))

                for t in range(NT):
                    z_ = z_ready(l, G_CONV, t)
                    if t in (0, 4):
                        conv_silu(t // 4)
                    fn(Y[:, t, Y_CONV:Y_CONV + CW], z_[:, 0:CW], ACT.Silu).then_inc(z_read, 1)

                def q_hi_copy(h):
                    for b in range(2):
                        bank = aux_ready(act, ("QA", l, h, b))
                        if h == 0 and b == 0:
                            act.wait_ge(z_done, (l + 1) * UNITS)
                        if h > 0 and b == 0:
                            act.wait_ge(scores_ready, l * STEPS + h * NT)
                        fn(q_hi[:, b * BANK:(b + 1) * BANK], bank, ACT.Copy).then_inc(q_hi_ready, 1)

                def q_rope_hi(h):
                    for b in range(2):
                        bank = aux_ready(act, ("qr", l, h, b))
                        for r in range(2):
                            ins = fn(qr_st[r * ROPE:(r + 1) * ROPE, b * BANK:(b + 1) * BANK], bank[0:ROPE, :], ACT.Copy)
                        ins.then_inc(qr_hi_ready, 1)

                def v_split(h):
                    for b in range(2):
                        bank = aux_ready(act, ("V", l, h, b))
                        fn(v_hl[:, 4 * b:4 * b + 4, 0, :], bank.rearrange("p (k n) -> p k n", k=4),
                           ACT.Copy).then_inc(v_hi_ready, 1)

                def exp(n):
                    keys = (ORDER[n % NT] + 1) * P
                    act.wait_ge(max_ready, l * STEPS + n + 1)
                    if n >= 2:
                        emptied(act, ("PT", l, n - 2, ORDER[(n - 2) % NT] // 4))
                    if n >= 4:
                        emptied(act, ("O", l, n - 4))
                    src = ps[:, 2 * (n % 2):2 * (n % 2) + 2, :].rearrange("p a b -> p (a b)")[:, 0:keys]
                    fn(xb[:, n % 2, 0:keys], src, ACT.Exp, bias=nmax[:, n % 2:n % 2 + 1],
                       accum_out=rsum[:, n % 4:n % 4 + 1]).then_inc(probs_ready, 1)

                def p_hi(n):
                    i = ORDER[n % NT]
                    for b in range(i // 4 + 1):
                        bank = aux_ready(act, ("PT", l, n, b))
                        if n > 0 and b == 0:
                            aux_ready(act, ("O", l, n - 1))
                        m = min(4, i + 1 - 4 * b)
                        fn(pt_hi[:, 4 * b:4 * b + m, :], bank[:, 0:m * P].rearrange("p (k n) -> p k n", k=m),
                           ACT.Copy).then_inc(p_hi_ready, 1)

                def pv_lo(n):
                    bank = aux_ready(act, ("O", l, n))
                    if n >= 2:
                        emptied(act, ("O", l, n - 2))
                    fn(qtmp[:, n % 2, 0:P], bank[:, P:2 * P], ACT.Copy).then_inc(pv_lo_copied, 1)

                def y_hi(t):
                    for b in range(2):
                        bank = aux_ready(act, ("yT", l, t, b))
                        if t >= 2:
                            act.wait_ge(out_ready, l * NT + t - 1)
                        else:
                            act.wait_ge(scores_ready, (l + 1) * STEPS)
                        fn(yT_hi[:, t % 2, 4 * b:4 * b + 4, :], bank.rearrange("p (k n) -> p k n", k=4),
                           ACT.Copy).then_inc(y_hi_ready, 1)

                q_hi_copy(0)
                q_rope_hi(0)
                v_split(0)
                exp(0)
                for n in range(STEPS):
                    pos, h = n % NT, n // NT
                    if n > 0:
                        pv_lo(n - 1)
                    if pos == 0 and h > 0:
                        v_split(h)
                    p_hi(n)
                    if pos == NT - 2 and h + 1 < HEADS:
                        q_rope_hi(h + 1)
                    if n + 1 < STEPS:
                        exp(n + 1)
                    if pos == NT - 3 and h + 1 < HEADS:
                        q_hi_copy(h + 1)
                    if n >= STEPS - 2:
                        y_hi(n - (STEPS - 2))
                    if pos in (2, 4):
                        hi_piece(l, 2 * NCH + 2 * h + (pos - 2) // 2)
                pv_lo(STEPS - 1)

                for t in range(NT):
                    g = l * NT + t
                    if 2 <= t + 1 < NT:
                        y_hi(t + 1)
                    act.wait_ge(out_ready, g + 1)
                    src = ps[:, 2 * (t % 2):2 * (t % 2) + 2, :].rearrange("p a b -> p (a b)")
                    if t == NT - 1 and l + 1 < DEPTH:
                        h_hi(l + 1, 0)
                        h_hi(l + 1, 1)
                    square_sum(src, Y[:, t, :], ssq[:, 2 + t % 2:3 + t % 2]).then_inc(out_squared, 1)
                    if t == NT - 1 and l + 1 < DEPTH:
                        h_hi(l + 1, 2)
                    act.wait_ge(x_updated, g + 1)
                    dst = out if l + 1 == DEPTH else x_mid
                    act.dma_start(dst[t * P:(t + 1) * P, :], xb[:, t % 2, :]).then_inc(result_stored[t % 2], 16)
                    if l + 1 < DEPTH:
                        square_sum(xb[:, t % 2, :], Y[:, t, :], ssq[:, 4 + t % 2:5 + t % 2]).then_inc(x_squared, 1)
                        if 3 <= t < 7:
                            hi_piece(l + 1, t - 3)
            for i in range(2):
                act.wait_ge(result_stored[i], DEPTH * NT // 2 * 16)

        @block.vector
        def _(dve):
            v = nc.vector
            chain = [0]

            def link(ins):
                chain[0] += 1
                ins.then_inc(dve_chain, 1)
                dve.wait_ge(dve_chain, chain[0])

            def r_sqrt(src, n, scale, y, tmp):
                link(v.tensor_scalar(tmp[:, 0:n], src, scale, EPS, ALU.mult, ALU.add))
                link(v.tensor_scalar(y.bitcast(I32), tmp[:, 0:n].bitcast(I32), -0.5, float(0x5F3759DF), ALU.mult, ALU.add))
                link(v.tensor_scalar(tmp[:, 0:n], tmp[:, 0:n], -0.5, None, ALU.mult))
                for _ in range(3):
                    if n == 1:
                        link(v.scalar_tensor_tensor(tmp[:, 8:9], y, y, tmp[:, 0:1], ALU.mult, ALU.mult))
                    else:
                        link(v.tensor_tensor(tmp[:, 8:8 + n], y, y, ALU.mult))
                        link(v.tensor_tensor(tmp[:, 8:8 + n], tmp[:, 8:8 + n], tmp[:, 0:n], ALU.mult))
                    link(v.scalar_tensor_tensor(y, tmp[:, 8:8 + n], 1.5, y, ALU.add, ALU.mult))

            TMP = st[:, 0:16]
            RS = st[:, 16:17]

            def lo_split(dst, bank, hi, s_from, value, name):
                dve.wait_ge(s_from, value)
                aux_release(v.tensor_tensor(dst, bank, hi.bitcast(F32), ALU.subtract), name)

            def ada_step(l, stage, i):
                for n, (l_, stage_, i_, job, j) in enumerate(ada_plan()):
                    if (l_, stage_, i_) == (l, stage, i):
                        ada_piece(n, job, j)

            def ada_piece(n, job, j):
                l, third, half = job
                hs = slice(half * BANK, (half + 1) * BANK)
                o, w = acc[:, hs], araw[:, n % 2, :]
                dst = {"scale": A_bc, "shift": S_bc, "gate": acc}[third][:, hs]
                dve.wait_ge(ada_arrived[n % 2], (n // 2 + 1) * 16)
                if j == 0:
                    k = ada_jobs.index(job)
                    if k >= 2:
                        aux_ready(dve, ("ada", *ada_jobs[k - 2]))
                    v.tensor_scalar(o, w, silu_c[:, 0:1], None, ALU.mult).then_inc(ada_used, 1)
                elif j < KD:
                    piece_used(dve, ada_order.index((job, j - 1)))
                    ins = v.scalar_tensor_tensor(o, w, silu_c[:, j:j + 1], o, ALU.mult, ALU.add)
                    ins.then_inc(ada_summed if j == KD - 1 else ada_used, 1)
                elif j == KD:
                    bank = aux_ready(dve, ("ada", *job))
                    aux_release(v.tensor_tensor(dst, bank, w, ALU.add), ("ada", *job))
                else:
                    emptied(dve, ("ada", *job))
                    v.scalar_tensor_tensor(dst, dst, 1.0 if third == "scale" else 0.0, w, ALU.add,
                                           ALU.mult).then_inc(ada_used, 1)

            def h_norm(g, t):
                dve.wait_ge(x_squared, g * NT + t + 1)
                r_sqrt(ssq[:, 4 + t % 2:5 + t % 2], 1, 1.0 / D, RS, TMP)
                v.scalar_tensor_tensor(Y[:, t, :], xb[:, t % 2, :], RS, A_bc[:, :], ALU.mult,
                                       ALU.mult).then_inc(h_normed, 1)

            dve.wait_ge(once_arrived, 48)
            link(v.memset(st[:, :], 0.0))
            dve.wait_ge(silu_ready, 1)
            v.tensor_copy(silu_bc[:, :, :], silu_c[:, 0:KD].unsqueeze(2).to_broadcast([P, KD, P])).then_inc(silu_bc_ready, 1)
            link(v.tensor_copy(posf[:, :], posi[:, :]))
            half_ = ROPE // 2
            ang = sind[:, :, half_:ROPE]
            turns = sind[:, :, 0:half_]
            for t in range(NT):
                ins = v.tensor_scalar(sind[:, t, half_:ROPE], freq[:, :], posf[:, t:t + 1], None, ALU.mult)
            link(ins)
            TWO_PI = 6.283185307179586
            link(v.tensor_scalar(turns, ang, 1.0 / TWO_PI, None, ALU.mult))
            turns_i = cosd[:, :, half_:ROPE].bitcast(I32)
            link(v.tensor_copy(turns_i, turns))
            link(v.tensor_copy(turns, turns_i))
            rest = TWO_PI
            parts = []
            for bits in (5, 15, 24):
                q = round(rest * 2.0 ** bits) / 2.0 ** bits
                parts.append(q)
                rest -= q
            for part in parts + [rest]:
                link(v.scalar_tensor_tensor(ang, turns, -part, ang, ALU.mult, ALU.add))
            PI = 3.1415925
            link(v.tensor_scalar(ang, ang, PI, -PI, ALU.min, ALU.max))
            cosv = cosd[:, :, 0:half_]
            link(v.tensor_scalar(cosv, ang, -1.0, None, ALU.mult))
            link(v.tensor_tensor(cosv, cosv, ang, ALU.min))
            v.tensor_scalar(cosv, cosv, TWO_PI / 4, None, ALU.add).then_inc(angles_ready, 1)
            dve.wait_ge(boot_arrived[2], 16)
            for k in range(4):
                w, sc = boot[:, 1, k, :], silu_c[:, k:k + 1]
                if k == 0:
                    ins = v.tensor_scalar(acc[:, :], w, sc, None, ALU.mult)
                else:
                    ins = v.scalar_tensor_tensor(acc[:, :], w, sc, acc[:, :], ALU.mult, ALU.add)
                if k < 3:
                    link(ins)
            ins.then_inc(ada_summed, 1)
            for half in range(2):
                hs = slice(half * BANK, (half + 1) * BANK)
                bank = aux_ready(dve, ("boot", 0, half))
                emptied(dve, ("boot", "g_pre", half))
                aux_release(v.scalar_tensor_tensor(A_bc[:, hs], bank, 1.0, A_bc[:, hs], ALU.add, ALU.mult),
                            ("boot", 0, half))
            emptied(dve, ("boot", 0, 1))
            dve.wait_ge(sines_ready, 2)
            v.tensor_scalar(sind[:, :, 0:half_], ang, -1.0, None, ALU.mult)
            link(v.tensor_copy(cosd[:, :, half_:ROPE], cosv))
            def first_norm(t0, t1):
                dve.wait_ge(x_squared, t1)
                r_sqrt(ssq[:, 8 + t0:8 + t1], t1 - t0, 1.0 / D, st[:, 48 + t0:48 + t1], TMP)
                for t in range(t0, t1):
                    v.scalar_tensor_tensor(Y[:, t, :], Y[:, t, :], st[:, 48 + t:49 + t], A_bc[:, :], ALU.mult,
                                           ALU.mult).then_inc(h_normed, 1)

            first_norm(0, 2)
            for half in range(2):
                hs = slice(half * BANK, (half + 1) * BANK)
                bank = aux_ready(dve, ("boot", 1, half))
                aux_release(v.tensor_copy(S_bc[:, hs], bank), ("boot", 1, half))
            emptied(dve, ("boot", 1, 1))
            for t in range(H0):
                dve.wait_ge(h_normed, t + 1)
                v.tensor_tensor(Y[:, t, :], Y[:, t, :], S_bc[:, :], ALU.add).then_inc(first_h_ready, 1)
            first_norm(2, 4)

            def h_lo(l, t):
                for b in range(2):
                    name = ("hT", l, t, b)
                    bank = aux_ready(dve, name)
                    sl = (slice(None), slice(4 * b, 4 * b + 4), slice(t * P, (t + 1) * P))
                    lo_split(act_lo[sl], bank.rearrange("p (k n) -> p k n", k=4), act_hi[sl], h_hi_ready,
                             (l * NT + t) * 2 + b + 1, name)

            def q_norm(l):
                dve.wait_ge(z_read, l * UNITS + unit(Q, NT - 1) + 1)
                r_sqrt(ssq[:, 16:24], NT, 1.0 / Q_RANK, st[:, 32:40], TMP)
                for t in range(NT):
                    y = Y[:, t, Y_Q:Y_Q + CW]
                    v.tensor_scalar(y, y, st[:, 32 + t:33 + t], None, ALU.mult).then_inc(q_normed, 1)

            def rope(dst, src, cos, sin, t1, t2):
                h2 = ROPE // 2
                v.tensor_tensor(t1, src, cos, ALU.mult)
                v.tensor_tensor(t2[:, :, 0:h2], src[:, :, h2:ROPE], sin[:, :, 0:h2], ALU.mult)
                link(v.tensor_tensor(t2[:, :, h2:ROPE], src[:, :, 0:h2], sin[:, :, h2:ROPE], ALU.mult))
                return v.tensor_tensor(dst, t1, t2, ALU.add)

            def kv_norm(l):
                dve.wait_ge(z_read, l * UNITS + unit(KV, NT - 1) + 1)
                kr = Y[:, :, Y_KV + P:Y_KV + P + ROPE]
                t1 = scr[:, :].rearrange("p (a n) -> p a n", a=NT)
                t2 = qtmp[:, :, :].rearrange("p a b -> p (a b)").rearrange("p (a n) -> p a n", a=NT)
                rope(kr, kr, cosd[:, :, :], sind[:, :, :], t1, t2)
                r_sqrt(ssq[:, 24:32], NT, 1.0 / KV_RANK, st[:, 32:40], TMP)
                for t in range(NT):
                    y = Y[:, t, Y_KV:Y_KV + P]
                    v.tensor_scalar(y, y, st[:, 32 + t:33 + t], None, ALU.mult).then_inc(kv_normed, 1)

            def kv_lo_split(l, t):
                name = ("kvT", l, t)
                bank = aux_ready(dve, name)
                ts = slice(t * P, (t + 1) * P)
                dve.wait_ge(kv_hi_ready, l * NT + t + 1)
                v.tensor_tensor(kv_lo[:, ts], bank[:, 0:P], kv_hi[:, ts].bitcast(F32), ALU.subtract)
                aux_release(v.tensor_tensor(kr_st[ROPE:P, ts], bank[0:ROPE, P:2 * P], kr_st[0:ROPE, ts].bitcast(F32),
                                            ALU.subtract), name)

            pairs = [(ct, k) for ct in range(2) for k in range(CONV_K)]

            def conv_pair(l, m):
                if m >= len(pairs):
                    return
                ct, k = pairs[m]
                for half in range(2):
                    n = conv_taps(l, ct, k, half)
                    src = convh[:, ct, k + half * BANK:k + (half + 1) * BANK]
                    o = convo[:, half, :]
                    if ct == 1:
                        o = Y[:, 4 * half:4 * half + 4, Y_CONV + P:Y_CONV + CW]
                        src = src.rearrange("p (t n) -> p t n", t=4)
                    if k == 0:
                        if m == 0 and half == 0:
                            emptied(dve, ("taps", l))
                            emptied(dve, ("uT", l, HEADS - 1))
                        v.tensor_scalar(o, src, taps[:, ct, 0:1], cols[:, CB + ct:CB + ct + 1], ALU.mult,
                                        ALU.add).then_inc(conv_done, 1)
                    else:
                        dve.wait_ge(conv_done, n - 2)
                        v.scalar_tensor_tensor(o, src, taps[:, ct, k:k + 1], o, ALU.mult, ALU.add).then_inc(conv_done, 1)

            def absorb_operands(l, h):
                bank = aux_ready(dve, ("uT", l, h))
                if h >= 2:
                    aux_ready(dve, ("Wq", l, h - 2))
                place_ = (gtmp, qtmp)[h % 2][:, :, :].rearrange("p a b -> p (a b)")
                aux_release(v.tensor_copy(place_[:, 0:3 * P], bank[:, 0:3 * P]), ("uT", l, h))

            def absorbed(l, h):
                bank = aux_ready(dve, ("Wq", l, h))
                aux_release(v.tensor_copy(Wq[:, :, h, :], bank[:, 0:2 * P].rearrange("p (k n) -> p k n", k=2)),
                            ("Wq", l, h))

            def small_weights(l):
                dve.wait_ge(small_arrived, prep_all(l))
                link(v.tensor_scalar(cols[:, 16:18], cols[:, GQ:GQ + 2], SCALE, None, ALU.mult))
                for k in range(2):
                    ins = v.tensor_scalar(uq_raw[:, k, :, :], uq_raw[:, k, :, :], cols[:, 16 + k:17 + k], None, ALU.mult)
                v.tensor_scalar(uk_raw[:, :, :], uk_raw[:, :, :], cols[:, GKV:GKV + 1], None, ALU.mult)
                link(v.tensor_scalar(uv_raw[:, :, :], uv_raw[:, :, :], cols[:, GKV:GKV + 1], None, ALU.mult))
                link(v.tensor_copy(uv_hi[:, :, :], uv_raw[:, :, :]))
                v.tensor_tensor(uv_lo[:, :, :], uv_raw[:, :, :], uv_hi[:, :, :].bitcast(F32), ALU.subtract)
                v.tensor_copy(uqr[:, :, :, :], uq_raw[:, :, :, NOPE:NOPE + ROPE]).then_inc(small_scaled, 1)

            def sgu_stats(l, t):
                dve.wait_ge(z_read, l * UNITS + unit(SGU_V, t) + 1)
                ins = v.bn_stats(bst[:, t, :], Y[:, t, Y_SGU:Y_SGU + CW])
                if t == NT - 1:
                    link(ins)

            def sgu_norm(l):
                for t in range(NT):
                    ins = v.bn_aggr(mv[:, t, :], bst[:, t, :])
                link(ins)
                r_sqrt(mv[:, :, 1], NT, 1.0, st[:, 24:24 + NT], TMP)
                for t in range(NT):
                    y = Y[:, t, Y_SGU:Y_SGU + CW]
                    v.tensor_scalar(y, y, mv[:, t, 0:1], st[:, 24 + t:25 + t], ALU.subtract, ALU.mult).then_inc(v_normed, 1)

            def sgu_mix(l, half):
                for pair in range(2):
                    name = ("sgu", l, half, pair)
                    bank = aux_ready(dve, name)
                    for i in range(2):
                        g = 2 * pair + i
                        ins = v.tensor_scalar(Y[:, 4 * half:4 * half + 4, Y_SGU + g * 64:Y_SGU + (g + 1) * 64],
                                              bank[:, i * 256:(i + 1) * 256].rearrange("p (t n) -> p t n", t=4),
                                              cols[:, BS + g:BS + g + 1], None, ALU.add)
                    aux_release(ins, name)

            def conv_token(l, ct):
                for half in range(2):
                    name = ("cT", l, ct, half)
                    bank = aux_ready(dve, name)
                    aux_release(v.tensor_copy(Y[:, 4 * half:4 * half + 4, Y_CONV + ct * P:Y_CONV + (ct + 1) * P],
                                              bank.rearrange("p (k n) -> p k n", k=4)), name)

            def conv_norm(l):
                emptied(dve, ("cT", l, 1, 1))
                for t in range(NT):
                    ins = v.bn_stats(bst[:, t, :], Y[:, t, Y_CONV:Y_CONV + CW])
                link(ins)
                for t in range(NT):
                    ins = v.bn_aggr(mv[:, t, :], bst[:, t, :])
                link(ins)
                r_sqrt(mv[:, :, 1], NT, 1.0, st[:, 24:24 + NT], TMP)
                for t in range(NT):
                    yc = Y[:, t, Y_CONV:Y_CONV + CW]
                    v.tensor_scalar(yc, yc, mv[:, t, 0:1], st[:, 24 + t:25 + t], ALU.subtract,
                                    ALU.mult).then_inc(conv_normed, 1)

            def q_rotate(l, pair, b):
                name = ("RT", l, pair, b)
                bank = aux_ready(dve, name)
                if pair == 0:
                    aux_ready(dve, ("cT", l, 1, b))
                else:
                    aux_ready(dve, ("qr", l, 1, b))
                if b == 1:
                    emptied(dve, ("RT", l, pair, 0))
                for h in range(2):
                    src = bank.rearrange("p (t h n) -> p t h n", t=4, h=2)[:, :, h, :]
                    t1 = scr[:, 0:256].rearrange("p (a n) -> p a n", a=4)
                    t2 = scr[:, 256:512].rearrange("p (a n) -> p a n", a=4)
                    ins = rope(qrt[:, 4 * b:4 * b + 4, h, :], src, cosd[:, 4 * b:4 * b + 4, :],
                               sind[:, 4 * b:4 * b + 4, :], t1, t2)
                    if h == 0:
                        link(ins)
                aux_release(ins, name)

            def q_nope_lo(l, h):
                for b in range(2):
                    name = ("QA", l, h, b)
                    bs = slice(b * BANK, (b + 1) * BANK)
                    lo_split(q_lo[:, bs], aux_ready(dve, name), q_hi[:, bs], q_hi_ready, (l * HEADS + h) * 2 + b + 1, name)

            def q_rope_lo(l, h):
                for b in range(2):
                    name = ("qr", l, h, b)
                    bs = slice(b * BANK, (b + 1) * BANK)
                    lo_split(qr_lo[:, bs], aux_ready(dve, name)[0:ROPE, :], qr_st[0:ROPE, bs], qr_hi_ready,
                             (l * HEADS + h) * 2 + b + 1, name)

            def v_lo_split(l, h):
                for b in range(2):
                    name = ("V", l, h, b)
                    ks = slice(4 * b, 4 * b + 4)
                    bank = aux_ready(dve, name).rearrange("p (k n) -> p k n", k=4)
                    lo_split(v_hl[:, ks, 1, :], bank, v_hl[:, ks, 0, :], v_hi_ready,
                             (l * HEADS + h) * 2 + b + 1, name)

            def row_max(l, n):
                keys = (ORDER[n % NT] + 1) * P
                dve.wait_ge(scores_ready, l * STEPS + n + 1)
                if n >= 2:
                    dve.wait_ge(probs_ready, l * STEPS + n - 1)
                src = ps[:, 2 * (n % 2):2 * (n % 2) + 2, :].rearrange("p a b -> p (a b)")[:, 0:keys]
                v.tensor_reduce(nmax[:, n % 2:n % 2 + 1], src, AX_X, ALU.max, negate=True).then_inc(max_ready, 1)

            def p_lo_split(l, n):
                i = ORDER[n % NT]
                for b in range(i // 4 + 1):
                    name = ("PT", l, n, b)
                    m = min(4, i + 1 - 4 * b)
                    sl = (slice(None), slice(4 * b, 4 * b + m), slice(None))
                    lo_split(pt_lo[sl], aux_ready(dve, name)[:, 0:m * P].rearrange("p (k n) -> p k n", k=m), pt_hi[sl],
                             p_hi_ready, pt_count(l, n, b), name)

            def att_out(l, n):
                h, i = n // NT, ORDER[n % NT]
                name = ("O", l, n)
                o = qtmp[:, n % 2, 0:P]
                v.reciprocal(st[:, 40 + n % 2:41 + n % 2], rsum[:, n % 4:n % 4 + 1])
                bank = aux_ready(dve, name)
                dve.wait_ge(pv_lo_copied, l * STEPS + n + 1)
                link(v.tensor_tensor(o, bank[:, 0:P], o, ALU.add))
                y = Y[:, i, h * P:(h + 1) * P]
                aux_release(v.scalar_tensor_tensor(y, o, st[:, 40 + n % 2:41 + n % 2], y, ALU.mult, ALU.mult), name)

            def y_lo(l, t):
                for b in range(2):
                    name = ("yT", l, t, b)
                    sl = (slice(None), t % 2, slice(4 * b, 4 * b + 4), slice(None))
                    lo_split(yT_lo[sl], aux_ready(dve, name).rearrange("p (k n) -> p k n", k=4), yT_hi[sl], y_hi_ready,
                             (l * NT + t) * 2 + b + 1, name)

            def conv_gate(l, t):
                name = ("pw", l, t)
                bank = aux_ready(dve, name)
                dve.wait_ge(z_read, (l + 1) * UNITS)
                y = Y[:, t, Y_CONV:Y_CONV + CW]
                aux_release(v.tensor_tensor(y, bank[:, 0:CW], y, ALU.mult), name)

            for l in range(DEPTH):
                if l == 0:
                    h_lo(l, 0)
                    h_lo(l, 1)
                    first_norm(4, 6)
                for t in range(NT):
                    if t + 2 < NT and (l == 0 or t > 0):
                        h_lo(l, t + 2)
                    if l == 0 and t == 0:
                        first_norm(6, NT)
                q_norm(l)
                small_weights(l)
                ada_step(l, CONV_A, 0)
                ada_step(l, CONV_A, 1)
                bank = aux_ready(dve, ("taps", l))
                aux_release(v.tensor_copy(taps[:, :, :], bank[:, 0:64].rearrange("p (c k) -> p c k", c=2)[:, :, 0:CONV_K]),
                            ("taps", l))
                bank = aux_ready(dve, ("ws", l))
                aux_release(v.tensor_copy(wsT[:, :, :], bank.rearrange("p (g n) -> p g n", g=HEADS)),
                            ("ws", l))
                ada_step(l, CONV_A, 2)
                for h in range(2):
                    absorb_operands(l, h)
                ada_step(l, CONV_A, 3)
                for h in range(2):
                    absorbed(l, h)
                for h in range(2, 4):
                    absorb_operands(l, h)
                for i in range(4):
                    dve.wait_ge(z_read, l * UNITS + unit(CONV_B, i) + 1)
                    ct, half = i // 2, i % 2
                    ch = convh[:, ct, HALO + half * BANK:HALO + (half + 1) * BANK]
                    v.scalar_tensor_tensor(ch, scr[:, :], 1.0, ch, ALU.add, ALU.mult).then_inc(glu_done, 1)
                    if i == 0:
                        absorbed(l, 2)
                        absorbed(l, 3)
                    if i >= 2:
                        dve.wait_ge(glu_done, l * 4 + i)
                        for m in range(3 * (i - 2), 3 * (i - 1)):
                            conv_pair(l, m)
                    ada_step(l, CONV_B, i)
                dve.wait_ge(glu_done, (l + 1) * 4)
                m = 6
                for t in range(NT):
                    for _ in range(2 if t % 3 == 2 else 1):
                        conv_pair(l, m)
                        m += 1
                    ada_step(l, KV, t)
                kv_norm(l)
                for t in range(NT):
                    sgu_stats(l, t)
                    if t >= 2:
                        conv_pair(l, m)
                        m += 1
                    if t >= 5:
                        kv_lo_split(l, 2 * (t - 5))
                        kv_lo_split(l, 2 * (t - 5) + 1)
                sgu_norm(l)
                kv_lo_split(l, 6)
                kv_lo_split(l, 7)
                for t in range(1, NT):
                    conv_pair(l, m)
                    m += 1
                    if t == 6:
                        sgu_mix(l, 0)
                for t in range(2 * NT):
                    if t == 1:
                        sgu_mix(l, 1)
                    for _ in range(2):
                        conv_pair(l, m)
                        m += 1
                    if t == 2:
                        conv_token(l, 0)
                while m < len(pairs):
                    conv_pair(l, m)
                    m += 1
                for t in range(NT):
                    ada_step(l, G_SGU, t)
                    if t == 2:
                        conv_token(l, 1)
                        conv_norm(l)
                for t in range(NT):
                    ada_step(l, G_CONV, t)
                    if t in (4, 5):
                        q_rotate(l, 0, t - 4)
                q_nope_lo(l, 0)
                q_rope_lo(l, 0)
                v_lo_split(l, 0)
                row_max(l, 0)
                row_max(l, 1)
                ada_step(l, ATT, 0)
                conv_gate(l, 0)
                for n in range(STEPS):
                    pos, h = n % NT, n // NT
                    if n > 0:
                        att_out(l, n - 1)
                    if pos == 0 and h > 0:
                        v_lo_split(l, h)
                    p_lo_split(l, n)
                    if pos == NT - 2 and h + 1 < HEADS:
                        q_rope_lo(l, h + 1)
                    if pos == NT - 1 and h + 1 < HEADS:
                        row_max(l, n + 1)
                    if n in (10, 12):
                        q_rotate(l, 1, (n - 10) // 2)
                    if n + 2 < STEPS and pos != NT - 2:
                        row_max(l, n + 2)
                    if pos == NT - 3 and h + 1 < HEADS:
                        q_nope_lo(l, h + 1)
                    if n + 1 < NT:
                        conv_gate(l, n + 1)
                    if n >= STEPS - 2:
                        y_lo(l, n - (STEPS - 2))
                    if n > 0:
                        ada_step(l, ATT, n)
                att_out(l, STEPS - 1)
                for t in range(NT):
                    if 2 <= t + 1 < NT:
                        y_lo(l, t + 1)
                    g = l * NT + t
                    if t == NT - 1 and l + 1 < DEPTH:
                        h_lo(l + 1, 0)
                        h_lo(l + 1, 1)
                    dve.wait_ge(out_squared, g + 1)
                    r_sqrt(ssq[:, 2 + t % 2:3 + t % 2], 1, 1.0 / D, RS, TMP)
                    src = ps[:, 2 * (t % 2):2 * (t % 2) + 2, :].rearrange("p a b -> p (a b)")
                    v.scalar_tensor_tensor(Y[:, t, :], src, RS, acc[:, :], ALU.mult, ALU.mult).then_inc(out_read, 1)
                    dve.wait_ge(out_read, g + 1)
                    before = 4 * l
                    dve.wait_ge(x_arrived[t % 2], (before + t // 2 + 1) * 16)
                    v.tensor_tensor(xb[:, t % 2, :], xb[:, t % 2, :], Y[:, t, :], ALU.add).then_inc(x_updated, 1)
                    if t == NT - 1 and l + 1 < DEPTH:
                        h_lo(l + 1, 2)
                    if l + 1 < DEPTH:
                        h_norm(l + 1, t)

        @block.gpsimd
        def _(pool):
            g_ = nc.gpsimd
            chain = [0]
            g_.memset(ident[:, :], 0.0).then_inc(pool_done, 1)
            g_.memset(ones[:, :], 1.0).then_inc(pool_done, 1)
            g_.memset(mask[:, :], 0.0).then_inc(pool_done, 1)
            g_.memset(convh[:, :, 0:HALO], 0.0)
            pool.wait_ge(pool_done, 3)
            g_.affine_select(out=ident[:, :], in_=ident[:, :], compare_op=ALU.not_equal, fill=1.0, base=0,
                             pattern=[[-1, P]], channel_multiplier=1).then_inc(pool_done, 1)
            g_.affine_select(out=mask[:, :], in_=mask[:, :], compare_op=ALU.is_ge, fill=MASKED, base=0,
                             pattern=[[-1, P]], channel_multiplier=1).then_inc(pool_done, 1)
            pool.wait_ge(pool_done, 5)
            g_.tensor_copy(ident_r[:, :], ident[:, :])
            g_.tensor_copy(mask_r[:, :], mask[:, :]).then_inc(pool_done, 1)

            def lo_piece(l, p):
                n = l * W_PIECES + p
                pool.wait_ge(w_hi_ready, n + 1)
                if p < 2 * NCH:
                    cc = l * NCH + p // 2
                    width = CHUNKS[p // 2][1]
                    sl = (slice(None), cc % 2, slice(4 * (p % 2), 4 * (p % 2) + 4), slice(0, width))
                    hi, lo = w_hi[sl], w_lo[sl]
                    src = wraw[:, n % 2, :].rearrange("p (k n) -> p k n", k=4)[:, :, 0:width]
                else:
                    k = p - 2 * NCH
                    hi, lo, src = act_hi[:, k, :], act_lo[:, k, :], wraw[:, n % 2, :]
                g_.tensor_tensor(lo, src, hi.bitcast(F32), ALU.subtract).then_inc(w_split, 1)

            def add_shift(g, t):
                if g == 0:
                    for half in range(2):
                        emptied(pool, ("boot", 1, half))
                pool.wait_ge(h_normed, g * NT + t + 1)
                g_.tensor_tensor(Y[:, t, :], Y[:, t, :], S_bc[:, :], ALU.add).then_inc(h_ready, 1)

            lo_piece(0, 0)
            lo_piece(0, 1)
            for t in range(H0, NT):
                add_shift(0, t)
            lo_piece(0, 2)
            lo_piece(0, 3)
            for l in range(DEPTH):
                for p in range(4, 6):
                    lo_piece(l, p)
                emptied(pool, ("ws", l))
                g_.affine_select(out=wsT[:, :, :], in_=wsT[:, :, :], compare_op=ALU.is_ge, fill=0.0, base=0,
                                 pattern=[[0, HEADS], [1, P]], channel_multiplier=-1).then_inc(ws_masked, 1)
                for p in range(6, 12):
                    lo_piece(l, p)
                for t in range(NT):
                    pool.wait_ge(v_normed, l * NT + t + 1)
                    gv = Y[:, t, Y_SGU:Y_SGU + CW]
                    chain[0] += 1
                    g_.tensor_tensor(gv, gv, sgu_g[:, :], ALU.mult).then_inc(pool_done, 1)
                    pool.wait_ge(pool_done, 6 + chain[0])
                    g_.tensor_tensor(gv, gv, sgu_b[:, :], ALU.add).then_inc(v_scaled, 1)
                    if t in (4, 7):
                        lo_piece(l, 12 + (t - 4) // 3)
                for t in range(NT):
                    for pair in range(2):
                        emptied(pool, ("sgu", l, t // 4, pair))
                    pool.wait_ge(z_read, l * UNITS + unit(SGU_U, t) + 1)
                    y = Y[:, t, Y_SGU:Y_SGU + CW]
                    g_.tensor_tensor(y, y, Y[:, t, Y_U:Y_U + CW], ALU.mult).then_inc(sgu_multiplied, 1)
                for p in range(14, 18):
                    lo_piece(l, p)
                for t in range(NT):
                    pool.wait_ge(z_read, l * UNITS + unit(G_SGU, t) + 1)
                    y = Y[:, t, Y_SGU:Y_SGU + CW]
                    g_.tensor_tensor(y, y, gtmp[:, t % 2, :], ALU.mult).then_inc(sgu_multiplied, 1)
                    if t in (2, 5):
                        lo_piece(l, 18 + (t - 2) // 3)
                for p in range(2 * NCH, W_PIECES):
                    lo_piece(l, p)
                if l + 1 < DEPTH:
                    for t in range(NT):
                        add_shift(l + 1, t)
                        if 3 <= t < 7:
                            lo_piece(l + 1, t - 3)


_INS = ["x", "c", "positions", "w_ada", "b_ada", "g_pre", "g_post", "w_in", "q_norm_g", "w_uq", "kv_norm_g", "w_ukv",
        "conv_w", "conv_b", "conv_ln_g", "conv_ln_b", "w_pw2", "sgu_ln_g", "sgu_ln_b", "w_s", "b_s", "w_out"]


def kernel(**inputs):
    import numpy as np
    import concourse.bacc as bacc
    from concourse import mybir as mb
    from concourse.bass_utils import run_bass_kernel_spmd

    nc = bacc.Bacc("TRN2", target_bir_lowering=False, num_devices=1, dynamic_dma_scratch_size=1024)
    arrays = {n: np.ascontiguousarray(inputs[n]) for n in _INS}
    arrays["x"] = arrays["x"].reshape(SEQ, D)
    arrays["inv_freq"] = (10000.0 ** (-np.arange(0, ROPE, 2) / ROPE)).astype(np.float32)
    aps, in_map = {}, {}
    for name, arr in arrays.items():
        in_map[f"in_{name}"] = arr
        aps[name] = nc.dram_tensor(f"in_{name}", arr.shape, mb.dt.from_np(arr.dtype), kind="ExternalInput").ap()
    x_mid = nc.dram_tensor("x_mid", (SEQ, D), mb.dt.float32).ap()
    out = nc.dram_tensor("out", (SEQ, D), mb.dt.float32, kind="ExternalOutput").ap()
    trunk(nc, aps, out, x_mid)
    r = run_bass_kernel_spmd(nc, [in_map], core_ids=[0])
    return r.results[0]["out"].reshape(1, SEQ, D)
```
